# Optimizing a Trainium2 kernel written in Bass

```python
import math
import jax, jax.numpy as jnp
from jax import lax
import numpy as np

D_MODEL = 1024
BATCH = 1
SEQ = 512
DEPTH = 2
DEC_BATCH = 8
DEC_SEQ = 1
PAST_LEN = 256
PAGE_SIZE = 128

D_MIX = D_MODEL
D_RNN = D_MIX // 2
RNN_BLOCKS = 8
RNN_BLOCK_W = D_RNN // RNN_BLOCKS
CONV_W = 4
LRU_C = 8.0
D_ATT = D_MIX - D_RNN
HEAD_DIM = 64
N_DIFF_HEADS = D_ATT // (2 * HEAD_DIM)
N_QK_HEADS = 2 * N_DIFF_HEADS
V_DIM = 2 * HEAD_DIM
ROPE_THETA = 10000.0
D_PROJ = 2 * D_RNN + 3 * D_ATT
N_GROUPS = 4
EXPERTS_PER_GROUP = 8
N_EXPERTS = N_GROUPS * EXPERTS_PER_GROUP
TOP_K = 2
D_EXPERT = 512
Q_BLOCK = 128
DISPATCH_BLOCK = 128
NORM_EPS = 1e-6
SUBLN_EPS = 1e-5
NEG_INF = -1e30

kernel_name = 'hymba_rglru_diffattn_hmoe_step'

def rmsnorm(x, g, eps=NORM_EPS):
    xf = x.astype(jnp.float32)
    y = xf * lax.rsqrt(jnp.mean(xf * xf, axis=-1, keepdims=True) + eps)
    return (y * g.astype(jnp.float32)).astype(x.dtype)

def rope(x, pos):
    half = HEAD_DIM // 2
    inv = ROPE_THETA ** (-jnp.arange(half, dtype=jnp.float32) / half)
    ang = pos.astype(jnp.float32)[:, None] * inv[None, :]
    cos = jnp.cos(ang)[None, :, None, :]
    sin = jnp.sin(ang)[None, :, None, :]
    xf = x.astype(jnp.float32)
    x1, x2 = xf[..., :half], xf[..., half:]
    return jnp.concatenate([x1 * cos - x2 * sin, x2 * cos + x1 * sin], axis=-1).astype(x.dtype)

def causal_conv(x, buf, w, b):
    S = x.shape[1]
    xp = jnp.concatenate([buf.astype(x.dtype), x], axis=1)
    y = b.astype(x.dtype)
    for j in range(CONV_W):
        y = y + xp[:, j:j + S] * w[j]
    return y, xp[:, -(CONV_W - 1):]

def rg_lru(xc, pos, h0, w_ga, b_ga, w_gx, b_gx, lru_lambda):
    B, S, _ = xc.shape
    xb = xc.reshape(B, S, RNN_BLOCKS, RNN_BLOCK_W)
    r = jax.nn.sigmoid((jnp.einsum('bsni,nij->bsnj', xb, w_ga) + b_ga).astype(jnp.float32)).reshape(B, S, D_RNN)
    i = jax.nn.sigmoid((jnp.einsum('bsni,nij->bsnj', xb, w_gx) + b_gx).astype(jnp.float32)).reshape(B, S, D_RNN)
    log_a = -LRU_C * r * jax.nn.softplus(-lru_lambda.astype(jnp.float32))
    a = jnp.exp(log_a)
    mult = jnp.sqrt(-jnp.expm1(2.0 * log_a))
    mult = jnp.where((pos == 0)[None, :, None], 1.0, mult)
    bt = mult * i * xc.astype(jnp.float32)
    bt = bt.at[:, 0].add(a[:, 0] * h0.astype(jnp.float32))

    def comb(lhs, rhs):
        a1, b1 = lhs
        a2, b2 = rhs
        return a1 * a2, a2 * b1 + b2

    _, hs = lax.associative_scan(comb, (a, bt), axis=1)
    return hs, hs[:, -1]

def diff_attn_block(q, qpos, k, v, kpos, lam):
    B, Q = q.shape[:2]
    s = jnp.einsum('bqhd,bkhd->bhqk', q, k).astype(jnp.float32) * (HEAD_DIM ** -0.5)
    s = jnp.where((kpos[None, :] <= qpos[:, None])[None, None], s, NEG_INF)
    p = jax.nn.softmax(s, axis=-1).reshape(B, N_DIFF_HEADS, 2, Q, -1)
    amap = p[:, :, 0] - lam * p[:, :, 1]
    return jnp.einsum('bgqk,bkgd->bqgd', amap.astype(v.dtype), v)

def prompt_attention(q, k, v, pos, lam):
    B, S = q.shape[:2]
    nb = S // Q_BLOCK
    qb = q.reshape(B, nb, Q_BLOCK, N_QK_HEADS, HEAD_DIM).transpose(1, 0, 2, 3, 4)
    pb = pos.reshape(nb, Q_BLOCK)
    out = lax.map(lambda a: diff_attn_block(a[0], a[1], k, v, pos, lam), (qb, pb))
    return out.transpose(1, 0, 2, 3, 4).reshape(B, S, N_DIFF_HEADS, V_DIM)

def mixer(x, pos, conv_buf, h0, attend, ln1_g, w_in, conv_w, conv_b, w_ga, b_ga, w_gx, b_gx,
          lru_lambda, lam_q1, lam_k1, lam_q2, lam_k2, subln_g, lambda_init, w_out):
    B, S, _ = x.shape
    h = rmsnorm(x, ln1_g)
    proj = h @ w_in
    x_rnn, g_rnn, q, k, v = jnp.split(proj, [D_RNN, 2 * D_RNN, 2 * D_RNN + D_ATT, 2 * D_RNN + 2 * D_ATT], axis=-1)
    xc, new_buf = causal_conv(x_rnn, conv_buf, conv_w, conv_b)
    hs, h_last = rg_lru(xc, pos, h0, w_ga, b_ga, w_gx, b_gx, lru_lambda)
    y_rnn = hs.astype(x.dtype) * jax.nn.gelu(g_rnn)
    q = rope(q.reshape(B, S, N_QK_HEADS, HEAD_DIM), pos)
    k = rope(k.reshape(B, S, N_QK_HEADS, HEAD_DIM), pos)
    v = v.reshape(B, S, N_DIFF_HEADS, V_DIM)
    lam = (jnp.exp(jnp.sum(lam_q1.astype(jnp.float32) * lam_k1.astype(jnp.float32)))
           - jnp.exp(jnp.sum(lam_q2.astype(jnp.float32) * lam_k2.astype(jnp.float32))) + lambda_init)
    o = attend(q, k, v, lam)
    o = rmsnorm(o, subln_g, SUBLN_EPS) * (1.0 - lambda_init)
    y = jnp.concatenate([y_rnn, o.reshape(B, S, D_ATT)], axis=-1) @ w_out
    return x + y, k, v, h_last, new_buf

def hier_route(h, w_rg, b_rg, w_re, b_re):
    N = h.shape[0]
    hf = h.astype(jnp.float32)
    gp = jax.nn.softmax(hf @ w_rg.astype(jnp.float32) + b_rg.astype(jnp.float32), axis=-1)
    g = jnp.argmax(gp, axis=-1).astype(jnp.int32)
    pg = jnp.max(gp, axis=-1)
    el = (hf @ w_re.astype(jnp.float32) + b_re.astype(jnp.float32)).reshape(N, N_GROUPS, EXPERTS_PER_GROUP)
    sel = jnp.take_along_axis(el, g[:, None, None], axis=1)[:, 0]
    ep = jax.nn.softmax(sel, axis=-1)
    vals, idx = lax.top_k(ep, TOP_K)
    gate = pg[:, None] * vals / jnp.sum(vals, axis=-1, keepdims=True)
    return g[:, None] * EXPERTS_PER_GROUP + idx.astype(jnp.int32), gate

def moe_ffn(h, expert_idx, gate, w_e_in, w_e_out):
    N, D = h.shape
    A = N * TOP_K
    flat_e = expert_idx.reshape(A)
    order = jnp.argsort(flat_e)
    sorted_e = flat_e[order]
    tok = order // TOP_K
    counts = jnp.bincount(flat_e, length=N_EXPERTS)
    padded = (counts + DISPATCH_BLOCK - 1) // DISPATCH_BLOCK * DISPATCH_BLOCK
    pad_end = jnp.cumsum(padded)
    pad_start = pad_end - padded
    seg_start = jnp.cumsum(counts) - counts
    dest = pad_start[sorted_e] + jnp.arange(A) - seg_start[sorted_e]
    n_blocks = -(-A // DISPATCH_BLOCK) + N_EXPERTS
    rows = jnp.full((n_blocks * DISPATCH_BLOCK,), N, dtype=jnp.int32).at[dest].set(tok.astype(jnp.int32))
    block_expert = jnp.minimum(jnp.searchsorted(pad_end // DISPATCH_BLOCK, jnp.arange(n_blocks), side='right'),
                               N_EXPERTS - 1).astype(jnp.int32)
    hpad = jnp.concatenate([h, jnp.zeros((1, D), h.dtype)], axis=0)
    xb = hpad[rows].reshape(n_blocks, DISPATCH_BLOCK, D)

    def expert_block(args):
        xblk, e = args
        gt, up = jnp.split(xblk @ w_e_in[e], 2, axis=-1)
        return (jax.nn.silu(gt) * up) @ w_e_out[e]

    yb = lax.map(expert_block, (xb, block_expert)).reshape(-1, D)
    contrib = yb[dest] * gate.reshape(A)[order][:, None].astype(yb.dtype)
    return jnp.zeros((N, D), h.dtype).at[tok].add(contrib.astype(h.dtype))

def channel_mixer(x, ln2_g, w_rg, b_rg, w_re, b_re, w_e_in, w_e_out):
    B, S, D = x.shape
    h = rmsnorm(x, ln2_g).reshape(B * S, D)
    eidx, gate = hier_route(h, w_rg, b_rg, w_re, b_re)
    return x + moe_ffn(h, eidx, gate, w_e_in, w_e_out).reshape(B, S, D)

def setup_inputs(seed: int = 0) -> dict:
    key = jax.random.key(seed)
    ks = jax.random.split(key, 32)
    f32 = jnp.float32
    n_pages = PAST_LEN // PAGE_SIZE
    n_pool = (DEC_BATCH * n_pages * 5) // 4
    nrm = lambda k, shape, s: jax.random.normal(k, shape, f32) * s
    u = jax.random.uniform(ks[10], (DEPTH, D_RNN), f32, 0.9, 0.999)
    s_l = u ** (1.0 / LRU_C)
    page_table = jax.random.permutation(ks[7], n_pool)[:DEC_BATCH * n_pages].reshape(DEC_BATCH, n_pages).astype(jnp.int32)
    return {
        'x_prompt': nrm(ks[0], (BATCH, SEQ, D_MODEL), 1.0),
        'x_sample': nrm(ks[1], (DEC_BATCH, DEC_SEQ, D_MODEL), 1.0),
        'cache_k': nrm(ks[2], (DEPTH, n_pool, PAGE_SIZE, N_QK_HEADS, HEAD_DIM), 1.0),
        'cache_v': nrm(ks[3], (DEPTH, n_pool, PAGE_SIZE, N_DIFF_HEADS, V_DIM), 1.0),
        'state_h': nrm(ks[4], (DEPTH, DEC_BATCH, D_RNN), 0.5),
        'state_conv': nrm(ks[5], (DEPTH, DEC_BATCH, CONV_W - 1, D_RNN), 1.0),
        'page_table': page_table,
        'ln1_g': 1.0 + nrm(ks[6], (DEPTH, D_MODEL), 0.02),
        'w_in': nrm(ks[8], (DEPTH, D_MODEL, D_PROJ), D_MODEL ** -0.5),
        'conv_w': nrm(ks[9], (DEPTH, CONV_W, D_RNN), CONV_W ** -0.5),
        'conv_b': nrm(ks[11], (DEPTH, D_RNN), 0.01),
        'w_ga': nrm(ks[12], (DEPTH, RNN_BLOCKS, RNN_BLOCK_W, RNN_BLOCK_W), RNN_BLOCK_W ** -0.5),
        'b_ga': nrm(ks[13], (DEPTH, RNN_BLOCKS, RNN_BLOCK_W), 0.01),
        'w_gx': nrm(ks[14], (DEPTH, RNN_BLOCKS, RNN_BLOCK_W, RNN_BLOCK_W), RNN_BLOCK_W ** -0.5),
        'b_gx': nrm(ks[15], (DEPTH, RNN_BLOCKS, RNN_BLOCK_W), 0.01),
        'lru_lambda': jnp.log(s_l) - jnp.log1p(-s_l),
        'lam_q1': nrm(ks[16], (DEPTH, HEAD_DIM), 0.1),
        'lam_k1': nrm(ks[17], (DEPTH, HEAD_DIM), 0.1),
        'lam_q2': nrm(ks[18], (DEPTH, HEAD_DIM), 0.1),
        'lam_k2': nrm(ks[19], (DEPTH, HEAD_DIM), 0.1),
        'subln_g': 1.0 + nrm(ks[20], (DEPTH, V_DIM), 0.02),
        'w_out': nrm(ks[21], (DEPTH, D_MIX, D_MODEL), D_MIX ** -0.5),
        'ln2_g': 1.0 + nrm(ks[22], (DEPTH, D_MODEL), 0.02),
        'w_route_group': nrm(ks[23], (DEPTH, D_MODEL, N_GROUPS), D_MODEL ** -0.5),
        'b_route_group': nrm(ks[24], (DEPTH, N_GROUPS), 0.01),
        'w_route_expert': nrm(ks[25], (DEPTH, D_MODEL, N_EXPERTS), D_MODEL ** -0.5),
        'b_route_expert': nrm(ks[26], (DEPTH, N_EXPERTS), 0.01),
        'w_exp_in': nrm(ks[27], (DEPTH, N_EXPERTS, D_MODEL, 2 * D_EXPERT), D_MODEL ** -0.5),
        'w_exp_out': nrm(ks[28], (DEPTH, N_EXPERTS, D_EXPERT, D_MODEL), D_EXPERT ** -0.5),
        'ln_f': 1.0 + nrm(ks[29], (D_MODEL,), 0.02),
    }

def reference(x_prompt, x_sample, cache_k, cache_v, state_h, state_conv, page_table,
              ln1_g, w_in, conv_w, conv_b, w_ga, b_ga, w_gx, b_gx, lru_lambda,
              lam_q1, lam_k1, lam_q2, lam_k2, subln_g, w_out, ln2_g,
              w_route_group, b_route_group, w_route_expert, b_route_expert,
              w_exp_in, w_exp_out, ln_f):
    Bp, Sp, _ = x_prompt.shape
    Bs, Ss, _ = x_sample.shape
    n_pages = page_table.shape[1]
    past_len = n_pages * cache_k.shape[2]
    pos_p = jnp.arange(Sp)
    pos_s = past_len + jnp.arange(Ss)
    kpos_s = jnp.arange(past_len + Ss)
    xp, xs = x_prompt, x_sample
    kp_l, vp_l, hp_l, cp_l, ks_l, vs_l, hs_l, cs_l = [], [], [], [], [], [], [], []
    for l in range(DEPTH):
        lambda_init = 0.8 - 0.6 * math.exp(-0.3 * l)
        w = (ln1_g[l], w_in[l], conv_w[l], conv_b[l], w_ga[l], b_ga[l], w_gx[l], b_gx[l], lru_lambda[l],
             lam_q1[l], lam_k1[l], lam_q2[l], lam_k2[l], subln_g[l], lambda_init, w_out[l])
        attend_p = lambda q, k, v, lam: prompt_attention(q, k, v, pos_p, lam)
        xp, kp, vp, hp, cp = mixer(xp, pos_p, jnp.zeros((Bp, CONV_W - 1, D_RNN), xp.dtype),
                                   jnp.zeros((Bp, D_RNN), xp.dtype), attend_p, *w)
        past_k = cache_k[l][page_table].reshape(Bs, past_len, N_QK_HEADS, HEAD_DIM)
        past_v = cache_v[l][page_table].reshape(Bs, past_len, N_DIFF_HEADS, V_DIM)

        def attend_s(q, k, v, lam, past_k=past_k, past_v=past_v):
            kk = jnp.concatenate([past_k, k.astype(past_k.dtype)], axis=1)
            vv = jnp.concatenate([past_v, v.astype(past_v.dtype)], axis=1)
            return diff_attn_block(q, pos_s, kk, vv, kpos_s, lam)

        xs, k_s, v_s, h_s, c_s = mixer(xs, pos_s, state_conv[l], state_h[l], attend_s, *w)
        xp = channel_mixer(xp, ln2_g[l], w_route_group[l], b_route_group[l], w_route_expert[l],
                           b_route_expert[l], w_exp_in[l], w_exp_out[l])
        xs = channel_mixer(xs, ln2_g[l], w_route_group[l], b_route_group[l], w_route_expert[l],
                           b_route_expert[l], w_exp_in[l], w_exp_out[l])
        kp_l.append(kp); vp_l.append(vp); hp_l.append(hp.astype(xp.dtype)); cp_l.append(cp)
        ks_l.append(k_s.astype(cache_k.dtype)); vs_l.append(v_s.astype(cache_v.dtype))
        hs_l.append(h_s.astype(state_h.dtype)); cs_l.append(c_s.astype(state_conv.dtype))
    y_prompt = rmsnorm(xp, ln_f)
    y_sample = rmsnorm(xs, ln_f)
    return (y_prompt, y_sample,
            jnp.stack(kp_l), jnp.stack(vp_l), jnp.stack(hp_l), jnp.stack(cp_l),
            jnp.stack(ks_l), jnp.stack(vs_l), jnp.stack(hs_l), jnp.stack(cs_l))


_drawn_inputs = setup_inputs


def setup_inputs(seed=0):
    import zlib

    import numpy as np

    out = dict(_drawn_inputs(seed))
    spreads = {}
    factors = {'b_ga': 17.717,
     'b_gx': 6.814,
     'lam_k2': 3.435,
     'b_route_expert': 3.285,
     'ln_f': 24.99,
     'b_route_group': 3.839}
    for name, (base, spread) in spreads.items():
        noise = np.random.default_rng([zlib.crc32(name.encode()), seed]).standard_normal(out[name].shape)
        drawn = base * np.exp(spread * noise) if base else spread * noise
        out[name] = __import__('jax').numpy.asarray(drawn.astype(out[name].dtype))
    for name, factor in factors.items():
        out[name] = (out[name] * factor).astype(out[name].dtype)
    return out
```

```python
import math
from contextlib import ExitStack

import concourse.bass as bass
from concourse import mybir
import numpy as np

ALU = mybir.AluOpType
ACT = mybir.ActivationFunctionType
AX = mybir.AxisListType
F32 = mybir.dt.float32
BF16 = mybir.dt.bfloat16
I32 = mybir.dt.int32

P = 128
D = 1024
KC = D // P
SEQ = 512
NT = SEQ // P
NTT = NT + 1
NS = 8
DEPTH = 2
D_RNN = 512
NC = D_RNN // P
CONV_W = 4
HEAD = 64
NG = 4
NH = 2 * NG
D_PROJ = 2560
PAST = 256
PAGE = 128
N_PAGES = PAST // PAGE
N_EXP = 32
N_GRP = 4
EPG = 8
D_EXP = 512
CAP = 64
MAX_OVF = (SEQ + NS) * 2 // CAP
NBLK = N_EXP + MAX_OVF
SCALE = HEAD ** -0.5
EPS = 1e-6
SUB_EPS = 1e-5
NEG = -1e30
WBUF = 12288
NBUF = 3

CONSTS = [("cos", NT * 64), ("sin", NT * 64), ("cos_s", 64), ("sin_s", 64), ("ident", P), ("mask", P),
          ("tri", P), ("iota_e", N_EXP), ("iota_blk", NBLK), ("cap_steps", MAX_OVF), ("iota_ovf", MAX_OVF),
          ("slot_row", P), ("tok", NTT), ("delta", NS * 32), ("first4", N_GRP), ("first8", EPG),
          ("half", 1), ("neghalf", 8), ("sel_b", 64), ("sel_t", NS), ("mask_h", NH), ("mask_g", NG),
          ("even", 1), ("odd", 1), ("one", 1)]
C_AT = {}
_at = 0
for _name, _w in CONSTS:
    C_AT[_name] = (_at, _at + _w)
    _at += _w
C_W = _at
PF = {"conv_w": (0, 16), "conv_b": (16, 20), "b_ga": (20, 24), "b_gx": (24, 28), "lam": (28, 32),
      "g1": (32, 40), "g2": (40, 48)}
PF_W = 48
PB = {"subln": (0, 128), "b_route": (128, 164), "lq1": (164, 228), "lk1": (228, 292), "lq2": (292, 356),
      "lk2": (356, 420), "lam_init": (420, 421), "one_less": (421, 422)}
PB_W = 422


def chain(eng, sem):
    count = [0]

    def settle(ins):
        count[0] += 1
        ins.then_inc(sem, 1)
        eng.wait_ge(sem, count[0])
        return ins
    return settle


def hybrid_step(nc, A, O):
    ctx = ExitStack()
    with ctx:
        def sb(name, shape, dt=F32):
            return ctx.enter_context(nc.sbuf_tensor(name, shape, dt))

        all_sems = []

        def sem(name):
            s = ctx.enter_context(nc.semaphore(name))
            all_sems.append(s)
            return s

        def once(name):
            return ctx.enter_context(nc.semaphore(name))

        def barrier_and_clear(sems):
            ids = range(sems[0].num, sems[-1].num + 1)
            assert len(ids) == len(sems)
            nc.all_engine_barrier()
            nc.gpsimd.dma_reset(ids)
            nc.gpsimd.sem_clear(ids)
            nc.all_engine_barrier()

        n_pool = A["cache_k"].shape[1]
        xn_dram = nc.dram_tensor("normed_rows", (SEQ + NS, D), F32, kind="Internal").ap()
        y_dram = nc.dram_tensor("expert_rows", (NBLK * CAP, D), F32, kind="Internal").ap()

        W = sb("W", [P, NBUF * WBUF])
        x = sb("x", [P, NTT, D])
        v_nat = sb("v_nat", [P, NT, 512])
        qT = sb("qT", [P, NG, SEQ])
        R = sb("R", [P, 6, 512])
        C = sb("C", [P, C_W])
        gate_w = sb("gate_w", [P, 2, NC, P])
        pf = sb("pf", [P, PF_W])
        pb = sb("pb", [P, PB_W])
        route_w = R[:, 5, 224:512].rearrange("p (k n) -> p k n", k=KC)
        hTs = sb("hTs", [P, KC, NS])
        yTs = sb("yTs", [P, KC, NS])
        ident_b = sb("ident_b", [P, P], BF16)
        mask_b = sb("mask_b", [P, P], BF16)
        tri_b = sb("tri_b", [P, P], BF16)
        ones_b = sb("ones_b", [P, P], BF16)
        pages = sb("pages", [1, NS * N_PAGES], I32)
        hc = sb("hc", [P, 2, NC])
        hbias = sb("hbias", [P, 2, NC])
        sp = sb("sp", [P, 6, NC])
        neglam = sb("neglam", [P, 4])
        subg = sb("subg", [P, P])
        st = sb("st", [P, 4, NTT])
        idx_i = sb("idx_i", [P, NBLK], I32)
        slot_i = sb("slot_i", [P, 2, NTT], I32)
        gate = sb("gate", [P, 2, NTT])
        ovf_i = sb("ovf_i", [P, MAX_OVF + 1], I32)
        cur = sb("cur", [P, 1], I32)
        PS = ctx.enter_context(nc.psum_tensor("PS", [P, 8, 512], F32))

        def c(name, rows=P):
            a, b = C_AT[name]
            return C[0:rows, a:b]

        def f(name):
            a, b = PF[name]
            return pf[:, a:b]

        def b_(name, rows=P):
            a, b = PB[name]
            return pb[0:rows, a:b]

        ident = c("ident")
        wg = W[:, 0:4096].rearrange("p (k n) -> p k n", k=KC)
        wx = W[:, 4096:8192].rearrange("p (k n) -> p k n", k=KC)
        wqkv = [W[:, 8192 + 4096 * i:12288 + 4096 * i].rearrange("p (k n) -> p k n", k=KC) for i in range(3)]
        hT = W[:, 20480:24576].rearrange("p (k n) -> p k n", k=KC)
        kc_nat = W[:, 0:8192].rearrange("p (g n) -> p g n", g=16)
        vc_nat = W[:, 8192:16384].rearrange("p (g n) -> p g n", g=16)
        RN = 24576
        w_out = W[:, 16384:24576].rearrange("p (k n) -> p k n", k=KC)
        yT = W[:, 32768:36864].rearrange("p (k n) -> p k n", k=KC)
        kT = yT[:, 4:8, :]

        def rn(a, n, rows=P):
            return W[0:rows, RN + a:RN + a + n]

        sxg = rn(0, 1024, NS)
        stc = rn(1024, 512, NS * 3)
        sqkv = [rn(512 * i, 512, NS) for i in range(3)]
        xn = [W[:, 32768:33792], W[:, 33792:34816]]
        junk = W[:, 34816:35840]
        sth = rn(1536, 512, NS)
        xr = [rn(2048, 516), rn(2564, 516)]
        xc = [rn(3080 + 512 * i, 512) for i in range(NC)]
        ra, ix, aa, th = (rn(5128 + 512 * i, 512) for i in range(4))
        sT = rn(7176, 192)
        xcs = rn(7368, 32).rearrange("p (c b) -> p c b", c=NC)
        s_ri = rn(7400, 64).rearrange("p (g c b) -> p g c b", g=2, c=NC)
        s_la, s_a, s_th, s_t1, s_t2 = (rn(7464 + 32 * i, 32).rearrange("p (c b) -> p c b", c=NC) for i in range(5))
        small = rn(7624, 48).rearrange("p (c n) -> p c n", c=NC)
        small_rows = rn(7672, 512, 12)
        xe = [v_nat[:, i, :] for i in range(NBUF)]
        xTe = [qT[:, i, :].rearrange("p (h c t) -> p h c t", h=2, c=4) for i in range(2)]
        hs = [R[:, 0, 256 * i:256 * i + 256] for i in range(2)]
        hh = [R[:, 1, 256 * i:256 * i + 256] for i in range(2)]
        hTe = [R[:, 2, 256 * i:256 * i + 256].rearrange("p (j h t) -> p j h t", j=2, h=2) for i in range(2)]
        ye = [R[:, 3 + i, :] for i in range(2)]

        def expert_in(i):
            return W[:, WBUF * i:WBUF * i + 8192].rearrange("p (k n) -> p k n", k=KC)

        def expert_out(i):
            return W[:, WBUF * i + 8192:WBUF * (i + 1)].rearrange("p (k n) -> p k n", k=4)

        w_in_rows = A["w_exp_in"].rearrange("l e (k p) n -> (l e) p k n", p=P)
        w_out_rows = A["w_exp_out"].rearrange("l e (k p) n -> (l e) p k n", p=P)
        y_blocks = y_dram.rearrange("(j r) n -> j r n", r=CAP)
        ck = A["cache_k"].rearrange("l g p h d -> (l g) p (h d)")
        cv = A["cache_v"].rearrange("l g p h d -> (l g) p (h d)")

        s_start = once("start_loads")
        s_made = once("tables_made")
        s_zero = once("overflow_rows_zeroed")
        s_cleared = once("zeros_made")
        with nc.Block() as block:
            @block.gpsimd
            def _(pool):
                pool.memset(v_nat[:, :, :], 0.0).then_inc(s_cleared, 1)
                pool.wait_ge(s_cleared, 1)
                rest = y_dram[N_EXP * CAP:, :].rearrange("(a p r) n -> a p (r n)", a=4, p=P)
                for i in range(4):
                    pool.dma_start(rest[i], v_nat[:, :, :].rearrange("p a n -> p (a n)")).then_inc(s_zero, 16)

            @block.sync
            def _(sp_):
                sp_.dma_start(x[:, 0:NT, :], A["x_prompt"].rearrange("b (t p) d -> p (b t) d", p=P)).then_inc(s_start, 16)
                sp_.dma_start(x[0:NS, NT, :], A["x_sample"].rearrange("b s d -> (b s) d")).then_inc(s_start, 16)
                sp_.dma_start(C[:, :], A["consts"]).then_inc(s_start, 16)
                sp_.dma_start(pages[:, :], A["page_row"]).then_inc(s_start, 16)
                sp_.wait_ge(s_start, 64)

            @block.vector
            def _(dve):
                dve.wait_ge(s_start, 64)
                dve.tensor_copy(ident_b[:, :], ident).then_inc(s_made, 1)
                dve.tensor_copy(mask_b[:, :], c("mask")).then_inc(s_made, 1)
                dve.tensor_copy(tri_b[:, :], c("tri")).then_inc(s_made, 1)
                dve.memset(ones_b[:, :], 1.0).then_inc(s_made, 1)
                dve.wait_ge(s_made, 4)

        params = sem("params_loaded")
        gate_params = sem("gate_params_loaded")
        states = sem("states_loaded")
        w_ready = [sem(f"w_in_{n}_loaded") for n in "gxqkv"]
        sumsq = sem("sum_of_squares")
        mean_eps = sem("mean_plus_eps")
        rstd = sem("rstd_ready")
        xn_ready = sem("normed_ready")
        turned = sem("normed_turned")
        hT_ready = sem("hT_ready")
        proj = sem("projection_done")
        gx_read = sem("gate_and_x_read")
        rope_read = sem("rotary_read_psum")
        rope_sum = sem("rotary_done")
        rope_turned = sem("rotary_turned")
        rope_kept = sem("rotary_turned_kept")
        k_stored = [sem("k_rows_stored_even"), sem("k_rows_stored_odd")]
        stored = sem("project_rows_stored")
        v_kept = sem("v_kept")
        conv_done = sem("conv_done")
        gates_done = sem("gate_products_done")
        gates_read = sem("gate_products_read")
        decay_done = sem("decay_done")
        m2_done = sem("one_less_a2_done")
        mult_done = sem("mult_done")
        scan_done = sem("scan_done")
        y_done = sem("rnn_output_done")
        s_proj = sem("sample_projection_done")
        s_read = sem("sample_projection_read")
        s_turned = sem("sample_turned")
        s_kept = sem("sample_turned_kept")
        s_conv = sem("sample_conv_done")
        s_gates = sem("sample_gates_done")
        s_pe = sem("sample_steps_dve")
        s_act = sem("sample_steps_act")
        small_turned = sem("last_states_turned")
        small_kept = sem("last_states_kept")
        k_pages = sem("k_pages_loaded")
        dve1, act1, pool1 = sem("dve_steps_1"), sem("act_steps_1"), sem("pool_steps_1")
        const_done = sem("recurrence_constants")
        sp_exp = sem("softplus_exp")

        v_pages = sem("v_pages_loaded")
        a_row = sem("sample_rotary_done")
        a_bc = sem("query_spread")
        a_prod = sem("query_product_done")
        a_s = sem("sample_scores_done")
        a_pe = sem("sample_attention_pe")
        a_dve = sem("sample_attention_dve")
        a_act = sem("sample_attention_act")
        a_pool = sem("sample_attention_pool")
        a_stored = sem("sample_rows_stored")
        a_done = sem("sample_attention_done")
        lam_dve, lam_act = sem("lambda_sums"), sem("lambda_exps")
        scores = sem("scores_done")
        negmax = sem("negmax_ready")
        exps = sem("exps_done")
        amap = sem("map_difference_done")
        map_turned = sem("map_turned")
        map_kept = sem("map_turned_kept")
        av = sem("av_done")
        o_read = sem("o_read")
        o_var = sem("o_mean_square")
        o_rstd = sem("o_rstd")
        o_norm = sem("o_normed")
        o_turned = sem("o_turned")
        o_kept = sem("o_turned_kept")
        dve2, act2, pool2 = sem("dve_steps_2"), sem("act_steps_2"), sem("pool_steps_2")
        w_out_ready = sem("w_out_loaded")
        e_in = [sem(f"expert_in_{i}_loaded") for i in range(NBUF)]
        e_out = [sem(f"expert_out_{i}_loaded") for i in range(NBUF)]

        w_route = sem("router_weights_loaded")
        op_done = sem("output_product_done")
        x_new = sem("x_updated")
        sumsq2, mean2, rstd2, xn2_ready = sem("sumsq_2"), sem("mean_eps_2"), sem("rstd_2"), sem("normed_2")
        xn2_stored = [sem("normed_stored_even"), sem("normed_stored_odd")]
        turned2, h2_ready, logits = sem("turned_2"), sem("h2T_ready"), sem("logits_done")
        hot = sem("expert_hot_ready")
        ranks = sem("ranks_done")
        place = sem("slot_hot_ready")
        slots_done = sem("slot_tokens_done")
        r_act_in, r_act = sem("router_exp_input"), sem("router_exp_done")
        dve3, act3 = sem("dve_steps_3"), sem("act_steps_3")

        gathered = [sem(f"rows_gathered_{i}") for i in range(NBUF)]
        xe_turned = sem("rows_turned")
        xTe_ready = sem("xT_ready")
        in_done = sem("expert_in_done")
        silu_done = sem("silu_done")
        h_ready = sem("h_ready")
        h_turned = sem("h_turned")
        hT_kept = sem("h_turned_kept")
        out_done = sem("expert_out_done")
        y_kept = sem("expert_rows_kept")
        y_stored = [sem("expert_rows_stored_even"), sem("expert_rows_stored_odd")]

        in_loop = len(all_sems)
        v_w, v_g, v_t, v_x, v_i, v_s, v_h, v_ht, v_hk, v_o, v_y, v_st = (
            sem("ovf_" + n) for n in ("weights", "rows", "turned", "xT", "in", "silu", "h", "h_turned", "h_kept",
                                      "out", "kept", "stored"))
        ovf_sems = all_sems[in_loop:]

        got = [sem("slot_rows_0"), sem("slot_rows_1"), sem("slot_rows_2"), sem("slot_rows_3")]
        added = sem("slot_rows_added")
        dve4 = sem("dve_steps_4")

        with nc.Fori(0, DEPTH) as layer:
            with nc.Block() as block:
                @block.sync
                def _(sp_):
                    def w_cols(dst, col, s):
                        src = A["w_in"][bass.ds(layer, 1), :, col:col + 512].rearrange("l (k p) n -> p (l k) n", p=P)
                        sp_.dma_start(dst, src).then_inc(s, 16)

                    sp_.dma_start(pf[:, :], A["pf"][bass.ds(layer, 1)].rearrange("l p n -> p (l n)")).then_inc(params, 16)
                    sp_.dma_start(pb[:, :], A["pb"][bass.ds(layer, 1)].rearrange("l p n -> p (l n)")).then_inc(params, 16)
                    w_cols(wg, 512, w_ready[0])
                    w_cols(wx, 0, w_ready[1])
                    sp_.dma_start(gate_w[:, :, :, :], A["gate_w"][bass.ds(layer, 1)].rearrange("l p g c n -> p (l g) c n")).then_inc(gate_params, 16)
                    sp_.dma_start(stc, A["state_conv"][bass.ds(layer, 1)].rearrange("l b j n -> (l b j) n")).then_inc(states, 16)
                    sp_.dma_start(sth, A["state_h"][bass.ds(layer, 1)].rearrange("l b n -> (l b) n")).then_inc(states, 16)
                    for i in range(3):
                        w_cols(wqkv[i], 1024 + 512 * i, w_ready[2 + i])
                    sp_.wait_ge(s_proj, 1)
                    with sp_.Fori(0, NS * N_PAGES) as i:
                        page = sp_.value_load(pages[0:1, bass.ds(i, 1)], min_val=0, max_val=n_pool - 1)
                        sp_.dma_start(kc_nat[:, bass.ds(i, 1), :], ck[bass.ds(page + layer * n_pool, 1)].rearrange("g p n -> p g n")).then_inc(k_pages, 16)

                @block.scalar
                def _(act):
                    settle = chain(act, act1)

                    def square(t):
                        n = P if t < NT else NS
                        act.activation(junk[0:n, :], x[0:n, t, :], ACT.Square, accum_out=st[0:n, 0, t:t + 1]).then_inc(sumsq, 1)
                        act.wait_ge(sumsq, t + 1)

                    def scale(t):
                        n = P if t < NT else NS
                        act.wait_ge(rstd, t + 1)
                        if t >= 2:
                            act.wait_ge(turned, 2 * (t - 1))
                        act.activation(xn[t % 2][0:n, :], x[0:n, t, :], ACT.Copy, scale=st[0:n, 2, t:t + 1]).then_inc(xn_ready, 1)

                    act.wait_ge(sp_exp, 1)
                    act.activation(sp[:, 1, :], sp[:, 0, :], ACT.Exp, scale=-1.0).then_inc(sp_exp, 1)
                    square(0)
                    for t in range(NTT):
                        if t + 1 < NTT:
                            square(t + 1)
                        scale(t)
                    act.wait_ge(hT_ready, 2 * NT + 1)
                    for i in range(NC):
                        act.wait_ge(proj, i + 1)
                        act.activation(yT[:, i, :], PS[:, i % 4, :], ACT.Gelu_apprx_tanh).then_inc(gx_read, 1)
                    for i in range(NC):
                        act.wait_ge(proj, NC + i + 1)
                        if i == 0:
                            act.wait_ge(const_done, 2)
                        if i >= 2:
                            act.wait_ge(conv_done, i - 1)
                        act.activation(xr[i % 2][:, 3:515], PS[:, (NC + i) % 4, :], ACT.Copy).then_inc(gx_read, 1)
                    act.wait_ge(s_proj, 1)
                    for j in range(2):
                        act.activation(sxg[:, 512 + 256 * j:768 + 256 * j], PS[32 * j:32 * j + NS, 4, 0:256], ACT.Gelu_apprx_tanh).then_inc(s_read, 1)
                    for j in range(2):
                        act.activation(sxg[:, 256 * j:256 * j + 256], PS[64 + 32 * j:64 + 32 * j + NS, 4, 0:256], ACT.Copy).then_inc(s_read, 1)

                    def keep_turned(i):
                        t = i // 2
                        dst = (qT if i % 2 == 0 else kT)[:, :, t * P:(t + 1) * P]
                        act.wait_ge(rope_turned, i + 1)
                        act.activation(dst, PS[:, 7, :].rearrange("p (j n) -> p j n", j=NG), ACT.Copy).then_inc(rope_kept, 1)

                    for t in range(NT):
                        if t == 1:
                            act.wait_ge(s_turned, 1)
                            act.activation(sT, PS[:, 4, 0:192], ACT.Copy).then_inc(s_kept, 1)
                        if t >= 1:
                            keep_turned(2 * t - 2)
                            keep_turned(2 * t - 1)
                        i = t
                        act.wait_ge(gates_done, i + 1)
                        if i >= 1:
                            act.wait_ge(y_done, i)
                        settle(act.activation(ra, PS[:, 5, :], ACT.Tanh, scale=0.5, bias=hbias[:, 0, i:i + 1]))
                        act.activation(ix, PS[:, 6, :], ACT.Tanh, scale=0.5, bias=hbias[:, 1, i:i + 1]).then_inc(gates_read, 1)
                        act.activation(th, ra, ACT.Tanh, scale=hc[:, 1, i:i + 1], bias=hc[:, 1, i:i + 1]).then_inc(decay_done, 1)
                        settle(act.activation(aa, ra, ACT.Exp, scale=hc[:, 0, i:i + 1], bias=hc[:, 0, i:i + 1]))
                        act.activation(ra, aa, ACT.Square).then_inc(decay_done, 1)
                        act.wait_ge(m2_done, i + 1)
                        act.activation(th, th, ACT.Sqrt).then_inc(mult_done, 1)
                        act.wait_ge(proj, 8 + 3 * t + 3)
                        if t == 0:
                            act.wait_ge(s_zero, 64)
                        act.activation(v_nat[:, t, :], PS[:, (8 + 3 * t + 2) % 4, :], ACT.Copy).then_inc(v_kept, 1)
                    keep_turned(6)
                    keep_turned(7)
                    act.wait_ge(s_pe, 1)
                    act.activation(s_ri, s_ri, ACT.Tanh).then_inc(s_act, 1)
                    act.wait_ge(s_pe, 2)
                    act.activation(s_a, s_la, ACT.Exp).then_inc(s_act, 1)
                    act.activation(s_th, s_la, ACT.Tanh, scale=-1.0).then_inc(s_act, 1)
                    act.wait_ge(s_pe, 3)
                    act.activation(s_th, s_th, ACT.Sqrt).then_inc(s_act, 1)
                    act.wait_ge(s_proj, 2)
                    act.wait_ge(s_turned, 1)
                    act.wait_ge(stored, 16 * (NT + 2))
                    for j in range(3):
                        act.activation(sqkv[j], PS[32 * j:32 * j + NS, 4, :], ACT.Copy).then_inc(s_read, 1)
                    act.wait_ge(small_turned, 1)
                    act.activation(small_rows, PS[0:12, 7, :], ACT.Copy).then_inc(small_kept, 1)

                def spread(dve, t):
                    g1 = f("g1")
                    if t < NT:
                        for h in range(2):
                            u = 2 * t + h
                            dve.wait_ge(turned, u + 1)
                            dve.tensor_tensor(hT[:, 4 * h:4 * h + 4, t * P:(t + 1) * P], PS[:, u % 4, :].rearrange("p (k n) -> p k n", k=4),
                                              g1[:, 4 * h:4 * h + 4].unsqueeze(2).to_broadcast([P, 4, P]), ALU.mult).then_inc(hT_ready, 1)
                    else:
                        dve.wait_ge(turned, 2 * NT + 1)
                        dve.tensor_tensor(hTs[:, :, :], PS[:, 0, 0:64].rearrange("p (k n) -> p k n", k=KC),
                                          g1.unsqueeze(2).to_broadcast([P, KC, NS]), ALU.mult).then_inc(hT_ready, 1)

                @block.vector
                def _(dve):
                    settle = chain(dve, dve1)
                    dve.wait_ge(params, 32)
                    settle(dve.tensor_scalar(sp[:, 5, :], f("lam"), -1.0, None, ALU.mult))
                    settle(dve.tensor_tensor(sp[:, 0, :], f("lam"), sp[:, 5, :], ALU.max))
                    dve.tensor_scalar(sp[:, 5, :], sp[:, 5, :], 0.0, None, ALU.max).then_inc(sp_exp, 1)
                    dve.wait_ge(sp_exp, 2)
                    settle(dve.tensor_scalar(sp[:, 2, :], sp[:, 1, :], 2.0, None, ALU.add))
                    settle(dve.reciprocal(sp[:, 2, :], sp[:, 2, :]))
                    settle(dve.tensor_tensor(sp[:, 2, :], sp[:, 2, :], sp[:, 1, :], ALU.mult))
                    settle(dve.tensor_tensor(sp[:, 3, :], sp[:, 2, :], sp[:, 2, :], ALU.mult))
                    settle(dve.tensor_scalar(sp[:, 4, :], sp[:, 3, :], 1.0 / 17, 1.0 / 15, ALU.mult, ALU.add))
                    for k in (13, 11, 9, 7, 5, 3, 1):
                        settle(dve.tensor_tensor(sp[:, 4, :], sp[:, 4, :], sp[:, 3, :], ALU.mult))
                        settle(dve.tensor_scalar(sp[:, 4, :], sp[:, 4, :], 1.0 / k, None, ALU.add))
                    settle(dve.tensor_tensor(sp[:, 4, :], sp[:, 4, :], sp[:, 2, :], ALU.mult))
                    settle(dve.scalar_tensor_tensor(sp[:, 4, :], sp[:, 4, :], 2.0, sp[:, 5, :], ALU.mult, ALU.add))
                    settle(dve.tensor_scalar(hc[:, 0, :], sp[:, 4, :], -4.0, None, ALU.mult))
                    settle(dve.tensor_scalar(hc[:, 1, :], sp[:, 4, :], 4.0, None, ALU.mult))
                    settle(dve.tensor_scalar(hbias[:, 0, :], f("b_ga"), 0.5, None, ALU.mult))
                    dve.tensor_scalar(hbias[:, 1, :], f("b_gx"), 0.5, None, ALU.mult).then_inc(const_done, 1)
                    settle(dve.memset(xr[0][:, 0:3], 0.0))
                    dve.memset(xr[1][:, 0:3], 0.0).then_inc(const_done, 1)
                    for t in range(NTT):
                        n = P if t < NT else NS
                        dve.wait_ge(sumsq, t + 1)
                        dve.tensor_scalar(st[0:n, 1, t:t + 1], st[0:n, 0, t:t + 1], 1.0 / D, EPS, ALU.mult, ALU.add).then_inc(mean_eps, 1)
                        if t >= 1:
                            spread(dve, t - 1)
                    spread(dve, NT)

                    for i in range(NC):
                        cw, cb = f("conv_w"), f("conv_b")
                        dve.wait_ge(gx_read, NC + i + 1)
                        settle(dve.tensor_scalar(xc[i], xr[i % 2][:, 0:512], cw[:, 4 * i:4 * i + 1], cb[:, i:i + 1], ALU.mult, ALU.add))
                        settle(dve.tensor_copy(small[:, i, 9:12], xr[i % 2][:, 512:515]))
                        for j in range(1, CONV_W):
                            ins = dve.scalar_tensor_tensor(xc[i], xr[i % 2][:, j:j + 512], cw[:, 4 * i + j:4 * i + j + 1], xc[i], ALU.mult, ALU.add)
                            if j < CONV_W - 1:
                                settle(ins)
                        ins.then_inc(conv_done, 1)
                    dve.wait_ge(conv_done, NC)

                    def rotary(i):
                        t, which = i // 2, i % 2
                        unit = 8 + 3 * t + which
                        bank = PS[:, unit % 4, :].rearrange("p (h n) -> p h n", h=NH)
                        A_ = R[:, i % 4, :].rearrange("p (h n) -> p h n", h=NH)
                        B_ = R[:, 4 + i % 2, :].rearrange("p (h n) -> p h n", h=NH)
                        cos = c("cos").rearrange("p (t n) -> p t n", t=NT)[:, t:t + 1, :].to_broadcast([P, NH, 64])
                        sin = c("sin").rearrange("p (t n) -> p t n", t=NT)[:, t:t + 1, :]
                        dve.wait_ge(proj, unit + 1)
                        if i >= 4:
                            dve.wait_ge(rope_turned, i - 3)
                            if which == 1:
                                dve.wait_ge(k_stored[t % 2], 16 * (t // 2))
                        if i >= 2:
                            dve.wait_ge(rope_sum, i - 1)
                        settle(dve.tensor_tensor(A_, bank, cos, ALU.mult))
                        settle(dve.tensor_tensor(B_[:, :, 0:32], bank[:, :, 32:64], sin[:, :, 0:32].to_broadcast([P, NH, 32]), ALU.mult))
                        dve.tensor_tensor(B_[:, :, 32:64], bank[:, :, 0:32], sin[:, :, 32:64].to_broadcast([P, NH, 32]), ALU.mult).then_inc(rope_read, 1)

                    def wide(a):
                        return a.unsqueeze(2).to_broadcast([P, NC, NS])

                    for t in range(NT):
                        i = t
                        rotary(2 * t)
                        rotary(2 * t + 1)
                        dve.wait_ge(decay_done, 2 * i + 2)
                        dve.scalar_tensor_tensor(th, ra, 1.0, th, ALU.add, ALU.mult).then_inc(m2_done, 1)
                        dve.wait_ge(gates_read, i + 1)
                        settle(dve.scalar_tensor_tensor(ix, ix, 1.0, xc[i], ALU.add, ALU.mult))
                        dve.wait_ge(mult_done, i + 1)
                        settle(dve.memset(th[:, 0:1], 1.0))
                        settle(dve.scalar_tensor_tensor(ix, ix, 0.5, th, ALU.mult, ALU.mult))
                        settle(dve.tensor_tensor_scan(ra, aa, ix, 0.0, ALU.mult, ALU.add))
                        dve.tensor_copy(small[:, i, 8:9], ra[:, 511:512]).then_inc(scan_done, 1)
                        if t == 1:
                            dve.wait_ge(s_kept, 1)
                            kept = sT[:, 64:160].rearrange("p (c b j) -> p c b j", c=NC, b=NS)
                            cw = f("conv_w").rearrange("p (c j) -> p c j", c=NC)
                            settle(dve.tensor_tensor(xcs, sT[:, 0:32].rearrange("p (c b) -> p c b", c=NC), wide(cw[:, :, 3]), ALU.mult))
                            for j in range(3):
                                settle(dve.tensor_tensor(s_t1, kept[:, :, :, j], wide(cw[:, :, j]), ALU.mult))
                                settle(dve.tensor_tensor(xcs, xcs, s_t1, ALU.add))
                            dve.tensor_tensor(xcs, xcs, wide(f("conv_b")), ALU.add).then_inc(s_conv, 1)
                    dve.wait_ge(s_gates, 1)
                    for g in range(2):
                        ins = dve.scalar_tensor_tensor(s_ri[:, g], PS[:, 4, 256 + 32 * g:288 + 32 * g].rearrange("p (c b) -> p c b", c=NC), 0.5,
                                                       wide(hbias[:, g, :]), ALU.mult, ALU.add)
                        if g == 0:
                            settle(ins)
                    ins.then_inc(s_pe, 1)
                    dve.wait_ge(s_act, 1)
                    dve.scalar_tensor_tensor(s_la, s_ri[:, 0], 1.0, wide(hc[:, 0, :]), ALU.add, ALU.mult).then_inc(s_pe, 1)
                    dve.wait_ge(s_act, 3)
                    settle(dve.tensor_tensor(s_t1, s_a, s_a, ALU.mult))
                    dve.scalar_tensor_tensor(s_th, s_t1, 1.0, s_th, ALU.add, ALU.mult).then_inc(s_pe, 1)
                    settle(dve.scalar_tensor_tensor(s_t2, s_ri[:, 1], 1.0, xcs, ALU.add, ALU.mult))
                    dve.wait_ge(s_act, 4)
                    settle(dve.scalar_tensor_tensor(s_t2, s_t2, 0.5, s_th, ALU.mult, ALU.mult))
                    settle(dve.tensor_tensor(s_t1, s_a, sT[:, 160:192].rearrange("p (c b) -> p c b", c=NC), ALU.mult))
                    settle(dve.tensor_tensor(small[:, :, 0:NS], s_t1, s_t2, ALU.add))
                    dve.tensor_tensor(yTs[:, 0:NC, :], small[:, :, 0:NS], sT[:, 32:64].rearrange("p (c b) -> p c b", c=NC), ALU.mult).then_inc(s_pe, 1)

                @block.gpsimd
                def _(pool):
                    settle = chain(pool, pool1)
                    for t in range(NTT):
                        n = P if t < NT else NS
                        pool.wait_ge(mean_eps, t + 1)
                        pool.tensor_tensor(st[0:n, 2, t:t + 1], st[0:n, 1, t:t + 1], c("neghalf", n)[:, 0:1], ALU.pow).then_inc(rstd, 1)
                    conv_dst = O["new_conv_sample"][bass.ds(layer, 1)].rearrange("l b j n -> (l b) j n")
                    conv_src = A["state_conv"][bass.ds(layer, 1)].rearrange("l b j n -> (l b) j n")
                    pool.dma_start(conv_dst[:, 0:2, :], conv_src[:, 1:3, :]).then_inc(stored, 16)
                    pool.wait_ge(s_read, 4)
                    pool.dma_start(conv_dst[:, 2, :], sxg[:, 0:512]).then_inc(stored, 16)
                    new_k = O["new_k_prompt"][bass.ds(layer, 1)].rearrange("l b (t p) h d -> (l b t) p (h d)", p=P)
                    new_v = O["new_v_prompt"][bass.ds(layer, 1)].rearrange("l b (t p) h d -> (l b t) p (h d)", p=P)
                    for t in range(NT):
                        for i in (2 * t, 2 * t + 1):
                            pool.wait_ge(rope_read, i + 1)
                            pool.tensor_tensor(R[:, i % 4, :], R[:, i % 4, :], R[:, 4 + i % 2, :], ALU.add).then_inc(rope_sum, 1)
                        pool.wait_ge(rope_sum, 2 * t + 2)
                        pool.dma_start(new_k[t], R[:, (2 * t + 1) % 4, :]).then_inc(k_stored[t % 2], 16)
                        pool.wait_ge(scan_done, t + 1)
                        pool.tensor_tensor(yT[:, t, :], yT[:, t, :], ra, ALU.mult).then_inc(y_done, 1)
                        pool.wait_ge(v_kept, t + 1)
                        pool.dma_start(new_v[t], v_nat[:, t, :]).then_inc(stored, 16)
                    pool.wait_ge(small_kept, 1)
                    pool.dma_start(O["new_h_sample"][bass.ds(layer, 1)].rearrange("l b n -> (l b) n"), small_rows[0:NS, :]).then_inc(stored, 16)
                    pool.dma_start(O["new_h_prompt"][bass.ds(layer, 1)].rearrange("l b n -> (l b) n"), small_rows[NS:NS + 1, :]).then_inc(stored, 16)
                    pool.dma_start(O["new_conv_prompt"][bass.ds(layer, 1)].rearrange("l b j n -> (l b j) n"), small_rows[NS + 1:12, :]).then_inc(stored, 16)
                    pool.wait_ge(stored, 16 * (NT + 5))
                    for s in k_stored:
                        pool.wait_ge(s, 32)

                @block.tensor
                def _(pe):
                    for t in range(NT):
                        pe.wait_ge(xn_ready, t + 1)
                        for h in range(2):
                            u = 2 * t + h
                            if u >= 4:
                                pe.wait_ge(hT_ready, u - 3)
                            for j in range(4):
                                k = 4 * h + j
                                ins = pe.transpose(PS[:, u % 4, j * P:(j + 1) * P], xn[t % 2][:, k * P:(k + 1) * P], ident)
                            ins.then_inc(turned, 1)
                    pe.wait_ge(xn_ready, NTT)
                    pe.wait_ge(hT_ready, 5)
                    for k in range(KC):
                        ins = pe.transpose(PS[:, 0, k * NS:(k + 1) * NS], xn[0][0:NS, k * P:(k + 1) * P], ident[0:NS, 0:NS])
                    ins.then_inc(turned, 1)
                    pe.wait_ge(hT_ready, 2 * NT + 1)

                    def bank_free(u):
                        if 4 <= u < 12:
                            pe.wait_ge(gx_read, u - 3)
                        elif u >= 12:
                            t, s = divmod(u - 12, 3)
                            if s < 2:
                                pe.wait_ge(rope_read, 2 * t + s + 1)
                            else:
                                pe.wait_ge(v_kept, t + 1)

                    for part, w in ((0, wg), (1, wx)):
                        pe.wait_ge(w_ready[part], 16)
                        for i in range(NC):
                            u = part * NC + i
                            bank_free(u)
                            for k in range(KC):
                                ins = pe.matmul(PS[:, u % 4, :], w[:, k, i * P:(i + 1) * P], hT[:, k, :], start=(k == 0), stop=(k == KC - 1))
                            ins.then_inc(proj, 1)
                    for k in range(KC):
                        for j in range(4):
                            w = wg if j < 2 else wx
                            ins = pe.matmul(PS[32 * j:32 * j + NS, 4, 0:256], hTs[:, k, :], w[:, k, 256 * (j % 2):256 * (j % 2) + 256],
                                            start=(k == 0), stop=(k == KC - 1))
                    ins.then_inc(s_proj, 1)

                    def turn_rotary(i):
                        pe.wait_ge(rope_sum, i + 1)
                        if i >= 1:
                            pe.wait_ge(rope_kept, i)
                        for j in range(NG):
                            ins = pe.transpose(PS[:, 7, j * P:(j + 1) * P], R[:, i % 4, j * P:(j + 1) * P], ident)
                        ins.then_inc(rope_turned, 1)

                    for t in range(NT):
                        for s in range(3):
                            if t >= 1 and s < 2:
                                turn_rotary(2 * t - 2 + s)
                            if s == 2:
                                if t == 0:
                                    pe.wait_ge(gate_params, 16)
                                pe.wait_ge(conv_done, t + 1)
                                if t >= 1:
                                    pe.wait_ge(gates_read, t)
                                pe.matmul(PS[:, 5, :], gate_w[:, 0, t, :], xc[t], start=True, stop=True)
                                pe.matmul(PS[:, 6, :], gate_w[:, 1, t, :], xc[t], start=True, stop=True).then_inc(gates_done, 1)
                            u = 8 + 3 * t + s
                            if t == 0:
                                pe.wait_ge(w_ready[2 + s], 16)
                            bank_free(u)
                            for k in range(KC):
                                ins = pe.matmul(PS[:, u % 4, :], hT[:, k, t * P:(t + 1) * P], wqkv[s][:, k, :], start=(k == 0), stop=(k == KC - 1))
                            ins.then_inc(proj, 1)
                        if t == 0:
                            pe.wait_ge(s_read, 4)
                            pe.wait_ge(states, 32)
                            for i in range(NC):
                                pe.transpose(PS[:, 4, 8 * i:8 * i + 8], sxg[:, i * P:(i + 1) * P], ident[0:NS, 0:NS])
                                pe.transpose(PS[:, 4, 32 + 8 * i:40 + 8 * i], sxg[:, 512 + i * P:512 + (i + 1) * P], ident[0:NS, 0:NS])
                                pe.transpose(PS[:, 4, 64 + 24 * i:88 + 24 * i], stc[:, i * P:(i + 1) * P], ident[0:24, 0:24])
                                ins = pe.transpose(PS[:, 4, 160 + 8 * i:168 + 8 * i], sth[:, i * P:(i + 1) * P], ident[0:NS, 0:NS])
                            ins.then_inc(s_turned, 1)
                        if t == 2:
                            pe.wait_ge(s_conv, 1)
                            pe.wait_ge(s_kept, 1)
                            for g in range(2):
                                for i in range(NC):
                                    ins = pe.matmul(PS[:, 4, 256 + 32 * g + 8 * i:264 + 32 * g + 8 * i], gate_w[:, g, i, :], xcs[:, i, :], start=True, stop=True)
                            ins.then_inc(s_gates, 1)
                    turn_rotary(6)
                    turn_rotary(7)
                    pe.wait_ge(s_pe, 1)
                    for k in range(KC):
                        for j in range(3):
                            ins = pe.matmul(PS[32 * j:32 * j + NS, 4, :], hTs[:, k, :], wqkv[j][:, k, :], start=(k == 0), stop=(k == KC - 1))
                    ins.then_inc(s_proj, 1)
                    pe.wait_ge(s_pe, 4)
                    pe.wait_ge(scan_done, NC)
                    pe.wait_ge(rope_kept, 8)
                    for i in range(NC):
                        ins = pe.transpose(PS[0:12, 7, i * P:(i + 1) * P], small[:, i, :], ident)
                    ins.then_inc(small_turned, 1)


            nc.all_engine_barrier()
            prod = [rn(1536 + 512 * i, 512) for i in range(2)]
            key_scores = rn(2560, 128).rearrange("p (g b h) -> p g b h", g=N_PAGES, b=NS)
            own = rn(2688, 8, NS)
            s_row = rn(2696, 260, 64)
            picked = rn(2956, 8, 64)
            s_stat = rn(2964, 8, 64)
            own_g = rn(2972, 4, 64)
            pair_sum = rn(2976, 64)
            spread_map = rn(3040, 2048).rearrange("p (g b m r) -> p g b m r", g=N_PAGES, b=NS, m=NG)
            own_map = rn(5088, 128, NS).rearrange("p (m r) -> p m r", m=NG)
            q_rot = rn(5216, 512, NS)
            k_rot = rn(5728, 512, NS)
            r_tmp = rn(6240, 512, NS)
            own_prod = rn(6752, 512, NS)
            so = rn(7264, 128)
            so2 = rn(7392, 128)
            so_st = rn(7520, 4)
            lam_prod = rn(7524, 128)
            lam_s = rn(7652, 4)
            o1 = rn(0, 512)
            o2 = rn(512, 512)
            prob = [R[:, 0:2, :], R[:, 2:4, :]]
            kept_map = [R[:, 4, :], R[:, 5, :]]
            negm = rn(7656, 64)
            lsum = rn(7720, 32)
            linv = rn(7752, 32)
            coef = rn(7784, 16)
            ost = rn(7800, 16)
            UNITS = [(g, t) for g in range(NG) for t in range(NT)]

            with nc.Block() as block:
                @block.sync
                def _(sp_):
                    with sp_.Fori(0, NS * N_PAGES) as i:
                        page = sp_.value_load(pages[0:1, bass.ds(i, 1)], min_val=0, max_val=n_pool - 1)
                        sp_.dma_start(vc_nat[:, bass.ds(i, 1), :], cv[bass.ds(page + layer * n_pool, 1)].rearrange("g p n -> p g n")).then_inc(v_pages, 16)
                    new_k = O["new_k_sample"][bass.ds(layer, 1)].rearrange("l b s h d -> (l b s) (h d)")
                    new_v = O["new_v_sample"][bass.ds(layer, 1)].rearrange("l b s h d -> (l b s) (h d)")
                    sp_.dma_start(new_v, sqkv[2]).then_inc(a_stored, 16)
                    sp_.wait_ge(a_row, 2)
                    sp_.dma_start(new_k, k_rot).then_inc(a_stored, 16)
                    sp_.wait_ge(a_stored, 32)
                    sp_.wait_ge(a_done, 1)
                    sp_.dma_start(w_out, A["w_out"][bass.ds(layer, 1)].rearrange("l (k p) n -> p (l k) n", p=P)).then_inc(w_out_ready, 16)
                    expert = layer * N_EXP
                    sp_.dma_start(expert_in(0), w_in_rows[bass.ds(expert, 1)].rearrange("e p k n -> p (e k) n")).then_inc(e_in[0], 16)
                    sp_.dma_start(expert_out(0), w_out_rows[bass.ds(expert, 1)].rearrange("e p k n -> p (e k) n")).then_inc(e_out[0], 16)

                @block.vector
                def _(dve):
                    settle = chain(dve, dve2)
                    settle(dve.tensor_tensor(lam_prod[:, 0:64], b_("lq1"), b_("lk1"), ALU.mult))
                    settle(dve.tensor_tensor(lam_prod[:, 64:128], b_("lq2"), b_("lk2"), ALU.mult))
                    dve.tensor_reduce(lam_s[:, 0:2], lam_prod.rearrange("p (a n) -> p a n", a=2), AX.X, ALU.add).then_inc(lam_dve, 1)
                    dve.wait_ge(lam_act, 1)
                    settle(dve.tensor_tensor(neglam[:, 1:2], lam_s[:, 3:4], lam_s[:, 2:3], ALU.subtract))
                    settle(dve.tensor_tensor(neglam[:, 0:1], neglam[:, 1:2], b_("lam_init"), ALU.subtract))
                    settle(dve.tensor_scalar(subg[:, :], b_("subln"), b_("one_less"), None, ALU.mult))
                    settle(dve.tensor_tensor(neglam[:, 2:3], neglam[:, 0:1], c("odd"), ALU.mult))
                    settle(dve.tensor_tensor(neglam[:, 3:4], neglam[:, 2:3], c("even"), ALU.add))

                    cos = c("cos_s", NS).unsqueeze(1).to_broadcast([NS, NH, 64])
                    sin = c("sin_s", NS).unsqueeze(1)
                    for src, dst in ((sqkv[0], q_rot), (sqkv[1], k_rot)):
                        a = src.rearrange("p (h n) -> p h n", h=NH)
                        d = dst.rearrange("p (h n) -> p h n", h=NH)
                        r = r_tmp.rearrange("p (h n) -> p h n", h=NH)
                        settle(dve.tensor_tensor(d, a, cos, ALU.mult))
                        settle(dve.tensor_tensor(r[:, :, 0:32], a[:, :, 32:64], sin[:, :, 0:32].to_broadcast([NS, NH, 32]), ALU.mult))
                        settle(dve.tensor_tensor(r[:, :, 32:64], a[:, :, 0:32], sin[:, :, 32:64].to_broadcast([NS, NH, 32]), ALU.mult))
                        dve.tensor_tensor(d, d, r, ALU.add).then_inc(a_row, 1)
                    dve.wait_ge(a_row, 2)
                    settle(dve.tensor_tensor(own_prod, q_rot, k_rot, ALU.mult))
                    dve.tensor_reduce(own, own_prod.rearrange("p (h n) -> p h n", h=NH), AX.X, ALU.add).then_inc(a_s, 1)
                    dve.wait_ge(k_pages, 16 * NS * N_PAGES)
                    for b in range(NS):
                        dve.wait_ge(a_bc, b + 1)
                        for g in range(N_PAGES):
                            settle(dve.tensor_tensor(prod[g], kc_nat[:, b * N_PAGES + g, :], PS[:, b % 2, :], ALU.mult))
                            ins = dve.tensor_reduce(key_scores[:, g, b, :], prod[g].rearrange("p (h n) -> p h n", h=NH), AX.X, ALU.add)
                            ins.then_inc(a_prod, 1)
                    dve.wait_ge(a_pe, 1)
                    settle(dve.tensor_copy(s_row[:, 0:PAST], PS[0:64, 2, 0:PAST]))
                    settle(dve.tensor_tensor(picked, PS[0:64, 3, 0:8], c("mask_h", 64), ALU.mult))
                    settle(dve.tensor_reduce(s_row[:, PAST:PAST + 1], picked, AX.X, ALU.add))
                    settle(dve.tensor_reduce(s_stat[:, 0:1], s_row[:, 0:PAST + 1], AX.X, ALU.max, negate=True))
                    dve.tensor_scalar(s_stat[:, 1:2], s_stat[:, 0:1], SCALE, None, ALU.mult).then_inc(a_dve, 1)
                    dve.wait_ge(a_act, 1)
                    settle(dve.reciprocal(s_stat[:, 3:4], s_stat[:, 2:3]))
                    settle(dve.tensor_tensor(s_stat[:, 4:5], s_stat[:, 3:4], neglam[0:64, 3:4], ALU.mult))
                    settle(dve.tensor_scalar(s_row[:, 0:PAST + 1], s_row[:, 0:PAST + 1], s_stat[:, 4:5], None, ALU.mult))
                    dve.tensor_scalar(own_g, c("mask_g", 64), s_row[:, PAST:PAST + 1], None, ALU.mult).then_inc(a_dve, 1)
                    dve.wait_ge(a_pe, 2)
                    settle(dve.tensor_reduce(pair_sum, PS[:, 2, 0:128].rearrange("p (n two) -> p n two", two=2), AX.X, ALU.add))
                    maps = pair_sum.rearrange("p (g b m) -> p g b m", g=N_PAGES, b=NS)
                    delta = c("delta").rearrange("p (b r) -> p b r", b=NS)
                    for g in range(N_PAGES):
                        dve.tensor_tensor(spread_map[:, g], maps[:, g].unsqueeze(3).to_broadcast([P, NS, NG, 32]),
                                          delta.unsqueeze(2).to_broadcast([P, NS, NG, 32]), ALU.mult).then_inc(a_dve, 1)
                    dve.tensor_tensor(own_map, PS[0:NS, 3, 16:20].unsqueeze(2).to_broadcast([NS, NG, 32]),
                                      c("ident", NS)[:, 0:32].unsqueeze(1).to_broadcast([NS, NG, 32]), ALU.mult).then_inc(a_dve, 1)
                    dve.wait_ge(a_pe, 3)
                    settle(dve.tensor_copy(so, PS[:, 4, 0:128]))
                    settle(dve.tensor_tensor(so2, so, so, ALU.mult))
                    settle(dve.tensor_reduce(so_st[:, 0:1], so2, AX.X, ALU.add))
                    dve.tensor_scalar(so_st[:, 1:2], so_st[:, 0:1], 1.0 / 128, SUB_EPS, ALU.mult, ALU.add).then_inc(a_dve, 1)
                    dve.wait_ge(a_pool, 1)
                    dve.scalar_tensor_tensor(so2, so, so_st[:, 2:3], subg[:, :], ALU.mult, ALU.mult).then_inc(a_dve, 1)
                    dve.wait_ge(a_pe, 4)
                    dve.tensor_copy(yTs[:, 4:8, :], PS[:, 3, 128:256].rearrange("p (m r) -> p m r", m=NG)[:, :, 0:NS]).then_inc(a_done, 1)

                    def best(u):
                        g, t = UNITS[u]
                        b = 2 * (u % 2)
                        dve.wait_ge(scores, u + 1)
                        settle(dve.tensor_reduce(negm[:, 4 * (u % 16):4 * (u % 16) + 2], PS[:, b:b + 2, 0:(t + 1) * P], AX.X, ALU.max, negate=True))
                        dve.tensor_scalar(negm[:, 4 * (u % 16) + 2:4 * (u % 16) + 4], negm[:, 4 * (u % 16):4 * (u % 16) + 2], SCALE, None, ALU.mult).then_inc(negmax, 1)

                    def difference(u):
                        g, t = UNITS[u]
                        n = (t + 1) * P
                        dve.wait_ge(exps, u + 1)
                        settle(dve.reciprocal(linv[:, 2 * u:2 * u + 2], lsum[:, 2 * u:2 * u + 2]))
                        settle(dve.scalar_tensor_tensor(coef[:, u:u + 1], lsum[:, 2 * u:2 * u + 1], linv[:, 2 * u + 1:2 * u + 2], neglam[:, 0:1], ALU.mult, ALU.mult))
                        dve.scalar_tensor_tensor(prob[u % 2][:, 0, 0:n], prob[u % 2][:, 1, 0:n], coef[:, u:u + 1], prob[u % 2][:, 0, 0:n], ALU.mult, ALU.add).then_inc(amap, 1)

                    def norm(g):
                        inv = linv.rearrange("p (g t m) -> p g t m", g=NG, t=NT)[:, g, :, 0]
                        o1v = o1.rearrange("p (t n) -> p t n", t=NT)
                        o2v = o2.rearrange("p (t n) -> p t n", t=NT)
                        dve.wait_ge(av, NT * (g + 1))
                        if g >= 1:
                            dve.wait_ge(o_turned, g)
                        dve.tensor_tensor(o1v, PS[:, 4, :].rearrange("p (t n) -> p t n", t=NT), inv.unsqueeze(2).to_broadcast([P, NT, P]), ALU.mult).then_inc(o_read, 1)
                        dve.wait_ge(o_read, g + 1)
                        settle(dve.tensor_tensor(o2, o1, o1, ALU.mult))
                        settle(dve.tensor_reduce(ost[:, 0:4], o2v, AX.X, ALU.add))
                        dve.tensor_scalar(ost[:, 4:8], ost[:, 0:4], 1.0 / 128, SUB_EPS, ALU.mult, ALU.add).then_inc(o_var, 1)
                        dve.wait_ge(o_rstd, g + 1)
                        settle(dve.tensor_tensor(o2v, o1v, ost[:, 8:12].unsqueeze(2).to_broadcast([P, NT, P]), ALU.mult))
                        dve.tensor_tensor(o1v, o2v, subg[:, :].unsqueeze(1).to_broadcast([P, NT, P]), ALU.mult).then_inc(o_norm, 1)

                    dve.wait_ge(a_done, 1)
                    n_u = len(UNITS)
                    for i in range(n_u + 3):
                        if i < n_u:
                            best(i)
                        if 1 <= i <= n_u:
                            difference(i - 1)
                        if i >= 6 and (i - 6) % 4 == 0:
                            norm((i - 6) // 4)

                @block.scalar
                def _(act):
                    act.wait_ge(lam_dve, 1)
                    act.activation(lam_s[:, 2:4], lam_s[:, 0:2], ACT.Exp).then_inc(lam_act, 1)
                    act.wait_ge(a_dve, 1)
                    act.activation(s_row[:, 0:PAST + 1], s_row[:, 0:PAST + 1], ACT.Exp, scale=SCALE, bias=s_stat[:, 1:2], accum_out=s_stat[:, 2:3]).then_inc(a_act, 1)

                    def exp_rows(u):
                        g, t = UNITS[u]
                        n = (t + 1) * P
                        act.wait_ge(negmax, u + 1)
                        if u >= 2:
                            act.wait_ge(map_turned, u - 1)
                        for m in range(2):
                            ins = act.activation(prob[u % 2][:, m, 0:n], PS[:, 2 * (u % 2) + m, 0:n], ACT.Exp, scale=SCALE,
                                                 bias=negm[:, 4 * (u % 16) + 2 + m:4 * (u % 16) + 3 + m], accum_out=lsum[:, 2 * u + m:2 * u + m + 1])
                        ins.then_inc(exps, 1)

                    def keep_map(u):
                        g, t = UNITS[u]
                        n = (t + 1) * P
                        act.wait_ge(map_turned, u + 1)
                        if u >= 2:
                            act.wait_ge(av, u - 1)
                        act.activation(kept_map[u % 2][:, 0:n], PS[:, 5 + u % 2, 0:n], ACT.Copy).then_inc(map_kept, 1)

                    def keep_o(g):
                        act.wait_ge(o_turned, g + 1)
                        act.activation(yT[:, 4 + g, :], PS[:, 7, :], ACT.Copy).then_inc(o_kept, 1)

                    n_u = len(UNITS)
                    for i in range(n_u + 4):
                        if i < n_u:
                            exp_rows(i)
                        if 1 <= i <= n_u:
                            keep_map(i - 1)
                        if i >= 7 and (i - 7) % 4 == 0:
                            keep_o((i - 7) // 4)

                @block.gpsimd
                def _(pool):
                    pool.wait_ge(a_dve, 6)
                    pool.tensor_tensor(so_st[:, 2:3], so_st[:, 1:2], c("neghalf")[:, 0:1], ALU.pow).then_inc(a_pool, 1)
                    for g in range(NG):
                        pool.wait_ge(o_var, g + 1)
                        pool.tensor_tensor(ost[:, 8:12], ost[:, 4:8], c("neghalf")[:, 0:4], ALU.pow).then_inc(o_rstd, 1)

                @block.tensor
                def _(pe):
                    pe.wait_ge(a_row, 1)
                    for b in range(NS):
                        if b >= 2:
                            pe.wait_ge(a_prod, 2 * b - 2)
                        pe.matmul(PS[:, b % 2, :], ident[0:NS, b:b + 1].to_broadcast([NS, P]), q_rot, start=True, stop=True).then_inc(a_bc, 1)
                    pe.wait_ge(a_s, 1)
                    pe.matmul(PS[0:64, 3, 0:8], c("sel_b", NS), own, start=True, stop=True)
                    pe.wait_ge(a_prod, 16)
                    for g in range(N_PAGES):
                        ins = pe.transpose(PS[0:64, 2, g * P:(g + 1) * P], key_scores[:, g].rearrange("p b h -> p (b h)"), ident)
                    ins.then_inc(a_pe, 1)
                    pe.wait_ge(a_dve, 2)
                    pe.matmul(PS[0:NS, 3, 16:20], c("sel_t", 64), own_g, start=True, stop=True)
                    for g in range(N_PAGES):
                        ins = pe.transpose(PS[:, 2, g * 64:(g + 1) * 64], s_row[:, g * P:(g + 1) * P], ident[0:64, 0:64])
                    ins.then_inc(a_pe, 1)
                    pe.wait_ge(a_dve, 5)
                    pe.wait_ge(v_pages, 16 * NS * N_PAGES)
                    for b in range(NS):
                        for g in range(N_PAGES):
                            for m in range(NG):
                                pe.matmul(PS[32 * m:32 * m + 32, 4, 0:P], spread_map[:, g, b, m, :], vc_nat[:, b * N_PAGES + g, m * P:(m + 1) * P],
                                          start=(b == 0 and g == 0), stop=False)
                    for m in range(NG):
                        ins = pe.matmul(PS[32 * m:32 * m + 32, 4, 0:P], own_map[:, m, :], sqkv[2][:, m * P:(m + 1) * P], start=False, stop=True)
                    ins.then_inc(a_pe, 1)
                    pe.wait_ge(a_dve, 7)
                    pe.transpose(PS[:, 3, 128:256], so2, ident).then_inc(a_pe, 1)

                    def score(u):
                        g, t = UNITS[u]
                        b = 2 * (u % 2)
                        if u >= 2:
                            pe.wait_ge(exps, u - 1)
                        for m in range(2):
                            pe.matmul(PS[:, b + m, 0:(t + 1) * P], qT[64 * m:64 * m + 64, g, t * P:(t + 1) * P], kT[64 * m:64 * m + 64, g, 0:(t + 1) * P],
                                      start=True, stop=False)
                        for m in range(2):
                            ins = pe.matmul(PS[:, b + m, t * P:(t + 1) * P], ident_b[:, :], mask_b[:, :], start=False, stop=True)
                        ins.then_inc(scores, 1)

                    def turn_map(u):
                        g, t = UNITS[u]
                        pe.wait_ge(amap, u + 1)
                        if u >= 2:
                            pe.wait_ge(map_kept, u - 1)
                        for j in range(t + 1):
                            ins = pe.transpose(PS[:, 5 + u % 2, j * P:(j + 1) * P], prob[u % 2][:, 0, j * P:(j + 1) * P], ident)
                        ins.then_inc(map_turned, 1)

                    def values(u):
                        g, t = UNITS[u]
                        pe.wait_ge(map_kept, u + 1)
                        if t == 0 and g >= 1:
                            pe.wait_ge(o_read, g)
                        for j in range(t + 1):
                            ins = pe.matmul(PS[:, 4, t * P:(t + 1) * P], kept_map[u % 2][:, j * P:(j + 1) * P], v_nat[:, j, g * P:(g + 1) * P],
                                            start=(j == 0), stop=(j == t))
                        ins.then_inc(av, 1)

                    def turn_o(g):
                        pe.wait_ge(o_norm, g + 1)
                        if g >= 1:
                            pe.wait_ge(o_kept, g)
                        for t in range(NT):
                            ins = pe.transpose(PS[:, 7, t * P:(t + 1) * P], o1[:, t * P:(t + 1) * P], ident)
                        ins.then_inc(o_turned, 1)

                    pe.wait_ge(a_done, 1)
                    n_u = len(UNITS)
                    for i in range(n_u + 4):
                        if i < n_u:
                            score(i)
                        if 1 <= i <= n_u:
                            turn_map(i - 1)
                        if 2 <= i <= n_u + 1:
                            values(i - 2)
                        if i >= 7 and (i - 7) % 4 == 0:
                            turn_o((i - 7) // 4)

            nc.all_engine_barrier()
            Rf = R[:, :, :].rearrange("p a n -> p (a n)")
            qf = qT[:, :, :].rearrange("p a n -> p (a n)")
            xn2 = [v_nat[:, 2 * i:2 * i + 2, :].rearrange("p a n -> p (a n)") for i in range(2)]
            h2T = [qT[:, 2 * i:2 * i + 2, :].rearrange("p a n -> p (a n)").rearrange("p (k n) -> p k n", k=KC) for i in range(2)]
            free_at = [0]

            def rr(n, rows=P):
                a = free_at[0]
                free_at[0] += n
                assert free_at[0] <= 2784
                return Rf[0:rows, a:a + n]

            lg = rr(NTT * 36).rearrange("p (t n) -> p t n", t=NTT)
            lg_g, lg_e = lg[:, :, 0:N_GRP], lg[:, :, N_GRP:36]
            emask = rr(160).rearrange("p (t g e) -> p t g e", t=NTT, g=N_GRP)
            E = rr(320).rearrange("p (k t e) -> p k t e", k=2, t=NTT)
            EW = rr(320).rearrange("p (k t e) -> p k t e", k=2, t=NTT)
            M_b = rr(80).bitcast(BF16).rearrange("p (t e) -> p t e", t=NTT)
            g_diff, g_exp, g_cand, g_hot = (rr(20).rearrange("p (t g) -> p t g", t=NTT) for _ in range(4))
            sel, sel2, cand = (rr(40).rearrange("p (t e) -> p t e", t=NTT) for _ in range(3))
            pick = rr(80).rearrange("p (k t e) -> p k t e", k=2, t=NTT)
            m_g, m_c, p_g, e_sum, m_1, m_2, e_d, e_2, rden = (rr(NTT) for _ in range(9))
            cnt, n_ovf, incl, base = (rr(N_EXP) for _ in range(4))
            rank, e_id, extra, base_k, is_ovf, blk, row_in = (rr(10) for _ in range(7))
            ovf_f = rr(MAX_OVF + 1)
            tok_hot = rr(2 * NTT * NBLK).rearrange("p (k t b) -> p k t b", k=2, t=NTT)
            row_hot = qf[:, 0:1280].rearrange("p (k n) -> p k n", k=10)
            steps_hot = qf[:, 1280:1792]

            def over(a, n):
                return a.unsqueeze(2).to_broadcast([a.shape[0], a.shape[1], n])

            with nc.Block() as block:
                @block.sync
                def _(sp_):
                    sp_.dma_start(route_w, A["route_w"][bass.ds(layer, 1)].rearrange("l p k n -> p (l k) n")).then_inc(w_route, 16)
                    for t in range(NTT):
                        n = P if t < NT else NS
                        sp_.wait_ge(xn2_ready, t + 1)
                        sp_.dma_start(xn_dram[t * P:t * P + n, :], xn2[t % 2][0:n, :]).then_inc(xn2_stored[t % 2], 16)
                        if t == 2:
                            sp_.wait_ge(op_done, 2 * NT + 1)
                            for i in (1, 2):
                                expert = layer * N_EXP + i
                                sp_.dma_start(expert_in(i), w_in_rows[bass.ds(expert, 1)].rearrange("e p k n -> p (e k) n")).then_inc(e_in[i], 16)
                                sp_.dma_start(expert_out(i), w_out_rows[bass.ds(expert, 1)].rearrange("e p k n -> p (e k) n")).then_inc(e_out[i], 16)
                    sp_.wait_ge(xn2_stored[0], 48)
                    sp_.wait_ge(xn2_stored[1], 32)

                @block.scalar
                def _(act):
                    def square(t):
                        n = P if t < NT else NS
                        act.wait_ge(x_new, 2 * t + 2 if t < NT else 2 * NT + 1)
                        if t >= 2:
                            act.wait_ge(turned2, 2 * t - 2)
                            act.wait_ge(xn2_stored[t % 2], 16 * (t // 2))
                        act.activation(xn2[t % 2][0:n, :], x[0:n, t, :], ACT.Square, accum_out=st[0:n, 0, t:t + 1]).then_inc(sumsq2, 1)

                    def scale(t):
                        n = P if t < NT else NS
                        act.wait_ge(rstd2, t + 1)
                        act.wait_ge(sumsq2, t + 1)
                        act.activation(xn2[t % 2][0:n, :], x[0:n, t, :], ACT.Copy, scale=st[0:n, 2, t:t + 1]).then_inc(xn2_ready, 1)

                    for i in range(NTT + 1):
                        if i >= 1:
                            scale(i - 1)
                        if i < NTT:
                            square(i)
                    act.wait_ge(r_act_in, 1)
                    act.activation(g_exp, g_diff, ACT.Exp).then_inc(r_act, 1)
                    act.wait_ge(r_act_in, 2)
                    act.activation(e_2, e_d, ACT.Exp).then_inc(r_act, 1)

                @block.gpsimd
                def _(pool):
                    for t in range(NTT):
                        n = P if t < NT else NS
                        pool.wait_ge(mean2, t + 1)
                        pool.tensor_tensor(st[0:n, 2, t:t + 1], st[0:n, 1, t:t + 1], c("neghalf", n)[:, 0:1], ALU.pow).then_inc(rstd2, 1)

                @block.tensor
                def _(pe):
                    def out_product(t):
                        if t == 0:
                            pe.wait_ge(w_out_ready, 16)
                        if t == NT:
                            for k in range(KC):
                                for j in range(4):
                                    ins = pe.matmul(PS[32 * j:32 * j + NS, 4, 0:256], yTs[:, k, :], w_out[:, k, 256 * j:256 * j + 256], start=(k == 0), stop=(k == KC - 1))
                            ins.then_inc(op_done, 1)
                            return
                        for h in range(2):
                            u = 2 * t + h
                            if u >= 4:
                                pe.wait_ge(x_new, u - 3)
                            for k in range(KC):
                                ins = pe.matmul(PS[:, u % 4, :], yT[:, k, t * P:(t + 1) * P], w_out[:, k, 512 * h:512 * h + 512], start=(k == 0), stop=(k == KC - 1))
                            ins.then_inc(op_done, 1)

                    def turn(t):
                        n = P if t < NT else NS
                        pe.wait_ge(xn2_ready, t + 1)
                        for h in range(2):
                            if t >= 1:
                                pe.wait_ge(h2_ready, 2 * t - 1 + h)
                            for j in range(4):
                                k = 4 * h + j
                                ins = pe.transpose(PS[:, 5 + h, j * P:j * P + n], xn2[t % 2][0:n, k * P:(k + 1) * P], ident[0:n, 0:n])
                            ins.then_inc(turned2, 1)

                    def route(t):
                        n = P if t < NT else NS
                        if t == 0:
                            pe.wait_ge(w_route, 16)
                        pe.wait_ge(h2_ready, 2 * t + 2)
                        for k in range(KC):
                            ins = pe.matmul(PS[0:n, 7, 36 * t:36 * t + 36], h2T[t % 2][:, k, 0:n], route_w[:, k, :], start=(k == 0), stop=(k == KC - 1))
                        ins.then_inc(logits, 1)

                    for i in range(NTT + 3):
                        if i < NTT:
                            out_product(i)
                        if 2 <= i <= NTT + 1:
                            turn(i - 2)
                        if i >= 3:
                            route(i - 3)
                    pe.wait_ge(hot, 1)
                    for t in range(NTT):
                        n = P if t < NT else NS
                        for s in range(t):
                            pe.matmul(PS[0:n, 0, 32 * t:32 * t + 32], ones_b[:, 0:n], M_b[:, s, :], start=(s == 0), stop=False)
                        pe.matmul(PS[0:n, 0, 32 * t:32 * t + 32], tri_b[0:n, 0:n], M_b[0:n, t, :], start=(t == 0), stop=True)
                    for t in range(NTT):
                        n = P if t < NT else NS
                        ins = pe.matmul(PS[:, 0, 160:192], ones_b[0:n, :], M_b[0:n, t, :], start=(t == 0), stop=(t == NTT - 1))
                    ins.then_inc(ranks, 1)
                    pe.wait_ge(place, 1)
                    for k in range(2):
                        for t in range(NTT):
                            n = P if t < NT else NS
                            ins = pe.matmul(PS[:, 1, 0:NBLK], row_hot[0:n, k * NTT + t, :], tok_hot[0:n, k, t, :], start=(k == 0 and t == 0), stop=(k == 1 and t == NTT - 1))
                    ins.then_inc(slots_done, 1)

                @block.vector
                def _(dve):
                    settle = chain(dve, dve3)
                    g2 = f("g2")

                    def residual(t):
                        if t == NT:
                            dve.wait_ge(op_done, 2 * NT + 1)
                            for j in range(4):
                                ins = dve.tensor_tensor(x[0:NS, NT, 256 * j:256 * j + 256], PS[32 * j:32 * j + NS, 4, 0:256], x[0:NS, NT, 256 * j:256 * j + 256], ALU.add)
                            ins.then_inc(x_new, 1)
                            return
                        for h in range(2):
                            dve.wait_ge(op_done, 2 * t + h + 1)
                            dve.tensor_tensor(x[:, t, 512 * h:512 * h + 512], PS[:, (2 * t + h) % 4, :], x[:, t, 512 * h:512 * h + 512], ALU.add).then_inc(x_new, 1)

                    def mean(t):
                        n = P if t < NT else NS
                        dve.wait_ge(sumsq2, t + 1)
                        dve.tensor_scalar(st[0:n, 1, t:t + 1], st[0:n, 0, t:t + 1], 1.0 / D, EPS, ALU.mult, ALU.add).then_inc(mean2, 1)

                    def keep(t):
                        n = P if t < NT else NS
                        if t >= 2:
                            dve.wait_ge(logits, t - 1)
                        for h in range(2):
                            dve.wait_ge(turned2, 2 * t + h + 1)
                            dve.tensor_tensor(h2T[t % 2][:, 4 * h:4 * h + 4, 0:n], PS[:, 5 + h, :].rearrange("p (k n) -> p k n", k=4)[:, :, 0:n],
                                              over(g2[:, 4 * h:4 * h + 4], n), ALU.mult).then_inc(h2_ready, 1)

                    for i in range(NTT + 2):
                        if i < NTT:
                            residual(i)
                        if 1 <= i <= NTT:
                            mean(i - 1)
                        if i >= 2:
                            keep(i - 2)

                    settle(dve.memset(lg, 0.0))
                    dve.wait_ge(logits, NTT)
                    br = b_("b_route").unsqueeze(1)
                    settle(dve.tensor_tensor(lg[:, 0:NT, :], PS[:, 7, 0:36 * NT].rearrange("p (t n) -> p t n", t=NT), br.to_broadcast([P, NT, 36]), ALU.add))
                    settle(dve.tensor_tensor(lg[0:NS, NT, :], PS[0:NS, 7, 36 * NT:36 * NTT], b_("b_route", NS), ALU.add))
                    settle(dve.tensor_reduce(m_g, lg_g, AX.X, ALU.max))
                    dve.tensor_tensor(g_diff, lg_g, over(m_g, N_GRP), ALU.subtract).then_inc(r_act_in, 1)
                    dve.wait_ge(r_act_in, 1)
                    first4 = c("first4").unsqueeze(1).to_broadcast([P, NTT, N_GRP])
                    first8 = c("first8").unsqueeze(1).to_broadcast([P, NTT, EPG])
                    settle(dve.scalar_tensor_tensor(g_cand, g_diff, 0.0, first4, ALU.is_ge, ALU.mult))
                    settle(dve.tensor_reduce(m_c, g_cand, AX.X, ALU.max))
                    settle(dve.tensor_tensor(g_hot, g_cand, over(m_c, N_GRP), ALU.is_equal))
                    settle(dve.tensor_tensor(emask, lg_e.rearrange("p t (g e) -> p t g e", g=N_GRP), g_hot.unsqueeze(3).to_broadcast([P, NTT, N_GRP, EPG]), ALU.mult))
                    settle(dve.tensor_reduce(sel, emask.rearrange("p t g e -> p t e g"), AX.X, ALU.add))

                    def first_best(logit, best, hot_out):
                        settle(dve.tensor_reduce(best, logit, AX.X, ALU.max))
                        settle(dve.tensor_tensor(cand, logit, over(best, EPG), ALU.is_ge))
                        settle(dve.tensor_tensor(cand, cand, first8, ALU.mult))
                        settle(dve.tensor_reduce(m_c, cand, AX.X, ALU.max))
                        settle(dve.tensor_tensor(hot_out, cand, over(m_c, EPG), ALU.is_equal))

                    first_best(sel, m_1, pick[:, 0])
                    settle(dve.scalar_tensor_tensor(sel2, pick[:, 0], NEG, sel, ALU.mult, ALU.add))
                    first_best(sel2, m_2, pick[:, 1])
                    dve.tensor_tensor(e_d, m_2, m_1, ALU.subtract).then_inc(r_act_in, 1)
                    for k in range(2):
                        settle(dve.tensor_tensor(E[:, k].rearrange("p t (g e) -> p t g e", g=N_GRP), g_hot.unsqueeze(3).to_broadcast([P, NTT, N_GRP, EPG]),
                                                 pick[:, k].unsqueeze(2).to_broadcast([P, NTT, N_GRP, EPG]), ALU.mult))
                    dve.tensor_tensor(M_b, E[:, 0], E[:, 1], ALU.add).then_inc(hot, 1)
                    dve.wait_ge(r_act, 2)
                    settle(dve.tensor_reduce(e_sum, g_exp, AX.X, ALU.add))
                    settle(dve.reciprocal(p_g, e_sum))
                    settle(dve.tensor_scalar(rden, e_2, 1.0, None, ALU.add))
                    settle(dve.reciprocal(rden, rden))
                    settle(dve.tensor_tensor(gate[:, 0, :], p_g, rden, ALU.mult))
                    settle(dve.tensor_tensor(gate[:, 1, :], gate[:, 0, :], e_2, ALU.mult))

                    Ef = E.rearrange("p k t e -> p (k t) e")
                    EWf = EW.rearrange("p k t e -> p (k t) e")

                    def per_choice(out, row):
                        settle(dve.tensor_tensor(EWf, Ef, row.unsqueeze(1).to_broadcast([P, 10, N_EXP]), ALU.mult))
                        settle(dve.tensor_reduce(out, EWf, AX.X, ALU.add))

                    per_choice(e_id, c("iota_e"))
                    dve.wait_ge(ranks, 1)
                    settle(dve.memset(EW, 0.0))
                    for k in range(2):
                        settle(dve.tensor_tensor(EW[:, k, 0:NT, :], E[:, k, 0:NT, :], PS[:, 0, 0:128].rearrange("p (t e) -> p t e", t=NT), ALU.mult))
                        settle(dve.tensor_tensor(EW[0:NS, k, NT, :], E[0:NS, k, NT, :], PS[0:NS, 0, 128:160], ALU.mult))
                    settle(dve.tensor_reduce(rank, EWf, AX.X, ALU.add))
                    settle(dve.tensor_copy(cnt, PS[:, 0, 160:192]))
                    sh = steps_hot[:, 0:N_EXP * MAX_OVF].rearrange("p (e m) -> p e m", e=N_EXP)
                    settle(dve.tensor_tensor(sh, over(cnt, MAX_OVF), c("cap_steps").unsqueeze(1).to_broadcast([P, N_EXP, MAX_OVF]), ALU.is_gt))
                    settle(dve.tensor_reduce(n_ovf, sh, AX.X, ALU.add))
                    settle(dve.tensor_tensor_scan(incl, c("one").to_broadcast([P, N_EXP]), n_ovf, 0.0, ALU.mult, ALU.add))
                    settle(dve.tensor_tensor(base, incl, n_ovf, ALU.subtract))
                    per_choice(base_k, base)
                    sk = steps_hot[:, 0:10 * MAX_OVF].rearrange("p (k m) -> p k m", k=10)
                    settle(dve.tensor_tensor(sk, over(rank, MAX_OVF), c("cap_steps").unsqueeze(1).to_broadcast([P, 10, MAX_OVF]), ALU.is_ge))
                    settle(dve.tensor_reduce(extra, sk, AX.X, ALU.add))
                    settle(dve.tensor_scalar(is_ovf, extra, 0.0, None, ALU.is_gt))
                    settle(dve.tensor_tensor(base_k, base_k, extra, ALU.add))
                    settle(dve.scalar_tensor_tensor(base_k, base_k, float(N_EXP - 1), e_id, ALU.add, ALU.subtract))
                    settle(dve.tensor_tensor(base_k, base_k, is_ovf, ALU.mult))
                    settle(dve.tensor_tensor(blk, base_k, e_id, ALU.add))
                    settle(dve.scalar_tensor_tensor(row_in, extra, -float(CAP), rank, ALU.mult, ALU.add))
                    settle(dve.scalar_tensor_tensor(slot_i[:, :, :].rearrange("p k t -> p (k t)"), blk, float(CAP), row_in, ALU.mult, ALU.add))
                    so_ = steps_hot[:, 0:N_EXP * MAX_OVF].rearrange("p (j e) -> p j e", j=MAX_OVF)
                    settle(dve.tensor_tensor(so_, incl.unsqueeze(1).to_broadcast([P, MAX_OVF, N_EXP]), over(c("iota_ovf"), N_EXP), ALU.is_le))
                    settle(dve.tensor_reduce(ovf_f[:, 1:MAX_OVF + 1], so_, AX.X, ALU.add))
                    settle(dve.tensor_copy(ovf_f[:, 0:1], incl[:, N_EXP - 1:N_EXP]))
                    settle(dve.tensor_scalar(ovf_i[:, :], ovf_f, float(N_EXP - 1), None, ALU.min))
                    settle(dve.tensor_tensor(row_hot, c("slot_row").unsqueeze(1).to_broadcast([P, 10, P]), over(row_in, P), ALU.is_equal))
                    for k in range(2):
                        bk = blk.rearrange("p (k t) -> p k t", k=2)[:, k, :]
                        settle(dve.tensor_tensor(tok_hot[:, k], c("iota_blk").unsqueeze(1).to_broadcast([P, NTT, NBLK]), over(bk, NBLK), ALU.is_equal))
                        ins = dve.tensor_tensor(tok_hot[:, k], tok_hot[:, k], over(c("tok"), NBLK), ALU.mult)
                        if k == 0:
                            settle(ins)
                    ins.then_inc(place, 1)
                    dve.wait_ge(slots_done, 1)
                    settle(dve.tensor_scalar(idx_i[:, :], PS[:, 1, 0:NBLK], 2.0, c("half"), ALU.mult, ALU.add))

            nc.all_engine_barrier()
            halves = xn_dram.rearrange("t (h n) -> (t h) n", h=2)
            g2hc = f("g2").rearrange("p (h c) -> p h c", h=2).unsqueeze(3).to_broadcast([P, 2, 4, CAP])

            def expert_pass(eng, step):
                for e in range(2):
                    step(e, e)
                with eng.Fori(0, (N_EXP - 2) // 6) as i:
                    for j in range(6):
                        step(i * 6 + (2 + j), 2 + j)

            def at_least(eng, s, value):
                if not isinstance(value, int) or value > 0:
                    eng.wait_ge(s, value)

            def turn_rows(pe, rows):
                for j in range(4):
                    ins = pe.transpose(PS[:, 0, j * P:(j + 1) * P], rows[:, j * P:(j + 1) * P], ident)
                return ins

            def in_product(pe, xt, w, bank):
                for k in range(KC):
                    for j in range(2):
                        cols = w[:, k, :].rearrange("p (u j n) -> p u j n", u=2, j=2)[:, :, j, :]
                        ins = pe.matmul(PS[64 * j:64 * j + 64, bank, :], xt[:, k // 4, k % 4, :], cols, start=(k == 0), stop=(k == KC - 1))
                return ins

            def out_product(pe, ht, w, bank):
                for k in range(4):
                    for j in range(2):
                        ins = pe.matmul(PS[64 * j:64 * j + 64, bank, :], ht[:, k % 2, k // 2, :], w[:, k, 512 * j:512 * j + 512], start=(k == 0), stop=(k == 3))
                return ins

            with nc.Block() as block:
                @block.sync
                def _(sp_):
                    def load(e, r):
                        expert = layer * N_EXP + e
                        sp_.wait_ge(in_done, e - 2)
                        sp_.dma_start(expert_in(r), w_in_rows[bass.ds(expert, 1)].rearrange("e p k n -> p (e k) n")).then_inc(e_in[r], 16)
                        sp_.wait_ge(out_done, e - 2)
                        sp_.dma_start(expert_out(r), w_out_rows[bass.ds(expert, 1)].rearrange("e p k n -> p (e k) n")).then_inc(e_out[r], 16)

                    with sp_.Fori(0, (N_EXP - NBUF) // NBUF) as i:
                        for r in range(NBUF):
                            load(i * NBUF + (NBUF + r), r)
                    for e in range(NBUF + (N_EXP - NBUF) // NBUF * NBUF, N_EXP):
                        load(e, e % NBUF)

                @block.gpsimd
                def _(pool):
                    for e in range(N_EXP):
                        if e >= NBUF:
                            pool.wait_ge(xe_turned, e - NBUF + 1)
                        pool.indirect_dma_start(xe[e % NBUF], None, halves, bass.IndirectOffsetOnAxis(idx_i[:, e:e + 1], 0)).then_inc(gathered[e % NBUF], 16)

                @block.vector
                def _(dve):
                    def step(e, s):
                        p2 = s % 2
                        dve.wait_ge(xe_turned, e + 1)
                        at_least(dve, in_done, e - 1)
                        dve.tensor_tensor(xTe[p2], PS[:, 0, :].rearrange("p (c h t) -> p h c t", c=4, h=2), g2hc, ALU.mult).then_inc(xTe_ready, 1)
                        dve.wait_ge(silu_done, e + 1)
                        at_least(dve, h_turned, e - 1)
                        dve.tensor_tensor(hh[p2], hs[p2], PS[:, 2 + p2, 256:512], ALU.mult).then_inc(h_ready, 1)

                    expert_pass(dve, step)

                @block.scalar
                def _(act):
                    def step(e, s):
                        p2 = s % 2
                        act.wait_ge(in_done, e + 1)
                        at_least(act, h_ready, e - 1)
                        act.activation(hs[p2], PS[:, 2 + p2, 0:256], ACT.Silu).then_inc(silu_done, 1)
                        act.wait_ge(h_turned, e + 1)
                        at_least(act, out_done, e - 1)
                        act.activation(hTe[p2], PS[:, 4, 0:256].rearrange("p (j h t) -> p j h t", j=2, h=2), ACT.Copy).then_inc(hT_kept, 1)
                        act.wait_ge(out_done, e + 1)
                        at_least(act, y_stored[p2], (e - p2) * 16)
                        act.activation(ye[p2], PS[:, 5 + p2, :], ACT.Copy).then_inc(y_kept, 1)
                        act.wait_ge(y_kept, e + 1)
                        for j in range(2):
                            act.dma_start(y_blocks[bass.ds(e, 1), :, 512 * j:512 * j + 512].rearrange("e r n -> r (e n)"), ye[p2][64 * j:64 * j + 64, :]).then_inc(y_stored[p2], 16)

                    expert_pass(act, step)
                    for s in y_stored:
                        act.wait_ge(s, 16 * N_EXP)

                @block.tensor
                def _(pe):
                    def turn(e, s):
                        pe.wait_ge(gathered[s % 3], (e // 3 + 1) * 16 if isinstance(e, int) else e_third(e, s))
                        at_least(pe, xTe_ready, e)
                        turn_rows(pe, xe[s % 3]).then_inc(xe_turned, 1)

                    def e_third(e, s):
                        return ((e - s % 3) * 16) // 3 + 16

                    def step(e, s, last=False):
                        p2, b = s % 2, s % 3
                        uses = (e // 3 + 1) * 16 if isinstance(e, int) else e_third(e, s)
                        pe.wait_ge(e_in[b], uses)
                        pe.wait_ge(xTe_ready, e + 1)
                        at_least(pe, h_ready, e - 1)
                        in_product(pe, xTe[p2], expert_in(b), 2 + p2).then_inc(in_done, 1)
                        if not last:
                            turn(e + 1, s + 1)
                        pe.wait_ge(h_ready, e + 1)
                        at_least(pe, hT_kept, e)
                        for j in range(2):
                            ins = pe.transpose(PS[:, 4, j * P:(j + 1) * P], hh[p2][:, j * P:(j + 1) * P], ident)
                        ins.then_inc(h_turned, 1)
                        pe.wait_ge(e_out[b], uses)
                        pe.wait_ge(hT_kept, e + 1)
                        at_least(pe, y_kept, e - 1)
                        out_product(pe, hTe[p2], expert_out(b), 5 + p2).then_inc(out_done, 1)

                    turn(0, 0)
                    step(0, 0)
                    with pe.Fori(0, (N_EXP - 2) // 6) as i:
                        for j in range(6):
                            step(i * 6 + (1 + j), 1 + j)
                    step(N_EXP - 1, N_EXP - 1, last=True)

            nc.all_engine_barrier()
            n_more = nc.values_load(ovf_i[0:1, 0:1], min_val=0, max_val=MAX_OVF)
            with nc.If(n_more > 0):
                with nc.Fori(0, n_more) as more:
                    with nc.Block() as block:
                        @block.sync
                        def _(sp_):
                            which = sp_.value_load(ovf_i[0:1, bass.ds(more + 1, 1)], min_val=0, max_val=N_EXP - 1)
                            expert = which + layer * N_EXP
                            sp_.dma_start(expert_in(0), w_in_rows[bass.ds(expert, 1)].rearrange("e p k n -> p (e k) n")).then_inc(v_w, 16)
                            sp_.dma_start(expert_out(0), w_out_rows[bass.ds(expert, 1)].rearrange("e p k n -> p (e k) n")).then_inc(v_w, 16)
                            sp_.wait_ge(v_y, 1)
                            for j in range(2):
                                sp_.dma_start(y_blocks[bass.ds(more + N_EXP, 1), :, 512 * j:512 * j + 512].rearrange("e r n -> r (e n)"), ye[0][64 * j:64 * j + 64, :]).then_inc(v_st, 16)
                            sp_.wait_ge(v_st, 32)

                        @block.gpsimd
                        def _(pool):
                            pool.tensor_copy(cur[:, 0:1], idx_i[:, bass.ds(more + N_EXP, 1)]).then_inc(v_g, 16)
                            pool.wait_ge(v_g, 16)
                            pool.indirect_dma_start(xe[0], None, halves, bass.IndirectOffsetOnAxis(cur[:, 0:1], 0)).then_inc(v_t, 16)

                        @block.tensor
                        def _(pe):
                            pe.wait_ge(v_t, 16)
                            turn_rows(pe, xe[0]).then_inc(v_x, 1)
                            pe.wait_ge(v_x, 2)
                            pe.wait_ge(v_w, 32)
                            in_product(pe, xTe[0], expert_in(0), 2).then_inc(v_i, 1)
                            pe.wait_ge(v_h, 1)
                            for j in range(2):
                                ins = pe.transpose(PS[:, 4, j * P:(j + 1) * P], hh[0][:, j * P:(j + 1) * P], ident)
                            ins.then_inc(v_ht, 1)
                            pe.wait_ge(v_hk, 1)
                            out_product(pe, hTe[0], expert_out(0), 5).then_inc(v_o, 1)

                        @block.vector
                        def _(dve):
                            dve.wait_ge(v_x, 1)
                            dve.tensor_tensor(xTe[0], PS[:, 0, :].rearrange("p (c h t) -> p h c t", c=4, h=2), g2hc, ALU.mult).then_inc(v_x, 1)
                            dve.wait_ge(v_s, 1)
                            dve.tensor_tensor(hh[0], hs[0], PS[:, 2, 256:512], ALU.mult).then_inc(v_h, 1)

                        @block.scalar
                        def _(act):
                            act.wait_ge(v_i, 1)
                            act.activation(hs[0], PS[:, 2, 0:256], ACT.Silu).then_inc(v_s, 1)
                            act.wait_ge(v_ht, 1)
                            act.activation(hTe[0], PS[:, 4, 0:256].rearrange("p (j h t) -> p j h t", j=2, h=2), ACT.Copy).then_inc(v_hk, 1)
                            act.wait_ge(v_o, 1)
                            act.activation(ye[0], PS[:, 5, :], ACT.Copy).then_inc(v_y, 1)

                    barrier_and_clear(ovf_sems)

            nc.all_engine_barrier()
            y_rows = [W[:, 1024 * i:1024 * i + 1024] for i in range(4)]
            picks = [(t, k) for t in range(NTT) for k in range(2)]
            with nc.Block() as block:
                @block.gpsimd
                def _(pool):
                    pool.wait_ge(s_zero, 64)
                    for i, (t, k) in enumerate(picks):
                        n = P if t < NT else NS
                        if i >= 4:
                            pool.wait_ge(added, i - 3)
                        pool.indirect_dma_start(y_rows[i % 4][0:n, :], None, y_dram, bass.IndirectOffsetOnAxis(slot_i[0:n, k, t:t + 1], 0)).then_inc(got[i % 4], 16)

                @block.vector
                def _(dve):
                    for i, (t, k) in enumerate(picks):
                        n = P if t < NT else NS
                        dve.wait_ge(got[i % 4], 16 * (i // 4 + 1))
                        dve.scalar_tensor_tensor(x[0:n, t, :], y_rows[i % 4][0:n, :], gate[0:n, k, t:t + 1], x[0:n, t, :], ALU.mult, ALU.add).then_inc(added, 1)
                        dve.wait_ge(added, i + 1)

            barrier_and_clear(all_sems)

        f_gain, f_sum, f_mean, f_rstd, f_out, f_stored = (once("final_" + n) for n in ("gain", "sum", "mean", "rstd", "rows", "stored"))
        gain = W[:, 0:1024]
        squares = W[:, 1024:2048]
        rows_out = W[:, 2048:2048 + NTT * D].rearrange("p (t n) -> p t n", t=NTT)
        with nc.Block() as block:
            @block.sync
            def _(sp_):
                sp_.dma_start(gain, A["ln_f"]).then_inc(f_gain, 16)
                yp = O["y_prompt"].rearrange("b (t p) n -> (b t) p n", p=P)
                ys = O["y_sample"].rearrange("b s n -> (b s) n")
                for t in range(NTT):
                    sp_.wait_ge(f_out, t + 1)
                    if t < NT:
                        sp_.dma_start(yp[t], rows_out[:, t, :]).then_inc(f_stored, 16)
                    else:
                        sp_.dma_start(ys, rows_out[0:NS, t, :]).then_inc(f_stored, 16)
                sp_.wait_ge(f_stored, 16 * NTT)

            @block.scalar
            def _(act):
                for t in range(NTT):
                    n = P if t < NT else NS
                    if t >= 1:
                        act.wait_ge(f_sum, t)
                    act.activation(squares[0:n, :], x[0:n, t, :], ACT.Square, accum_out=st[0:n, 0, t:t + 1]).then_inc(f_sum, 1)

            @block.gpsimd
            def _(pool):
                for t in range(NTT):
                    n = P if t < NT else NS
                    pool.wait_ge(f_mean, t + 1)
                    pool.tensor_tensor(st[0:n, 2, t:t + 1], st[0:n, 1, t:t + 1], c("neghalf", n)[:, 0:1], ALU.pow).then_inc(f_rstd, 1)

            @block.vector
            def _(dve):
                def mean(t):
                    n = P if t < NT else NS
                    dve.wait_ge(f_sum, t + 1)
                    dve.tensor_scalar(st[0:n, 1, t:t + 1], st[0:n, 0, t:t + 1], 1.0 / D, EPS, ALU.mult, ALU.add).then_inc(f_mean, 1)

                dve.wait_ge(f_gain, 16)
                mean(0)
                for t in range(NTT):
                    n = P if t < NT else NS
                    if t + 1 < NTT:
                        mean(t + 1)
                    dve.wait_ge(f_rstd, t + 1)
                    dve.scalar_tensor_tensor(rows_out[0:n, t, :], x[0:n, t, :], st[0:n, 2, t:t + 1], gain[0:n, :], ALU.mult, ALU.mult).then_inc(f_out, 1)


def constants():
    def rope(pos):
        half = HEAD // 2
        inv = (10000.0 ** (-np.arange(half, dtype=np.float32) / half)).astype(np.float32)
        ang = pos.astype(np.float32)[:, None] * inv[None, :]
        cos, sin = np.cos(ang), np.sin(ang)
        return np.concatenate([cos, cos], 1), np.concatenate([-sin, sin], 1)

    t = {}
    cos, sin = rope(np.arange(SEQ))
    t["cos"] = cos.reshape(NT, P, 64).transpose(1, 0, 2).reshape(P, -1)
    t["sin"] = sin.reshape(NT, P, 64).transpose(1, 0, 2).reshape(P, -1)
    t["cos_s"], t["sin_s"] = rope(np.full(P, PAST))
    row = np.arange(P)[:, None]
    t["ident"] = np.eye(P)
    t["mask"] = np.where(np.arange(P)[None, :] > row, NEG, 0.0)
    t["tri"] = (row < np.arange(P)[None, :]) * 1.0
    t["iota_e"] = np.arange(N_EXP)[None, :]
    t["iota_blk"] = np.arange(NBLK)[None, :]
    t["cap_steps"] = (np.arange(MAX_OVF)[None, :] + 1.0) * CAP
    t["iota_ovf"] = np.arange(MAX_OVF)[None, :]
    t["slot_row"] = np.arange(P)[None, :] % CAP
    t["tok"] = row + P * np.arange(NTT)[None, :]
    t["delta"] = (np.arange(NS)[:, None] == np.arange(32)[None, :]).reshape(1, -1) * 1.0
    t["first4"] = N_GRP - np.arange(N_GRP)[None, :]
    t["first8"] = EPG - np.arange(EPG)[None, :]
    t["half"] = (row >= CAP) * 1.0
    t["neghalf"] = np.full((1, 8), -0.5)
    t["sel_b"] = (row == np.arange(64)[None, :] // NH) * 1.0
    t["sel_t"] = (row // NH == np.arange(NS)[None, :]) * 1.0
    t["mask_h"] = (row % NH == np.arange(NH)[None, :]) * 1.0
    t["mask_g"] = (row % NH // 2 == np.arange(NG)[None, :]) * 1.0
    t["even"] = (row % 2 == 0) * 1.0
    t["odd"] = (row % 2 == 1) * 1.0
    t["one"] = np.ones((1, 1))
    out = np.zeros((P, C_W), np.float32)
    for name, (a, b) in C_AT.items():
        out[:, a:b] = t[name]
    return out


def laid_out(inp):
    def by_channel(a):
        return a.reshape(DEPTH, -1, P).transpose(0, 2, 1)

    big = ["x_prompt", "x_sample", "cache_k", "cache_v", "state_h", "state_conv", "w_in", "w_out", "w_exp_in", "w_exp_out"]
    a = {k: np.ascontiguousarray(inp[k]) for k in big}
    a["page_row"] = np.ascontiguousarray(inp["page_table"]).reshape(1, -1)
    cw = inp["conv_w"].reshape(DEPTH, CONV_W, NC, P).transpose(0, 3, 2, 1).reshape(DEPTH, P, 16)
    a["pf"] = np.ascontiguousarray(np.concatenate(
        [cw] + [by_channel(inp[k]) for k in ("conv_b", "b_ga", "b_gx", "lru_lambda", "ln1_g", "ln2_g")], 2))
    rows = [inp[k].reshape(DEPTH, 1, -1) for k in ("subln_g", "b_route_group", "b_route_expert", "lam_q1", "lam_k1", "lam_q2", "lam_k2")]
    li = np.array([0.8 - 0.6 * math.exp(-0.3 * n) for n in range(DEPTH)], np.float64)
    rows += [li.astype(np.float32).reshape(DEPTH, 1, 1), (1.0 - li).astype(np.float32).reshape(DEPTH, 1, 1)]
    a["pb"] = np.ascontiguousarray(np.broadcast_to(np.concatenate(rows, 2), (DEPTH, P, PB_W)))
    g = np.zeros((DEPTH, P, 2, NC, P), np.float32)
    for n, k in enumerate(("w_ga", "w_gx")):
        for i in range(NC):
            g[:, 0:64, n, i, 0:64] = inp[k][:, 2 * i]
            g[:, 64:128, n, i, 64:128] = inp[k][:, 2 * i + 1]
    a["gate_w"] = g
    r = np.concatenate([inp["w_route_group"], inp["w_route_expert"]], 2)
    a["route_w"] = np.ascontiguousarray(r.reshape(DEPTH, KC, P, 36).transpose(0, 2, 1, 3))
    a["ln_f"] = np.ascontiguousarray(np.broadcast_to(inp["ln_f"].reshape(1, D), (P, D)))
    a["consts"] = constants()
    return a


OUTS = [("y_prompt", (1, SEQ, D)), ("y_sample", (NS, 1, D)), ("new_k_prompt", (DEPTH, 1, SEQ, NH, HEAD)),
        ("new_v_prompt", (DEPTH, 1, SEQ, NG, 2 * HEAD)), ("new_h_prompt", (DEPTH, 1, D_RNN)),
        ("new_conv_prompt", (DEPTH, 1, CONV_W - 1, D_RNN)), ("new_k_sample", (DEPTH, NS, 1, NH, HEAD)),
        ("new_v_sample", (DEPTH, NS, 1, NG, 2 * HEAD)), ("new_h_sample", (DEPTH, NS, D_RNN)),
        ("new_conv_sample", (DEPTH, NS, CONV_W - 1, D_RNN))]


def kernel(**inputs):
    import concourse.bacc as _bacc
    from concourse.bass_utils import run_bass_kernel_spmd as _run

    nc = _bacc.Bacc("TRN2", target_bir_lowering=False, num_devices=1)
    arrays = laid_out({k: np.asarray(v) for k, v in inputs.items()})
    A = {k: nc.dram_tensor(f"in_{k}", v.shape, mybir.dt.from_np(v.dtype), kind="ExternalInput").ap() for k, v in arrays.items()}
    O = {k: nc.dram_tensor(f"out_{k}", s, F32, kind="ExternalOutput").ap() for k, s in OUTS}
    hybrid_step(nc, A, O)
    r = _run(nc, [{f"in_{k}": v for k, v in arrays.items()}], core_ids=[0])
    return tuple(r.results[0][f"out_{k}"] for k, _ in OUTS)
```

```python
import math
from contextlib import ExitStack

import concourse.bass as bass
from concourse import mybir
import numpy as np

ALU = mybir.AluOpType
ACT = mybir.ActivationFunctionType
AX = mybir.AxisListType
F32 = mybir.dt.float32
BF16 = mybir.dt.bfloat16
I32 = mybir.dt.int32

P = 128
D = 1024
KC = D // P
SEQ = 512
NT = SEQ // P
NTT = NT + 1
NS = 8
DEPTH = 2
D_RNN = 512
NC = D_RNN // P
CONV_W = 4
HEAD = 64
NG = 4
NH = 2 * NG
D_PROJ = 2560
PAST = 256
PAGE = 128
N_PAGES = PAST // PAGE
N_EXP = 32
N_GRP = 4
EPG = 8
D_EXP = 512
CAP = 64
MAX_OVF = (SEQ + NS) * 2 // CAP
NBLK = N_EXP + MAX_OVF
SCALE = HEAD ** -0.5
EPS = 1e-6
SUB_EPS = 1e-5
NEG = -1e30
WBUF = 12288
NBUF = 3
PEEL = 4

CONSTS = [("cos", NT * 64), ("sin", NT * 64), ("cos_s", 64), ("sin_s", 64), ("ident", P), ("mask", P),
          ("tri", P), ("iota_e", N_EXP), ("iota_blk", NBLK), ("cap_steps", MAX_OVF), ("iota_ovf", MAX_OVF),
          ("slot_row", CAP), ("tile_row", 1), ("tile_first", NTT), ("delta", NS * 32), ("first4", N_GRP), ("first8", EPG),
          ("half", 1), ("neghalf", 8), ("sel_b", 64), ("sel_t", NS), ("mask_h", NH), ("mask_g", NG),
          ("even", 1), ("odd", 1), ("one", 1)]
C_AT = {}
_at = 0
for _name, _w in CONSTS:
    C_AT[_name] = (_at, _at + _w)
    _at += _w
C_W = _at
PF = {"conv_w": (0, 16), "conv_b": (16, 20), "b_ga": (20, 24), "b_gx": (24, 28), "lam": (28, 32),
      "g1": (32, 40), "g2": (40, 48)}
PF_W = 48
PB = {"subln": (0, 128), "b_route": (128, 164), "lq1": (164, 228), "lk1": (228, 292), "lq2": (292, 356),
      "lk2": (356, 420), "lam_init": (420, 421), "one_less": (421, 422)}
PB_W = 422


def chain(eng, sem):
    count = [0]

    def settle(ins):
        count[0] += 1
        ins.then_inc(sem, 1)
        eng.wait_ge(sem, count[0])
        return ins
    return settle


def hybrid_step(nc, A, O):
    ctx = ExitStack()
    with ctx:
        def sb(name, shape, dt=F32):
            return ctx.enter_context(nc.sbuf_tensor(name, shape, dt))

        all_sems = []

        def sem(name):
            s = ctx.enter_context(nc.semaphore(name))
            all_sems.append(s)
            return s

        def once(name):
            return ctx.enter_context(nc.semaphore(name))

        def barrier_and_clear(sems):
            ids = range(sems[0].num, sems[-1].num + 1)
            assert len(ids) == len(sems)
            nc.all_engine_barrier()
            nc.gpsimd.dma_reset(ids)
            nc.gpsimd.sem_clear(ids)
            nc.all_engine_barrier()

        n_pool = A["cache_k"].shape[1]
        xn_dram = nc.dram_tensor("normed_rows", (SEQ + NS, D), F32, kind="Internal").ap()
        y_dram = nc.dram_tensor("expert_rows", (NBLK * CAP, D), F32, kind="Internal").ap()

        W = sb("W", [P, NBUF * WBUF])
        x = sb("x", [P, NTT, D])
        v_nat = sb("v_nat", [P, NT, 512])
        qT = sb("qT", [P, NG, SEQ])
        R = sb("R", [P, 6, 512])
        C = sb("C", [P, C_W])
        gate_w = sb("gate_w", [P, 2, NC, P])
        pf = sb("pf", [P, PF_W])
        pb = sb("pb", [P, PB_W])
        route_w = R[:, 5, 224:512].rearrange("p (k n) -> p k n", k=KC)
        hTs = sb("hTs", [P, KC, NS])
        yTs = sb("yTs", [P, KC, NS])
        ident_b = sb("ident_b", [P, P], BF16)
        mask_b = sb("mask_b", [P, P], BF16)
        tri_b = sb("tri_b", [P, P], BF16)
        ones_b = sb("ones_b", [P, P], BF16)
        pages = sb("pages", [1, NS * N_PAGES], I32)
        hc = sb("hc", [P, 2, NC])
        hbias = sb("hbias", [P, 2, NC])
        sp = sb("sp", [P, 6, NC])
        neglam = sb("neglam", [P, 4])
        subg = sb("subg", [P, P])
        st = sb("st", [P, 4, NTT])
        idx_i = sb("idx_i", [P, NBLK], I32)
        slot_i = sb("slot_i", [P, 2, NTT], I32)
        gate = sb("gate", [P, 2, NTT])
        ovf_i = sb("ovf_i", [P, MAX_OVF + 1], I32)
        cur = sb("cur", [P, 1], I32)
        PS = ctx.enter_context(nc.psum_tensor("PS", [P, 8, 512], F32))

        def c(name, rows=P):
            a, b = C_AT[name]
            return C[0:rows, a:b]

        def f(name):
            a, b = PF[name]
            return pf[:, a:b]

        def b_(name, rows=P):
            a, b = PB[name]
            return pb[0:rows, a:b]

        ident = c("ident")
        wg = W[:, 0:4096].rearrange("p (k n) -> p k n", k=KC)
        wx = W[:, 4096:8192].rearrange("p (k n) -> p k n", k=KC)
        wqkv = [W[:, 8192 + 4096 * i:12288 + 4096 * i].rearrange("p (k n) -> p k n", k=KC) for i in range(3)]
        hT = W[:, 20480:24576].rearrange("p (k n) -> p k n", k=KC)
        kc_nat = W[:, 0:8192].rearrange("p (g n) -> p g n", g=16)
        vc_nat = W[:, 8192:16384].rearrange("p (g n) -> p g n", g=16)
        RN = 24576
        AT = 16384
        w_out = W[:, 24576:32768].rearrange("p (k n) -> p k n", k=KC)
        yT = W[:, 32768:36864].rearrange("p (k n) -> p k n", k=KC)
        kT = yT[:, 4:8, :]

        def rn(a, n, rows=P):
            return W[0:rows, RN + a:RN + a + n]

        sxg = rn(0, 1024, NS)
        stc = rn(1024, 512, NS * 3)
        sqkv = [rn(512 * i, 512, NS) for i in range(3)]
        xn = [W[:, 32768:33792], W[:, 33792:34816]]
        junk = W[:, 34816:35840]
        sth = rn(1536, 512, NS)
        xr = [rn(2048, 516), rn(2564, 516)]
        xc = [rn(3080 + 512 * i, 512) for i in range(NC)]
        ra, ix, aa, th = (rn(5128 + 512 * i, 512) for i in range(4))
        sT = rn(7176, 192)
        xcs = rn(7368, 32).rearrange("p (c b) -> p c b", c=NC)
        s_ri = rn(7400, 64).rearrange("p (g c b) -> p g c b", g=2, c=NC)
        s_la, s_a, s_th, s_t1, s_t2 = (rn(7464 + 32 * i, 32).rearrange("p (c b) -> p c b", c=NC) for i in range(5))
        small = rn(7624, 48).rearrange("p (c n) -> p c n", c=NC)
        small_rows = rn(7672, 512, 12)
        xe = [v_nat[:, i, :] for i in range(NBUF)]
        xTe = [qT[:, i, :].rearrange("p (h c t) -> p h c t", h=2, c=4) for i in range(2)]
        hs = [R[:, 0, 256 * i:256 * i + 256] for i in range(2)]
        hh = [R[:, 1, 256 * i:256 * i + 256] for i in range(2)]
        hTe = [R[:, 2, 256 * i:256 * i + 256].rearrange("p (j h t) -> p j h t", j=2, h=2) for i in range(2)]
        ye = [R[:, 3 + i, :] for i in range(3)]

        def expert_in(i):
            return W[:, WBUF * i:WBUF * i + 8192].rearrange("p (k n) -> p k n", k=KC)

        def expert_out(i):
            return W[:, WBUF * i + 8192:WBUF * (i + 1)].rearrange("p (k n) -> p k n", k=4)

        def load_in_half(sp_, expert, r, h):
            src = w_in_rows[bass.ds(expert, 1), :, 4 * h:4 * h + 4, :].rearrange("e p k n -> p (e k) n")
            sp_.dma_start(expert_in(r)[:, 4 * h:4 * h + 4, :], src).then_inc(e_in[r][h], 16)

        w_in_rows = A["w_exp_in"].rearrange("l e (k p) n -> (l e) p k n", p=P)
        w_out_rows = A["w_exp_out"].rearrange("l e (k p) n -> (l e) p k n", p=P)
        y_blocks = y_dram.rearrange("(j r) n -> j r n", r=CAP)
        ck = A["cache_k"].rearrange("l g p h d -> (l g) p (h d)")
        cv = A["cache_v"].rearrange("l g p h d -> (l g) p (h d)")

        def squares_of_rows(act, t, ready):
            n = P if t < NT else NS
            act.activation(junk[0:n, :], x[0:n, t, :], ACT.Square, accum_out=st[0:n, 0, t:t + 1]).then_inc(ready, 1)
            act.wait_ge(ready, t + 1)

        def mean_of_squares(dve, summed, done):
            dve.wait_ge(summed, NTT)
            dve.tensor_scalar(st[:, 1, :], st[:, 0, :], 1.0 / D, EPS, ALU.mult, ALU.add).then_inc(done, 1)

        def inverse_roots(pool, summed, done):
            pool.wait_ge(summed, 1)
            pool.tensor_tensor(st[:, 2, :], st[:, 1, :], c("neghalf")[:, 0:NTT], ALU.pow).then_inc(done, 1)
            pool.wait_ge(done, 1)

        s_x = [once(f"x_tile_{t}_loaded") for t in range(NTT)]
        s_consts = once("constants_loaded")
        s_pages = once("page_table_loaded")
        s_made = once("tables_made")
        s_filled = once("fills_made")
        s_sum, s_mean, s_root = once("start_sums"), once("start_means"), once("start_roots")
        with nc.Block() as block:
            @block.gpsimd
            def _(pool):
                pool.memset(st[:, :, :], 1.0).then_inc(s_filled, 1)
                pool.memset(v_nat[:, :, :], 0.0).then_inc(s_filled, 1)
                pool.wait_ge(s_filled, 2)
                pool.wait_ge(s_consts, 16)
                inverse_roots(pool, s_mean, s_root)

            @block.sync
            def _(sp_):
                rows = A["x_prompt"].rearrange("b (t p) d -> p (b t) d", p=P)
                for t in range(NT):
                    sp_.dma_start(x[:, t, :], rows[:, t, :]).then_inc(s_x[t], 16)
                sp_.dma_start(x[0:NS, NT, :], A["x_sample"].rearrange("b s d -> (b s) d")).then_inc(s_x[NT], 16)
                sp_.dma_start(pages[:, :], A["page_row"]).then_inc(s_pages, 16)
                sp_.dma_start(C[:, :], A["consts"]).then_inc(s_consts, 16)
                sp_.wait_ge(s_pages, 16)

            @block.scalar
            def _(act):
                act.wait_ge(s_filled, 1)
                for t in range(NTT):
                    act.wait_ge(s_x[t], 16)
                    squares_of_rows(act, t, s_sum)

            @block.vector
            def _(dve):
                dve.wait_ge(s_consts, 16)
                dve.tensor_copy(ident_b[:, :], ident).then_inc(s_made, 1)
                dve.tensor_copy(mask_b[:, :], c("mask")).then_inc(s_made, 1)
                dve.tensor_copy(tri_b[:, :], c("tri")).then_inc(s_made, 1)
                dve.memset(ones_b[:, :], 1.0).then_inc(s_made, 1)
                dve.wait_ge(s_made, 4)
                mean_of_squares(dve, s_sum, s_mean)

        params = sem("params_loaded")
        gate_params = sem("gate_params_loaded")
        states = sem("states_loaded")
        w_ready = [sem(f"w_in_{n}_loaded") for n in "gxqkv"]
        s_zero = sem("overflow_rows_filled")
        xn_ready = sem("normed_ready")
        turned = sem("normed_turned")
        hT_ready = sem("hT_ready")
        proj = sem("projection_done")
        gx_read = sem("gate_and_x_read")
        rope_read = sem("rotary_read_psum")
        rope_sum = sem("rotary_done")
        rope_turned = sem("rotary_turned")
        rope_kept = sem("rotary_turned_kept")
        k_stored = [sem("k_rows_stored_even"), sem("k_rows_stored_odd")]
        stored = sem("project_rows_stored")
        conv_stored = sem("sample_conv_rows_stored")
        v_kept = sem("v_kept")
        conv_done = sem("conv_done")
        gates_done = sem("gate_products_done")
        gates_read = sem("gate_products_read")
        decay_done = sem("decay_done")
        m2_done = sem("one_less_a2_done")
        mult_done = sem("mult_done")
        scan_done = sem("scan_done")
        y_done = sem("rnn_output_done")
        s_proj = sem("sample_projection_done")
        s_read = sem("sample_projection_read")
        s_turned = sem("sample_turned")
        s_kept = sem("sample_turned_kept")
        s_conv = sem("sample_conv_done")
        s_gates = sem("sample_gates_done")
        s_pe = sem("sample_steps_dve")
        s_act = sem("sample_steps_act")
        small_turned = sem("last_states_turned")
        small_kept = sem("last_states_kept")
        k_pages = sem("k_pages_loaded")
        dve1, act1 = sem("dve_steps"), sem("act_steps")
        const_done = sem("recurrence_constants")
        sp_exp = sem("softplus_exp")

        v_pages = sem("v_pages_loaded")
        a_row = sem("sample_rotary_done")
        a_bc = sem("query_spread")
        a_mul = sem("query_product_done")
        a_prod = sem("query_product_summed")
        a_s = sem("sample_scores_done")
        a_pe = sem("sample_attention_pe")
        a_dve = sem("sample_attention_dve")
        a_act = sem("sample_attention_act")
        a_pool = sem("sample_attention_pool")
        a_stored = sem("sample_rows_stored")
        a_done = sem("sample_attention_done")
        lam_dve, lam_act = sem("lambda_sums"), sem("lambda_exps")
        scores = sem("scores_done")
        negmax = sem("negmax_ready")
        exps = sem("exps_done")
        amap = sem("map_difference_done")
        map_turned = sem("map_turned")
        map_kept = sem("map_turned_kept")
        av = sem("av_done")
        o_read = sem("o_read")
        o_sum = sem("o_sum_of_squares")
        o_var = sem("o_mean_square")
        o_rstd = sem("o_rstd")
        o_norm = sem("o_normed")
        o_turned = sem("o_turned")
        o_kept = sem("o_turned_kept")
        w_out_ready = sem("w_out_loaded")
        e_in = [[sem(f"expert_in_{i}_{h}_half_loaded") for h in ("first", "second")] for i in range(NBUF)]
        e_out = [sem(f"expert_out_{i}_loaded") for i in range(NBUF)]

        w_route = sem("router_weights_loaded")
        op_done = sem("output_product_done")
        x_new = sem("x_updated")
        sumsq2, mean2, rstd2, xn2_ready = sem("sumsq_2"), sem("mean_eps_2"), sem("rstd_2"), sem("normed_2")
        xn2_stored = [sem("normed_stored_even"), sem("normed_stored_odd")]
        turned2, h2_ready, logits = sem("turned_2"), sem("h2T_ready"), sem("logits_done")
        hot = sem("expert_hot_ready")
        ranks = sem("ranks_done")
        place = sem("slot_hot_ready")
        slots_done = sem("slot_tokens_done")
        slots_ready = sem("slot_indices_ready")
        r_act_in, r_act = sem("router_exp_input"), sem("router_exp_done")

        gathered = [sem(f"rows_gathered_{i}") for i in range(NBUF)]
        xe_turned = sem("rows_turned")
        xTe_ready = sem("xT_ready")
        in_half = sem("expert_in_half_done")
        in_done = sem("expert_in_done")
        ovf_ready = sem("overflow_blocks_known")
        silu_done = sem("silu_done")
        h_ready = sem("h_ready")
        h_turned = sem("h_turned")
        hT_kept = sem("h_turned_kept")
        out_done = sem("expert_out_done")
        y_kept = sem("expert_rows_kept")
        y_stored = [sem(f"expert_rows_stored_{i}") for i in range(3)]

        in_loop = len(all_sems)
        v_w, v_g, v_t, v_x, v_i, v_s, v_h, v_ht, v_hk, v_o, v_y, v_st = (
            sem("ovf_" + n) for n in ("weights", "rows", "turned", "xT", "in", "silu", "h", "h_turned", "h_kept",
                                      "out", "kept", "stored"))
        ovf_sems = all_sems[in_loop:]

        got = [sem(f"slot_rows_{t}_gathered") for t in range(NTT)]
        added = sem("slot_rows_added")
        sumsq, mean_eps, rstd = sem("next_sums"), sem("next_means"), sem("next_roots")

        with nc.Fori(0, DEPTH) as layer:
            def at(a, n, rows=P):
                return W[0:rows, AT + a:AT + a + n]

            prod = [at(1536 + 512 * i, 512) for i in range(N_PAGES)]
            key_scores = at(2560, 128).rearrange("p (g b h) -> p g b h", g=N_PAGES, b=NS)
            own = at(2688, 8, NS)
            s_row = at(2696, 260, 64)
            picked = at(2956, 8, 64)
            s_stat = at(2964, 8, 64)
            own_g = at(2972, 4, 64)
            pair_sum = at(2976, 64)
            spread_map = at(3040, 2048).rearrange("p (g b m r) -> p g b m r", g=N_PAGES, b=NS, m=NG)
            own_map = at(5088, 128, NS).rearrange("p (m r) -> p m r", m=NG)
            q_rot = at(5216, 512, NS)
            k_rot = at(5728, 512, NS)
            r_tmp = at(6240, 512, NS)
            own_prod = at(6752, 512, NS)
            so = at(7264, 128)
            so2 = at(7392, 128)
            so_st = at(7520, 4)
            lam_prod = at(7524, 128)
            lam_s = at(7652, 4)
            o1 = at(0, 512)
            o2 = at(512, 512)
            prob = [R[:, 0:2, :], R[:, 2:4, :]]
            kept_map = [R[:, 4, :], R[:, 5, :]]
            negm = at(7656, 64)
            lsum = at(7720, 32)
            linv = at(7752, 32)
            coef = at(7784, 16)
            ost = at(7800, 16)
            UNITS = [(g, t) for g in range(NG) for t in range(NT)]
            N_U = len(UNITS)

            def o_bank(g):
                return 5 + (NT * g + 8) % 2

            Rf = R[:, :, :].rearrange("p a n -> p (a n)")
            qf = qT[:, :, :].rearrange("p a n -> p (a n)")
            xn2 = [v_nat[:, 2 * i:2 * i + 2, :].rearrange("p a n -> p (a n)") for i in range(2)]
            h2T = [qT[:, 2 * i:2 * i + 2, :].rearrange("p a n -> p (a n)").rearrange("p (k n) -> p k n", k=KC) for i in range(2)]
            free_at = [0]

            def rr(n, rows=P):
                a = free_at[0]
                free_at[0] += n
                assert free_at[0] <= 2784
                return Rf[0:rows, a:a + n]

            lg = rr(NTT * 36).rearrange("p (t n) -> p t n", t=NTT)
            lg_g, lg_e = lg[:, :, 0:N_GRP], lg[:, :, N_GRP:36]
            emask = rr(160).rearrange("p (t g e) -> p t g e", t=NTT, g=N_GRP)
            E = rr(320).rearrange("p (k t e) -> p k t e", k=2, t=NTT)
            EW = rr(320).rearrange("p (k t e) -> p k t e", k=2, t=NTT)
            M_b = rr(80).bitcast(BF16).rearrange("p (t e) -> p t e", t=NTT)
            g_diff, g_exp, g_cand, g_hot = (rr(20).rearrange("p (t g) -> p t g", t=NTT) for _ in range(4))
            sel, sel2, cand = (rr(40).rearrange("p (t e) -> p t e", t=NTT) for _ in range(3))
            pick = rr(80).rearrange("p (k t e) -> p k t e", k=2, t=NTT)
            m_g, m_c, p_g, e_sum, m_1, m_2, e_d, e_2, rden = (rr(NTT) for _ in range(9))
            cnt, n_ovf, incl, base = (rr(N_EXP) for _ in range(4))
            rank, e_id, extra, base_k, blk, row_in = (rr(10) for _ in range(6))
            ovf_f = rr(MAX_OVF + 1)
            blk_hot = rr(2 * NTT * NBLK).rearrange("p (k t b) -> p k t b", k=2, t=NTT)
            tok_hot = qf[:, 320:320 + 2 * NTT * NBLK].bitcast(BF16).rearrange("p (a k t b) -> p a k t b", a=2, k=2, t=NTT)
            row_hot = qf[:, 0:10 * CAP // 2].bitcast(BF16).rearrange("p (k n) -> p k n", k=10)
            steps_hot = qf[:, 1280:1792]

            halves = xn_dram.rearrange("t (h n) -> (t h) n", h=2)

            def gather_rows(pool, e):
                pool.indirect_dma_start(xe[e % NBUF], None, halves, bass.IndirectOffsetOnAxis(idx_i[:, e:e + 1], 0)).then_inc(gathered[e % NBUF], 16)

            ORDER = [NT] + list(range(NT))

            def rows_of(p):
                return P if ORDER[p] < NT else NS

            def over(a, n):
                return a.unsqueeze(2).to_broadcast([a.shape[0], a.shape[1], n])

            g2hc = f("g2").rearrange("p (h c) -> p h c", h=2).unsqueeze(3).to_broadcast([P, 2, 4, CAP])

            def expert_pass(eng, step):
                for e in range(PEEL):
                    step(e, e)
                turns = (N_EXP - PEEL) // 6
                with eng.Fori(0, turns) as i:
                    for j in range(6):
                        step(i * 6 + (PEEL + j), PEEL + j)
                for e in range(PEEL + 6 * turns, N_EXP):
                    step(e, e)

            def at_least(eng, s, value):
                if not isinstance(value, int) or value > 0:
                    eng.wait_ge(s, value)

            def turn_rows(pe, rows):
                for j in range(4):
                    ins = pe.transpose(PS[:, 0, j * P:(j + 1) * P], rows[:, j * P:(j + 1) * P], ident)
                return ins

            def in_product(pe, xt, w, bank, before_second=None, half_done=None):
                for k in range(KC):
                    if k == 4 and before_second:
                        before_second()
                    for j in range(2):
                        cols = w[:, k, :].rearrange("p (u j n) -> p u j n", u=2, j=2)[:, :, j, :]
                        ins = pe.matmul(PS[64 * j:64 * j + 64, bank, :], xt[:, k // 4, k % 4, :], cols, start=(k == 0), stop=(k == KC - 1))
                    if k == 3 and half_done is not None:
                        ins.then_inc(half_done, 1)
                return ins

            def out_product(pe, ht, w, bank):
                for k in range(4):
                    for j in range(2):
                        ins = pe.matmul(PS[64 * j:64 * j + 64, bank, :], ht[:, k % 2, k // 2, :], w[:, k, 512 * j:512 * j + 512], start=(k == 0), stop=(k == 3))
                return ins

            with nc.Block() as block:
                @block.sync
                def _(sp_):
                    def w_cols(dst, col, s):
                        src = A["w_in"][bass.ds(layer, 1), :, col:col + 512].rearrange("l (k p) n -> p (l k) n", p=P)
                        sp_.dma_start(dst, src).then_inc(s, 16)

                    sp_.dma_start(pf[:, :], A["pf"][bass.ds(layer, 1)].rearrange("l p n -> p (l n)")).then_inc(params, 16)
                    sp_.dma_start(pb[:, :], A["pb"][bass.ds(layer, 1)].rearrange("l p n -> p (l n)")).then_inc(params, 16)
                    w_cols(wg, 512, w_ready[0])
                    w_cols(wx, 0, w_ready[1])
                    sp_.dma_start(gate_w[:, :, :, :], A["gate_w"][bass.ds(layer, 1)].rearrange("l p g c n -> p (l g) c n")).then_inc(gate_params, 16)
                    sp_.dma_start(stc, A["state_conv"][bass.ds(layer, 1)].rearrange("l b j n -> (l b j) n")).then_inc(states, 16)
                    sp_.dma_start(sth, A["state_h"][bass.ds(layer, 1)].rearrange("l b n -> (l b) n")).then_inc(states, 16)
                    for i in range(3):
                        w_cols(wqkv[i], 1024 + 512 * i, w_ready[2 + i])
                    sp_.wait_ge(s_proj, 1)
                    with sp_.Fori(0, NS * N_PAGES) as i:
                        page = sp_.value_load(pages[0:1, bass.ds(i, 1)], min_val=0, max_val=n_pool - 1)
                        sp_.dma_start(kc_nat[:, bass.ds(i, 1), :], ck[bass.ds(page + layer * n_pool, 1)].rearrange("g p n -> p g n")).then_inc(k_pages, 16)

                    sp_.wait_ge(s_proj, 2)
                    with sp_.Fori(0, NS * N_PAGES) as i:
                        page = sp_.value_load(pages[0:1, bass.ds(i, 1)], min_val=0, max_val=n_pool - 1)
                        sp_.dma_start(vc_nat[:, bass.ds(i, 1), :], cv[bass.ds(page + layer * n_pool, 1)].rearrange("g p n -> p g n")).then_inc(v_pages, 16)
                    new_k = O["new_k_sample"][bass.ds(layer, 1)].rearrange("l b s h d -> (l b s) (h d)")
                    new_v = O["new_v_sample"][bass.ds(layer, 1)].rearrange("l b s h d -> (l b s) (h d)")
                    sp_.wait_ge(s_read, 7)
                    sp_.dma_start(new_v, sqkv[2]).then_inc(a_stored, 16)
                    sp_.wait_ge(a_row, 2)
                    sp_.dma_start(new_k, k_rot).then_inc(a_stored, 16)
                    w_out_src = A["w_out"][bass.ds(layer, 1)].rearrange("l (k p) n -> p (l k) n", p=P)
                    sp_.wait_ge(stored, 16 * (NT + 3))
                    sp_.wait_ge(y_done, NC)
                    sp_.wait_ge(s_pe, 4)
                    sp_.dma_start(w_out[:, 2:KC, :], w_out_src[:, 2:KC, :]).then_inc(w_out_ready, 16)
                    expert = layer * N_EXP
                    sp_.wait_ge(a_prod, 2 * NS)
                    for h in range(2):
                        load_in_half(sp_, expert, 0, h)
                    sp_.wait_ge(a_stored, 32)
                    sp_.wait_ge(a_pe, 3)
                    sp_.dma_start(w_out[:, 0:2, :], w_out_src[:, 0:2, :]).then_inc(w_out_ready, 16)
                    sp_.dma_start(expert_out(0), w_out_rows[bass.ds(expert, 1)].rearrange("e p k n -> p (e k) n")).then_inc(e_out[0], 16)

                    sp_.wait_ge(av, N_U)
                    sp_.dma_start(route_w, A["route_w"][bass.ds(layer, 1)].rearrange("l p k n -> p (l k) n")).then_inc(w_route, 16)

                    def load_expert(i):
                        expert = layer * N_EXP + i
                        for h in range(2):
                            load_in_half(sp_, expert, i, h)
                        sp_.dma_start(expert_out(i), w_out_rows[bass.ds(expert, 1)].rearrange("e p k n -> p (e k) n")).then_inc(e_out[i], 16)

                    sp_.wait_ge(a_done, 1)
                    sp_.wait_ge(o_turned, NG)
                    load_expert(1)
                    for p, t in enumerate(ORDER):
                        n = rows_of(p)
                        sp_.wait_ge(xn2_ready, p + 1)
                        sp_.dma_start(xn_dram[t * P:t * P + n, :], xn2[p % 2][0:n, :]).then_inc(xn2_stored[p % 2], 16)
                        if p == 2:
                            sp_.wait_ge(op_done, 2 * NT + 1)
                            load_expert(2)

                    def load_in(e, r, expert):
                        sp_.wait_ge(in_half, e - 2)
                        load_in_half(sp_, expert, r, 0)
                        sp_.wait_ge(in_done, e - 2)
                        load_in_half(sp_, expert, r, 1)

                    def load_out(e, r, expert):
                        sp_.wait_ge(out_done, e - 2)
                        sp_.dma_start(expert_out(r), w_out_rows[bass.ds(expert, 1)].rearrange("e p k n -> p (e k) n")).then_inc(e_out[r], 16)

                    first = layer * N_EXP
                    load_in(NBUF, 0, first + NBUF)
                    turns = (N_EXP - NBUF - 1) // NBUF
                    with sp_.Fori(0, turns) as i:
                        for r in range(NBUF):
                            e = i * NBUF + (NBUF + 1 + r)
                            load_in(e, (1 + r) % NBUF, first + e)
                            load_out(e - 1, r, first + e - 1)
                    for e in range(NBUF + 1 + turns * NBUF, N_EXP):
                        load_in(e, e % NBUF, first + e)
                        load_out(e - 1, (e - 1) % NBUF, first + e - 1)
                    load_out(N_EXP - 1, (N_EXP - 1) % NBUF, first + N_EXP - 1)
                    sp_.wait_ge(ovf_ready, 1)
                    n_ovf_blocks = sp_.value_load(ovf_i[0:1, 0:1], min_val=0, max_val=MAX_OVF)
                    with sp_.If(n_ovf_blocks > 0):
                        which = sp_.value_load(ovf_i[0:1, 1:2], min_val=0, max_val=N_EXP - 1)
                        load_in(N_EXP, N_EXP % NBUF, first + which)
                        load_out(N_EXP, N_EXP % NBUF, first + which)

                @block.scalar
                def _(act):
                    settle = chain(act, act1)

                    def scale(t):
                        n = P if t < NT else NS
                        if t >= 2:
                            act.wait_ge(turned, 2 * (t - 1))
                        act.activation(xn[t % 2][0:n, :], x[0:n, t, :], ACT.Copy, scale=st[0:n, 2, t:t + 1]).then_inc(xn_ready, 1)

                    for t in range(NTT):
                        scale(t)
                    act.wait_ge(sp_exp, 1)
                    act.activation(sp[:, 1, :], sp[:, 0, :], ACT.Exp, scale=-1.0).then_inc(sp_exp, 1)
                    act.wait_ge(hT_ready, 2 * NT + 1)
                    for i in range(NC):
                        act.wait_ge(proj, i + 1)
                        act.activation(yT[:, i, :], PS[:, i % 4, :], ACT.Gelu_apprx_tanh).then_inc(gx_read, 1)
                    for i in range(NC):
                        act.wait_ge(proj, NC + i + 1)
                        if i == 0:
                            act.wait_ge(const_done, 2)
                        if i >= 2:
                            act.wait_ge(conv_done, i - 1)
                        act.activation(xr[i % 2][:, 3:515], PS[:, (NC + i) % 4, :], ACT.Copy).then_inc(gx_read, 1)
                    act.wait_ge(s_proj, 1)
                    for j in range(2):
                        act.activation(sxg[:, 512 + 256 * j:768 + 256 * j], PS[32 * j:32 * j + NS, 4, 0:256], ACT.Gelu_apprx_tanh).then_inc(s_read, 1)
                    for j in range(2):
                        act.activation(sxg[:, 256 * j:256 * j + 256], PS[64 + 32 * j:64 + 32 * j + NS, 4, 0:256], ACT.Copy).then_inc(s_read, 1)

                    def keep_turned(i):
                        t = i // 2
                        dst = (qT if i % 2 == 0 else kT)[:, :, t * P:(t + 1) * P]
                        act.wait_ge(rope_turned, i + 1)
                        act.activation(dst, PS[:, 7, :].rearrange("p (j n) -> p j n", j=NG), ACT.Copy, scale=SCALE if i % 2 == 0 else 1.0).then_inc(rope_kept, 1)

                    for t in range(NT):
                        if t == 1:
                            act.wait_ge(s_turned, 1)
                            act.activation(sT, PS[:, 4, 0:192], ACT.Copy).then_inc(s_kept, 1)
                        if t >= 1:
                            keep_turned(2 * t - 2)
                            keep_turned(2 * t - 1)
                        i = t
                        act.wait_ge(gates_done, i + 1)
                        if i >= 1:
                            act.wait_ge(y_done, i)
                        settle(act.activation(ra, PS[:, 5, :], ACT.Tanh, scale=0.5, bias=hbias[:, 0, i:i + 1]))
                        act.activation(ix, PS[:, 6, :], ACT.Tanh, scale=0.5, bias=hbias[:, 1, i:i + 1]).then_inc(gates_read, 1)
                        act.activation(th, ra, ACT.Tanh, scale=hc[:, 1, i:i + 1], bias=hc[:, 1, i:i + 1]).then_inc(decay_done, 1)
                        settle(act.activation(aa, ra, ACT.Exp, scale=hc[:, 0, i:i + 1], bias=hc[:, 0, i:i + 1]))
                        act.activation(ra, aa, ACT.Square).then_inc(decay_done, 1)
                        act.wait_ge(m2_done, i + 1)
                        act.activation(th, th, ACT.Sqrt).then_inc(mult_done, 1)
                        act.wait_ge(proj, 8 + 3 * t + 3)
                        if t == 0:
                            act.wait_ge(s_zero, 64)
                        act.activation(v_nat[:, t, :], PS[:, (8 + 3 * t + 2) % 4, :], ACT.Copy).then_inc(v_kept, 1)
                    keep_turned(6)
                    keep_turned(7)
                    act.wait_ge(s_pe, 1)
                    act.activation(s_ri, s_ri, ACT.Tanh).then_inc(s_act, 1)
                    act.wait_ge(s_pe, 2)
                    act.activation(s_a, s_la, ACT.Exp).then_inc(s_act, 1)
                    act.activation(s_th, s_la, ACT.Tanh, scale=-1.0).then_inc(s_act, 1)
                    act.wait_ge(s_pe, 3)
                    act.activation(s_th, s_th, ACT.Sqrt).then_inc(s_act, 1)
                    act.wait_ge(s_proj, 2)
                    act.wait_ge(s_turned, 1)
                    act.wait_ge(conv_stored, 32)
                    for j in range(3):
                        act.activation(sqkv[j], PS[32 * j:32 * j + NS, 4, :], ACT.Copy, scale=SCALE if j == 0 else 1.0).then_inc(s_read, 1)
                    act.wait_ge(small_turned, 1)
                    act.activation(small_rows, PS[0:12, 7, :], ACT.Copy).then_inc(small_kept, 1)

                    act.wait_ge(lam_dve, 1)
                    act.activation(lam_s[:, 2:4], lam_s[:, 0:2], ACT.Exp).then_inc(lam_act, 1)

                    def sample_exp():
                        act.wait_ge(a_dve, 1)
                        act.activation(s_row[:, 0:PAST + 1], s_row[:, 0:PAST + 1], ACT.Exp, bias=s_stat[:, 0:1], accum_out=s_stat[:, 2:3]).then_inc(a_act, 1)

                    def exp_rows(u):
                        g, t = UNITS[u]
                        n = (t + 1) * P
                        act.wait_ge(negmax, u + 1)
                        if u == 0:
                            act.wait_ge(rope_turned, 2 * NT)
                        if u < 2:
                            act.wait_ge(k_stored[u], 32)
                        if u >= 2:
                            act.wait_ge(map_turned, u - 1)
                        for m in range(2):
                            ins = act.activation(prob[u % 2][:, m, 0:n], PS[:, 2 * (u % 2) + m, 0:n], ACT.Exp,
                                                 bias=negm[:, 2 * u + m:2 * u + m + 1], accum_out=lsum[:, 2 * u + m:2 * u + m + 1])
                        ins.then_inc(exps, 1)

                    def keep_map(u):
                        g, t = UNITS[u]
                        n = (t + 1) * P
                        act.wait_ge(map_turned, u + 1)
                        if u >= 2:
                            act.wait_ge(av, u - 1)
                        act.activation(kept_map[u % 2][:, 0:n], PS[:, 5 + u % 2, 0:n], ACT.Copy).then_inc(map_kept, 1)

                    def keep_o(g):
                        act.wait_ge(o_turned, g + 1)
                        act.activation(yT[:, 4 + g, :], PS[:, o_bank(g), :], ACT.Copy).then_inc(o_kept, 1)

                    def squares_of_o(g):
                        act.wait_ge(o_read, g + 1)
                        if g >= 1:
                            act.wait_ge(o_rstd, g)
                        for t in range(NT):
                            ins = act.activation(o2[:, t * P:(t + 1) * P], o1[:, t * P:(t + 1) * P], ACT.Square, accum_out=ost[:, t:t + 1])
                        ins.then_inc(o_sum, 1)

                    for i in range(N_U + 6):
                        if i >= 9 and (i - 9) % 4 == 0:
                            keep_o((i - 9) // 4)
                        if 2 <= i <= N_U + 1:
                            keep_map(i - 2)
                        if i >= 7 and (i - 7) % 4 == 0 and i < N_U + 4:
                            squares_of_o((i - 7) // 4)
                        if i < N_U:
                            exp_rows(i)
                        if i == 8:
                            sample_exp()

                    def square(p):
                        n, t = rows_of(p), ORDER[p]
                        act.wait_ge(x_new, 2 * p + 1)
                        if p == 0:
                            act.wait_ge(stored, 16 * (NT + 3))
                        if p >= 2:
                            act.wait_ge(turned2, 2 * p - 2)
                            act.wait_ge(xn2_stored[p % 2], 16 * (p // 2))
                        act.activation(xn2[p % 2][0:n, :], x[0:n, t, :], ACT.Square, accum_out=st[0:n, 0, t:t + 1]).then_inc(sumsq2, 1)

                    def scale(p):
                        n, t = rows_of(p), ORDER[p]
                        act.wait_ge(rstd2, p + 1)
                        act.wait_ge(sumsq2, p + 1)
                        act.activation(xn2[p % 2][0:n, :], x[0:n, t, :], ACT.Copy, scale=st[0:n, 2, t:t + 1]).then_inc(xn2_ready, 1)

                    for i in range(NTT + 1):
                        if i >= 1:
                            scale(i - 1)
                        if i < NTT:
                            square(i)
                    act.wait_ge(r_act_in, 1)
                    act.activation(g_exp, g_diff, ACT.Exp).then_inc(r_act, 1)
                    act.wait_ge(r_act_in, 2)
                    act.activation(e_2, e_d, ACT.Exp).then_inc(r_act, 1)

                    def silu(e, s):
                        act.wait_ge(in_done, e + 1)
                        at_least(act, h_ready, e - 1)
                        act.activation(hs[s % 2], PS[:, 2 + s % 2, 0:256], ACT.Silu).then_inc(silu_done, 1)

                    def step(e, s):
                        p2 = s % 2
                        if not isinstance(e, int) or e < N_EXP - 1:
                            silu(e + 1, s + 1)
                        act.wait_ge(h_turned, e + 1)
                        at_least(act, out_done, e - 1)
                        act.activation(hTe[p2], PS[:, 4, 0:256].rearrange("p (j h t) -> p j h t", j=2, h=2), ACT.Copy).then_inc(hT_kept, 1)
                        if not isinstance(e, int) or 1 <= e < N_EXP:
                            store_rows(e - 1, s - 1)

                    def store_rows(e, s):
                        r = s % 3
                        act.wait_ge(out_done, e + 1)
                        at_least(act, y_stored[r], (e - r) * 32 // 3)
                        act.activation(ye[r], PS[:, 5 + s % 2, :], ACT.Copy).then_inc(y_kept, 1)
                        act.wait_ge(y_kept, e + 1)
                        for j in range(2):
                            act.dma_start(y_blocks[bass.ds(e, 1), :, 512 * j:512 * j + 512].rearrange("e r n -> r (e n)"), ye[r][64 * j:64 * j + 64, :]).then_inc(y_stored[r], 16)

                    act.wait_ge(ovf_ready, 1)
                    n_ovf_blocks = act.value_load(ovf_i[0:1, 0:1], min_val=0, max_val=MAX_OVF)
                    silu(0, 0)
                    expert_pass(act, step)
                    store_rows(N_EXP - 1, N_EXP - 1)
                    with act.If(n_ovf_blocks > 0):
                        silu(N_EXP, N_EXP)
                        step(N_EXP, N_EXP)
                        store_rows(N_EXP, N_EXP)
                        act.wait_ge(y_stored[N_EXP % 3], 32 * (N_EXP // 3 + 1))
                        act.wait_ge(y_kept, N_EXP + 1)
                    for r in range(3):
                        act.wait_ge(y_stored[r], 32 * ((N_EXP - 1 - r) // 3 + 1))

                def spread(dve, t):
                    g1 = f("g1")
                    if t < NT:
                        for h in range(2):
                            u = 2 * t + h
                            dve.wait_ge(turned, u + 1)
                            dve.tensor_tensor(hT[:, 4 * h:4 * h + 4, t * P:(t + 1) * P], PS[:, u % 4, :].rearrange("p (k n) -> p k n", k=4),
                                              g1[:, 4 * h:4 * h + 4].unsqueeze(2).to_broadcast([P, 4, P]), ALU.mult).then_inc(hT_ready, 1)
                    else:
                        dve.wait_ge(turned, 2 * NT + 1)
                        dve.tensor_tensor(hTs[:, :, :], PS[:, 0, 0:64].rearrange("p (k n) -> p k n", k=KC),
                                          g1.unsqueeze(2).to_broadcast([P, KC, NS]), ALU.mult).then_inc(hT_ready, 1)

                @block.vector
                def _(dve):
                    settle = chain(dve, dve1)
                    dve.wait_ge(params, 32)
                    for t in range(NTT):
                        spread(dve, t)
                    settle(dve.tensor_scalar(sp[:, 5, :], f("lam"), -1.0, None, ALU.mult))
                    settle(dve.tensor_tensor(sp[:, 0, :], f("lam"), sp[:, 5, :], ALU.max))
                    dve.tensor_scalar(sp[:, 5, :], sp[:, 5, :], 0.0, None, ALU.max).then_inc(sp_exp, 1)
                    dve.wait_ge(sp_exp, 2)
                    settle(dve.tensor_scalar(sp[:, 2, :], sp[:, 1, :], 2.0, None, ALU.add))
                    settle(dve.reciprocal(sp[:, 2, :], sp[:, 2, :]))
                    settle(dve.tensor_tensor(sp[:, 2, :], sp[:, 2, :], sp[:, 1, :], ALU.mult))
                    settle(dve.tensor_tensor(sp[:, 3, :], sp[:, 2, :], sp[:, 2, :], ALU.mult))
                    settle(dve.tensor_scalar(sp[:, 4, :], sp[:, 3, :], 1.0 / 17, 1.0 / 15, ALU.mult, ALU.add))
                    for k in (13, 11, 9, 7, 5, 3, 1):
                        settle(dve.tensor_tensor(sp[:, 4, :], sp[:, 4, :], sp[:, 3, :], ALU.mult))
                        settle(dve.tensor_scalar(sp[:, 4, :], sp[:, 4, :], 1.0 / k, None, ALU.add))
                    settle(dve.tensor_tensor(sp[:, 4, :], sp[:, 4, :], sp[:, 2, :], ALU.mult))
                    settle(dve.scalar_tensor_tensor(sp[:, 4, :], sp[:, 4, :], 2.0, sp[:, 5, :], ALU.mult, ALU.add))
                    settle(dve.tensor_scalar(hc[:, 0, :], sp[:, 4, :], -4.0, None, ALU.mult))
                    settle(dve.tensor_scalar(hc[:, 1, :], sp[:, 4, :], 4.0, None, ALU.mult))
                    settle(dve.tensor_scalar(hbias[:, 0, :], f("b_ga"), 0.5, None, ALU.mult))
                    dve.tensor_scalar(hbias[:, 1, :], f("b_gx"), 0.5, None, ALU.mult).then_inc(const_done, 1)
                    settle(dve.memset(xr[0][:, 0:3], 0.0))
                    dve.memset(xr[1][:, 0:3], 0.0).then_inc(const_done, 1)
                    for i in range(NC):
                        cw, cb = f("conv_w"), f("conv_b")
                        dve.wait_ge(gx_read, NC + i + 1)
                        settle(dve.tensor_scalar(xc[i], xr[i % 2][:, 0:512], cw[:, 4 * i:4 * i + 1], cb[:, i:i + 1], ALU.mult, ALU.add))
                        settle(dve.tensor_copy(small[:, i, 9:12], xr[i % 2][:, 512:515]))
                        for j in range(1, CONV_W):
                            ins = dve.scalar_tensor_tensor(xc[i], xr[i % 2][:, j:j + 512], cw[:, 4 * i + j:4 * i + j + 1], xc[i], ALU.mult, ALU.add)
                            if j < CONV_W - 1:
                                settle(ins)
                        ins.then_inc(conv_done, 1)
                    dve.wait_ge(conv_done, NC)

                    def rotary(i):
                        t, which = i // 2, i % 2
                        unit = 8 + 3 * t + which
                        bank = PS[:, unit % 4, :].rearrange("p (h n) -> p h n", h=NH)
                        A_ = R[:, i % 4, :].rearrange("p (h n) -> p h n", h=NH)
                        B_ = R[:, 4 + i % 2, :].rearrange("p (h n) -> p h n", h=NH)
                        cos = c("cos").rearrange("p (t n) -> p t n", t=NT)[:, t:t + 1, :].to_broadcast([P, NH, 64])
                        sin = c("sin").rearrange("p (t n) -> p t n", t=NT)[:, t:t + 1, :]
                        dve.wait_ge(proj, unit + 1)
                        if i >= 4:
                            dve.wait_ge(rope_turned, i - 3)
                            if which == 1:
                                dve.wait_ge(k_stored[t % 2], 16 * (t // 2))
                        if i >= 2:
                            dve.wait_ge(rope_sum, i - 1)
                        settle(dve.tensor_tensor(A_, bank, cos, ALU.mult))
                        settle(dve.tensor_tensor(B_[:, :, 0:32], bank[:, :, 32:64], sin[:, :, 0:32].to_broadcast([P, NH, 32]), ALU.mult))
                        dve.tensor_tensor(B_[:, :, 32:64], bank[:, :, 0:32], sin[:, :, 32:64].to_broadcast([P, NH, 32]), ALU.mult).then_inc(rope_read, 1)

                    def wide(a):
                        return a.unsqueeze(2).to_broadcast([P, NC, NS])

                    for t in range(NT):
                        i = t
                        rotary(2 * t)
                        rotary(2 * t + 1)
                        dve.wait_ge(decay_done, 2 * i + 2)
                        dve.scalar_tensor_tensor(th, ra, 1.0, th, ALU.add, ALU.mult).then_inc(m2_done, 1)
                        dve.wait_ge(gates_read, i + 1)
                        settle(dve.scalar_tensor_tensor(ix, ix, 1.0, xc[i], ALU.add, ALU.mult))
                        dve.wait_ge(mult_done, i + 1)
                        settle(dve.memset(th[:, 0:1], 1.0))
                        settle(dve.scalar_tensor_tensor(ix, ix, 0.5, th, ALU.mult, ALU.mult))
                        settle(dve.tensor_tensor_scan(ra, aa, ix, 0.0, ALU.mult, ALU.add))
                        dve.tensor_copy(small[:, i, 8:9], ra[:, 511:512]).then_inc(scan_done, 1)
                        if t == 1:
                            dve.wait_ge(s_kept, 1)
                            kept = sT[:, 64:160].rearrange("p (c b j) -> p c b j", c=NC, b=NS)
                            cw = f("conv_w").rearrange("p (c j) -> p c j", c=NC)
                            settle(dve.tensor_tensor(xcs, sT[:, 0:32].rearrange("p (c b) -> p c b", c=NC), wide(cw[:, :, 3]), ALU.mult))
                            for j in range(3):
                                settle(dve.tensor_tensor(s_t1, kept[:, :, :, j], wide(cw[:, :, j]), ALU.mult))
                                settle(dve.tensor_tensor(xcs, xcs, s_t1, ALU.add))
                            dve.tensor_tensor(xcs, xcs, wide(f("conv_b")), ALU.add).then_inc(s_conv, 1)
                    dve.wait_ge(s_gates, 1)
                    for g in range(2):
                        ins = dve.scalar_tensor_tensor(s_ri[:, g], PS[:, 4, 256 + 32 * g:288 + 32 * g].rearrange("p (c b) -> p c b", c=NC), 0.5,
                                                       wide(hbias[:, g, :]), ALU.mult, ALU.add)
                        if g == 0:
                            settle(ins)
                    ins.then_inc(s_pe, 1)
                    dve.wait_ge(s_act, 1)
                    dve.scalar_tensor_tensor(s_la, s_ri[:, 0], 1.0, wide(hc[:, 0, :]), ALU.add, ALU.mult).then_inc(s_pe, 1)
                    dve.wait_ge(s_act, 3)
                    settle(dve.tensor_tensor(s_t1, s_a, s_a, ALU.mult))
                    dve.scalar_tensor_tensor(s_th, s_t1, 1.0, s_th, ALU.add, ALU.mult).then_inc(s_pe, 1)
                    settle(dve.scalar_tensor_tensor(s_t2, s_ri[:, 1], 1.0, xcs, ALU.add, ALU.mult))
                    dve.wait_ge(s_act, 4)
                    settle(dve.scalar_tensor_tensor(s_t2, s_t2, 0.5, s_th, ALU.mult, ALU.mult))
                    settle(dve.tensor_tensor(s_t1, s_a, sT[:, 160:192].rearrange("p (c b) -> p c b", c=NC), ALU.mult))
                    settle(dve.tensor_tensor(small[:, :, 0:NS], s_t1, s_t2, ALU.add))
                    dve.tensor_tensor(yTs[:, 0:NC, :], small[:, :, 0:NS], sT[:, 32:64].rearrange("p (c b) -> p c b", c=NC), ALU.mult).then_inc(s_pe, 1)

                    dve.wait_ge(s_proj, 2)
                    settle(dve.tensor_tensor(lam_prod[:, 0:64], b_("lq1"), b_("lk1"), ALU.mult))
                    settle(dve.tensor_tensor(lam_prod[:, 64:128], b_("lq2"), b_("lk2"), ALU.mult))
                    dve.tensor_reduce(lam_s[:, 0:2], lam_prod.rearrange("p (a n) -> p a n", a=2), AX.X, ALU.add).then_inc(lam_dve, 1)
                    dve.wait_ge(lam_act, 1)
                    settle(dve.tensor_tensor(neglam[:, 1:2], lam_s[:, 3:4], lam_s[:, 2:3], ALU.subtract))
                    settle(dve.tensor_tensor(neglam[:, 0:1], neglam[:, 1:2], b_("lam_init"), ALU.subtract))
                    settle(dve.tensor_scalar(subg[:, :], b_("subln"), b_("one_less"), None, ALU.mult))
                    settle(dve.tensor_tensor(neglam[:, 2:3], neglam[:, 0:1], c("odd"), ALU.mult))
                    settle(dve.tensor_tensor(neglam[:, 3:4], neglam[:, 2:3], c("even"), ALU.add))

                    cos = c("cos_s", NS).unsqueeze(1).to_broadcast([NS, NH, 64])
                    sin = c("sin_s", NS).unsqueeze(1)
                    dve.wait_ge(s_read, 7)
                    for src, dst in ((sqkv[0], q_rot), (sqkv[1], k_rot)):
                        a = src.rearrange("p (h n) -> p h n", h=NH)
                        d = dst.rearrange("p (h n) -> p h n", h=NH)
                        r = r_tmp.rearrange("p (h n) -> p h n", h=NH)
                        settle(dve.tensor_tensor(d, a, cos, ALU.mult))
                        settle(dve.tensor_tensor(r[:, :, 0:32], a[:, :, 32:64], sin[:, :, 0:32].to_broadcast([NS, NH, 32]), ALU.mult))
                        settle(dve.tensor_tensor(r[:, :, 32:64], a[:, :, 0:32], sin[:, :, 32:64].to_broadcast([NS, NH, 32]), ALU.mult))
                        dve.tensor_tensor(d, d, r, ALU.add).then_inc(a_row, 1)
                    dve.wait_ge(a_row, 2)
                    settle(dve.tensor_tensor(own_prod, q_rot, k_rot, ALU.mult))
                    dve.tensor_reduce(own, own_prod.rearrange("p (h n) -> p h n", h=NH), AX.X, ALU.add).then_inc(a_s, 1)
                    def page_scores(b):
                        if b == 0:
                            dve.wait_ge(k_pages, 16 * NS * N_PAGES)
                        dve.wait_ge(a_bc, b + 1)
                        if b >= 1:
                            dve.wait_ge(a_prod, 2 * b)
                        for g in range(N_PAGES):
                            dve.tensor_tensor(prod[g], kc_nat[:, b * N_PAGES + g, :], PS[:, 7, :], ALU.mult).then_inc(a_mul, 1)
                        for g in range(N_PAGES):
                            dve.wait_ge(a_mul, b * N_PAGES + g + 1)
                            dve.tensor_reduce(key_scores[:, g, b, :], prod[g].rearrange("p (h n) -> p h n", h=NH), AX.X, ALU.add).then_inc(a_prod, 1)

                    def sample_rows():
                        dve.wait_ge(a_pe, 1)
                        settle(dve.tensor_copy(s_row[:, 0:PAST], PS[0:64, 7, 0:PAST]))
                        settle(dve.tensor_tensor(picked, PS[0:64, 7, 256:264], c("mask_h", 64), ALU.mult))
                        settle(dve.tensor_reduce(s_row[:, PAST:PAST + 1], picked, AX.X, ALU.add))
                        dve.tensor_reduce(s_stat[:, 0:1], s_row[:, 0:PAST + 1], AX.X, ALU.max, negate=True).then_inc(a_dve, 1)

                    def sample_probs():
                        dve.wait_ge(a_act, 1)
                        settle(dve.reciprocal(s_stat[:, 3:4], s_stat[:, 2:3]))
                        settle(dve.tensor_tensor(s_stat[:, 4:5], s_stat[:, 3:4], neglam[0:64, 3:4], ALU.mult))
                        settle(dve.tensor_scalar(s_row[:, 0:PAST + 1], s_row[:, 0:PAST + 1], s_stat[:, 4:5], None, ALU.mult))
                        dve.tensor_scalar(own_g, c("mask_g", 64), s_row[:, PAST:PAST + 1], None, ALU.mult).then_inc(a_dve, 1)

                    def sample_maps():
                        dve.wait_ge(a_pe, 2)
                        settle(dve.tensor_reduce(pair_sum, PS[:, 7, 272:400].rearrange("p (n two) -> p n two", two=2), AX.X, ALU.add))
                        maps = pair_sum.rearrange("p (g b m) -> p g b m", g=N_PAGES, b=NS)
                        delta = c("delta").rearrange("p (b r) -> p b r", b=NS)
                        for g in range(N_PAGES):
                            dve.tensor_tensor(spread_map[:, g], maps[:, g].unsqueeze(3).to_broadcast([P, NS, NG, 32]),
                                              delta.unsqueeze(2).to_broadcast([P, NS, NG, 32]), ALU.mult).then_inc(a_dve, 1)
                        dve.tensor_tensor(own_map, PS[0:NS, 7, 264:268].unsqueeze(2).to_broadcast([NS, NG, 32]),
                                          c("ident", NS)[:, 0:32].unsqueeze(1).to_broadcast([NS, NG, 32]), ALU.mult).then_inc(a_dve, 1)

                    def sample_squares():
                        dve.wait_ge(a_pe, 3)
                        settle(dve.tensor_copy(so, PS[:, 7, 0:128]))
                        settle(dve.tensor_tensor(so2, so, so, ALU.mult))
                        settle(dve.tensor_reduce(so_st[:, 0:1], so2, AX.X, ALU.add))
                        dve.tensor_scalar(so_st[:, 1:2], so_st[:, 0:1], 1.0 / 128, SUB_EPS, ALU.mult, ALU.add).then_inc(a_dve, 1)

                    def sample_norm():
                        dve.wait_ge(a_pool, 1)
                        dve.scalar_tensor_tensor(so2, so, so_st[:, 2:3], subg[:, :], ALU.mult, ALU.mult).then_inc(a_dve, 1)

                    def sample_keep():
                        dve.wait_ge(a_pe, 4)
                        dve.tensor_copy(yTs[:, 4:8, :], PS[:, 7, 256:384].rearrange("p (m r) -> p m r", m=NG)[:, :, 0:NS]).then_inc(a_done, 1)

                    def best(u):
                        g, t = UNITS[u]
                        b = 2 * (u % 2)
                        dve.wait_ge(scores, u + 1)
                        dve.tensor_reduce(negm[:, 2 * u:2 * u + 2], PS[:, b:b + 2, 0:(t + 1) * P], AX.X, ALU.max, negate=True).then_inc(negmax, 1)

                    def difference(u):
                        g, t = UNITS[u]
                        n = (t + 1) * P
                        dve.wait_ge(exps, u + 1)
                        settle(dve.reciprocal(linv[:, 2 * u:2 * u + 2], lsum[:, 2 * u:2 * u + 2]))
                        settle(dve.scalar_tensor_tensor(coef[:, u:u + 1], lsum[:, 2 * u:2 * u + 1], linv[:, 2 * u + 1:2 * u + 2], neglam[:, 0:1], ALU.mult, ALU.mult))
                        dve.scalar_tensor_tensor(prob[u % 2][:, 0, 0:n], prob[u % 2][:, 1, 0:n], coef[:, u:u + 1], prob[u % 2][:, 0, 0:n], ALU.mult, ALU.add).then_inc(amap, 1)

                    o1v = o1.rearrange("p (t n) -> p t n", t=NT)

                    def read_o(g):
                        inv = linv.rearrange("p (g t m) -> p g t m", g=NG, t=NT)[:, g, :, 0]
                        dve.wait_ge(av, NT * (g + 1))
                        if g >= 1:
                            dve.wait_ge(o_turned, g)
                        dve.tensor_tensor(o1v, PS[:, 4, :].rearrange("p (t n) -> p t n", t=NT), inv.unsqueeze(2).to_broadcast([P, NT, P]), ALU.mult).then_inc(o_read, 1)

                    def norm(g):
                        dve.wait_ge(o_rstd, g + 1)
                        for t in range(NT):
                            ins = dve.scalar_tensor_tensor(o1v[:, t, :], o1v[:, t, :], ost[:, 8 + t:9 + t], subg[:, :], ALU.mult, ALU.mult)
                        ins.then_inc(o_norm, 1)

                    after = {8: sample_rows, 9: sample_probs, 10: sample_maps, 13: sample_squares, 14: sample_norm, 15: sample_keep}
                    for i in range(N_U + 6):
                        if i >= 7 and (i - 7) % 4 == 0 and i < N_U + 4:
                            read_o((i - 7) // 4)
                        if i < N_U:
                            best(i)
                        if i >= 8 and (i - 8) % 4 == 0:
                            norm((i - 8) // 4)
                        if 1 <= i <= N_U:
                            difference(i - 1)
                        if i < NS:
                            page_scores(i)
                        elif i in after:
                            after[i]()

                    g2 = f("g2")

                    def residual(p):
                        t = ORDER[p]
                        if t == NT:
                            dve.wait_ge(op_done, 1)
                            for j in range(4):
                                ins = dve.tensor_tensor(x[0:NS, NT, 256 * j:256 * j + 256], PS[32 * j:32 * j + NS, 4, 0:256], x[0:NS, NT, 256 * j:256 * j + 256], ALU.add)
                            ins.then_inc(x_new, 1)
                            return
                        for h in range(2):
                            dve.wait_ge(op_done, 2 * p + h)
                            dve.tensor_tensor(x[:, t, 512 * h:512 * h + 512], PS[:, (2 * t + h) % 4, :], x[:, t, 512 * h:512 * h + 512], ALU.add).then_inc(x_new, 1)

                    def mean(p):
                        n, t = rows_of(p), ORDER[p]
                        dve.wait_ge(sumsq2, p + 1)
                        dve.tensor_scalar(st[0:n, 1, t:t + 1], st[0:n, 0, t:t + 1], 1.0 / D, EPS, ALU.mult, ALU.add).then_inc(mean2, 1)

                    def keep(p):
                        n = rows_of(p)
                        if p >= 2:
                            dve.wait_ge(logits, p - 1)
                        for h in range(2):
                            dve.wait_ge(turned2, 2 * p + h + 1)
                            dve.tensor_tensor(h2T[p % 2][:, 4 * h:4 * h + 4, 0:n], PS[:, 5 + h, :].rearrange("p (k n) -> p k n", k=4)[:, :, 0:n],
                                              over(g2[:, 4 * h:4 * h + 4], n), ALU.mult).then_inc(h2_ready, 1)

                    for i in range(NTT + 2):
                        if i < NTT:
                            residual(i)
                        if 1 <= i <= NTT:
                            mean(i - 1)
                        if i >= 2:
                            keep(i - 2)

                    settle(dve.memset(lg, 0.0))
                    dve.wait_ge(logits, NTT)
                    br = b_("b_route").unsqueeze(1)
                    settle(dve.tensor_tensor(lg[:, 0:NT, :], PS[:, 7, 0:36 * NT].rearrange("p (t n) -> p t n", t=NT), br.to_broadcast([P, NT, 36]), ALU.add))
                    settle(dve.tensor_tensor(lg[0:NS, NT, :], PS[0:NS, 7, 36 * NT:36 * NTT], b_("b_route", NS), ALU.add))
                    settle(dve.tensor_reduce(m_g, lg_g, AX.X, ALU.max))
                    dve.tensor_tensor(g_diff, lg_g, over(m_g, N_GRP), ALU.subtract).then_inc(r_act_in, 1)
                    dve.wait_ge(r_act_in, 1)
                    first4 = c("first4").unsqueeze(1).to_broadcast([P, NTT, N_GRP])
                    first8 = c("first8").unsqueeze(1).to_broadcast([P, NTT, EPG])
                    settle(dve.scalar_tensor_tensor(g_cand, g_diff, 0.0, first4, ALU.is_ge, ALU.mult))
                    settle(dve.tensor_reduce(m_c, g_cand, AX.X, ALU.max))
                    settle(dve.tensor_tensor(g_hot, g_cand, over(m_c, N_GRP), ALU.is_equal))
                    settle(dve.tensor_tensor(emask, lg_e.rearrange("p t (g e) -> p t g e", g=N_GRP), g_hot.unsqueeze(3).to_broadcast([P, NTT, N_GRP, EPG]), ALU.mult))
                    settle(dve.tensor_reduce(sel, emask.rearrange("p t g e -> p t e g"), AX.X, ALU.add))

                    def first_best(logit, best, hot_out):
                        settle(dve.tensor_reduce(best, logit, AX.X, ALU.max))
                        settle(dve.tensor_tensor(cand, logit, over(best, EPG), ALU.is_ge))
                        settle(dve.tensor_tensor(cand, cand, first8, ALU.mult))
                        settle(dve.tensor_reduce(m_c, cand, AX.X, ALU.max))
                        settle(dve.tensor_tensor(hot_out, cand, over(m_c, EPG), ALU.is_equal))

                    first_best(sel, m_1, pick[:, 0])
                    settle(dve.scalar_tensor_tensor(sel2, pick[:, 0], NEG, sel, ALU.mult, ALU.add))
                    first_best(sel2, m_2, pick[:, 1])
                    dve.tensor_tensor(e_d, m_2, m_1, ALU.subtract).then_inc(r_act_in, 1)
                    for k in range(2):
                        settle(dve.tensor_tensor(E[:, k].rearrange("p t (g e) -> p t g e", g=N_GRP), g_hot.unsqueeze(3).to_broadcast([P, NTT, N_GRP, EPG]),
                                                 pick[:, k].unsqueeze(2).to_broadcast([P, NTT, N_GRP, EPG]), ALU.mult))
                    dve.tensor_tensor(M_b, E[:, 0], E[:, 1], ALU.add).then_inc(hot, 1)
                    Ef = E.rearrange("p k t e -> p (k t) e")
                    EWf = EW.rearrange("p k t e -> p (k t) e")

                    def per_choice(out, row):
                        settle(dve.tensor_tensor(EWf, Ef, row.unsqueeze(1).to_broadcast([P, 10, N_EXP]), ALU.mult))
                        settle(dve.tensor_reduce(out, EWf, AX.X, ALU.add))

                    per_choice(e_id, c("iota_e"))
                    dve.wait_ge(ranks, 1)
                    dve.tensor_tensor(EW[:, :, 0:NT, :], E[:, :, 0:NT, :], PS[:, 0, 0:128].rearrange("p (t e) -> p t e", t=NT).unsqueeze(1).to_broadcast([P, 2, NT, N_EXP]), ALU.mult)
                    settle(dve.tensor_tensor(EW[0:NS, :, NT, :], E[0:NS, :, NT, :], PS[0:NS, 0, 128:160].unsqueeze(1).to_broadcast([NS, 2, N_EXP]), ALU.mult))
                    settle(dve.tensor_reduce(rank, EWf, AX.X, ALU.add))
                    settle(dve.tensor_copy(cnt, PS[:, 0, 160:192]))
                    sh = steps_hot[:, 0:N_EXP * MAX_OVF].rearrange("p (e m) -> p e m", e=N_EXP)
                    settle(dve.tensor_tensor(sh, over(cnt, MAX_OVF), c("cap_steps").unsqueeze(1).to_broadcast([P, N_EXP, MAX_OVF]), ALU.is_gt))
                    settle(dve.tensor_reduce(n_ovf, sh, AX.X, ALU.add))
                    settle(dve.tensor_tensor_scan(incl, c("one").to_broadcast([P, N_EXP]), n_ovf, 0.0, ALU.mult, ALU.add))
                    settle(dve.tensor_tensor(base, incl, n_ovf, ALU.subtract))
                    per_choice(base_k, base)
                    sk = steps_hot[:, 0:10 * MAX_OVF].rearrange("p (k m) -> p k m", k=10)
                    settle(dve.tensor_tensor(sk, over(rank, MAX_OVF), c("cap_steps").unsqueeze(1).to_broadcast([P, 10, MAX_OVF]), ALU.is_ge))
                    settle(dve.tensor_reduce(extra, sk, AX.X, ALU.add))
                    settle(dve.tensor_tensor(base_k, base_k, extra, ALU.add))
                    settle(dve.scalar_tensor_tensor(base_k, base_k, float(N_EXP - 1), e_id, ALU.add, ALU.subtract))
                    settle(dve.scalar_tensor_tensor(base_k, extra, 0.0, base_k, ALU.is_gt, ALU.mult))
                    settle(dve.tensor_tensor(blk, base_k, e_id, ALU.add))
                    settle(dve.scalar_tensor_tensor(row_in, extra, -float(CAP), rank, ALU.mult, ALU.add))
                    settle(dve.tensor_tensor(row_hot, c("slot_row").unsqueeze(1).to_broadcast([P, 10, CAP]), over(row_in, CAP), ALU.is_equal))
                    settle(dve.tensor_tensor(blk_hot.rearrange("p k t b -> p (k t) b"), c("iota_blk").unsqueeze(1).to_broadcast([P, 10, NBLK]), over(blk, NBLK), ALU.is_equal))
                    dve.tensor_tensor(tok_hot[:, 0].rearrange("p k t b -> p (k t) b"), blk_hot.rearrange("p k t b -> p (k t) b"),
                                      c("tile_row").unsqueeze(2).to_broadcast([P, 10, NBLK]), ALU.mult)
                    ins = dve.tensor_tensor(tok_hot[:, 1], blk_hot, c("tile_first").unsqueeze(2).unsqueeze(1).to_broadcast([P, 2, NTT, NBLK]), ALU.mult)
                    ins.then_inc(place, 1)
                    dve.wait_ge(r_act, 2)
                    settle(dve.tensor_reduce(e_sum, g_exp, AX.X, ALU.add))
                    settle(dve.reciprocal(p_g, e_sum))
                    settle(dve.tensor_scalar(rden, e_2, 1.0, None, ALU.add))
                    settle(dve.reciprocal(rden, rden))
                    settle(dve.tensor_tensor(gate[:, 0, :], p_g, rden, ALU.mult))
                    settle(dve.tensor_tensor(gate[:, 1, :], gate[:, 0, :], e_2, ALU.mult))
                    settle(dve.scalar_tensor_tensor(slot_i[:, :, :].rearrange("p k t -> p (k t)"), blk, float(CAP), row_in, ALU.mult, ALU.add))
                    dve.wait_ge(slots_done, 1)
                    dve.tensor_scalar(idx_i[:, :], PS[:, 1, 0:NBLK], 2.0, c("half"), ALU.mult, ALU.add).then_inc(slots_ready, 1)
                    so_ = steps_hot[:, 0:N_EXP * MAX_OVF].rearrange("p (j e) -> p j e", j=MAX_OVF)
                    settle(dve.tensor_tensor(so_, incl.unsqueeze(1).to_broadcast([P, MAX_OVF, N_EXP]), over(c("iota_ovf"), N_EXP), ALU.is_le))
                    settle(dve.tensor_reduce(ovf_f[:, 1:MAX_OVF + 1], so_, AX.X, ALU.add))
                    settle(dve.tensor_copy(ovf_f[:, 0:1], incl[:, N_EXP - 1:N_EXP]))
                    dve.tensor_scalar(ovf_i[:, :], ovf_f, float(N_EXP - 1), None, ALU.min).then_inc(ovf_ready, 1)

                    def step(e, s):
                        p2 = s % 2
                        dve.wait_ge(xe_turned, e + 1)
                        at_least(dve, in_done, e - 1)
                        dve.tensor_tensor(xTe[p2], PS[:, 0, :].rearrange("p (c h t) -> p h c t", c=4, h=2), g2hc, ALU.mult).then_inc(xTe_ready, 1)
                        dve.wait_ge(silu_done, e + 1)
                        at_least(dve, h_turned, e - 1)
                        dve.tensor_tensor(hh[p2], hs[p2], PS[:, 2 + p2, 256:512], ALU.mult).then_inc(h_ready, 1)

                    expert_pass(dve, step)
                    dve.wait_ge(ovf_ready, 1)
                    n_ovf_blocks = dve.value_load(ovf_i[0:1, 0:1], min_val=0, max_val=MAX_OVF)
                    with dve.If(n_ovf_blocks > 0):
                        step(N_EXP, N_EXP)

                @block.gpsimd
                def _(pool):
                    pool.wait_ge(w_ready[4], 16)
                    rest = y_dram[N_EXP * CAP:, :].rearrange("(a p r) n -> a p (r n)", a=4, p=P)
                    for i in range(4):
                        pool.dma_start(rest[i], v_nat[:, :, :].rearrange("p a n -> p (a n)")).then_inc(s_zero, 16)
                    conv_dst = O["new_conv_sample"][bass.ds(layer, 1)].rearrange("l b j n -> (l b) j n")
                    conv_src = A["state_conv"][bass.ds(layer, 1)].rearrange("l b j n -> (l b) j n")
                    pool.dma_start(conv_dst[:, 0:2, :], conv_src[:, 1:3, :]).then_inc(conv_stored, 16)
                    pool.wait_ge(s_read, 4)
                    pool.dma_start(conv_dst[:, 2, :], sxg[:, 0:512]).then_inc(conv_stored, 16)
                    new_k = O["new_k_prompt"][bass.ds(layer, 1)].rearrange("l b (t p) h d -> (l b t) p (h d)", p=P)
                    new_v = O["new_v_prompt"][bass.ds(layer, 1)].rearrange("l b (t p) h d -> (l b t) p (h d)", p=P)
                    for t in range(NT):
                        for i in (2 * t, 2 * t + 1):
                            pool.wait_ge(rope_read, i + 1)
                            pool.tensor_tensor(R[:, i % 4, :], R[:, i % 4, :], R[:, 4 + i % 2, :], ALU.add).then_inc(rope_sum, 1)
                        pool.wait_ge(rope_sum, 2 * t + 2)
                        pool.dma_start(new_k[t], R[:, (2 * t + 1) % 4, :]).then_inc(k_stored[t % 2], 16)
                        pool.wait_ge(scan_done, t + 1)
                        pool.tensor_tensor(yT[:, t, :], yT[:, t, :], ra, ALU.mult).then_inc(y_done, 1)
                        pool.wait_ge(v_kept, t + 1)
                        pool.dma_start(new_v[t], v_nat[:, t, :]).then_inc(stored, 16)
                    pool.wait_ge(small_kept, 1)
                    pool.dma_start(O["new_h_sample"][bass.ds(layer, 1)].rearrange("l b n -> (l b) n"), small_rows[0:NS, :]).then_inc(stored, 16)
                    pool.dma_start(O["new_h_prompt"][bass.ds(layer, 1)].rearrange("l b n -> (l b) n"), small_rows[NS:NS + 1, :]).then_inc(stored, 16)
                    pool.dma_start(O["new_conv_prompt"][bass.ds(layer, 1)].rearrange("l b j n -> (l b j) n"), small_rows[NS + 1:12, :]).then_inc(stored, 16)

                    def root_of_o(g):
                        pool.wait_ge(o_sum, g + 1)
                        pool.tensor_scalar(ost[:, 4:8], ost[:, 0:4], 1.0 / 128, SUB_EPS, ALU.mult, ALU.add).then_inc(o_var, 1)
                        pool.wait_ge(o_var, g + 1)
                        pool.tensor_tensor(ost[:, 8:12], ost[:, 4:8], c("neghalf")[:, 0:4], ALU.pow).then_inc(o_rstd, 1)

                    root_of_o(0)
                    root_of_o(1)
                    pool.wait_ge(a_dve, 6)
                    pool.tensor_tensor(so_st[:, 2:3], so_st[:, 1:2], c("neghalf")[:, 0:1], ALU.pow).then_inc(a_pool, 1)
                    root_of_o(2)
                    root_of_o(3)

                    for p, t in enumerate(ORDER):
                        n = rows_of(p)
                        pool.wait_ge(mean2, p + 1)
                        pool.tensor_tensor(st[0:n, 2, t:t + 1], st[0:n, 1, t:t + 1], c("neghalf", n)[:, 0:1], ALU.pow).then_inc(rstd2, 1)
                    pool.wait_ge(xn2_stored[0], 48)
                    pool.wait_ge(xn2_stored[1], 32)
                    pool.wait_ge(turned2, 2 * NTT)
                    pool.wait_ge(slots_ready, 1)
                    for e in range(NBUF):
                        gather_rows(pool, e)

                    def next_rows(e):
                        pool.wait_ge(xe_turned, e - NBUF + 1)
                        gather_rows(pool, e)

                    for e in range(NBUF, N_EXP):
                        next_rows(e)
                    pool.wait_ge(ovf_ready, 1)
                    n_ovf_blocks = pool.value_load(ovf_i[0:1, 0:1], min_val=0, max_val=MAX_OVF)
                    with pool.If(n_ovf_blocks > 0):
                        next_rows(N_EXP)

                @block.tensor
                def _(pe):
                    for t in range(NT):
                        pe.wait_ge(xn_ready, t + 1)
                        for h in range(2):
                            u = 2 * t + h
                            if u >= 4:
                                pe.wait_ge(hT_ready, u - 3)
                            for j in range(4):
                                k = 4 * h + j
                                ins = pe.transpose(PS[:, u % 4, j * P:(j + 1) * P], xn[t % 2][:, k * P:(k + 1) * P], ident)
                            ins.then_inc(turned, 1)
                    pe.wait_ge(xn_ready, NTT)
                    pe.wait_ge(hT_ready, 5)
                    for k in range(KC):
                        ins = pe.transpose(PS[:, 0, k * NS:(k + 1) * NS], xn[0][0:NS, k * P:(k + 1) * P], ident[0:NS, 0:NS])
                    ins.then_inc(turned, 1)
                    pe.wait_ge(hT_ready, 2 * NT + 1)

                    def bank_free(u):
                        if 4 <= u < 12:
                            pe.wait_ge(gx_read, u - 3)
                        elif u >= 12:
                            t, s = divmod(u - 12, 3)
                            if s < 2:
                                pe.wait_ge(rope_read, 2 * t + s + 1)
                            else:
                                pe.wait_ge(v_kept, t + 1)

                    for part, w in ((0, wg), (1, wx)):
                        pe.wait_ge(w_ready[part], 16)
                        for i in range(NC):
                            u = part * NC + i
                            bank_free(u)
                            for k in range(KC):
                                ins = pe.matmul(PS[:, u % 4, :], w[:, k, i * P:(i + 1) * P], hT[:, k, :], start=(k == 0), stop=(k == KC - 1))
                            ins.then_inc(proj, 1)
                    for k in range(KC):
                        for j in range(4):
                            w = wg if j < 2 else wx
                            ins = pe.matmul(PS[32 * j:32 * j + NS, 4, 0:256], hTs[:, k, :], w[:, k, 256 * (j % 2):256 * (j % 2) + 256],
                                            start=(k == 0), stop=(k == KC - 1))
                    ins.then_inc(s_proj, 1)

                    def turn_rotary(i):
                        pe.wait_ge(rope_sum, i + 1)
                        if i >= 1:
                            pe.wait_ge(rope_kept, i)
                        for j in range(NG):
                            ins = pe.transpose(PS[:, 7, j * P:(j + 1) * P], R[:, i % 4, j * P:(j + 1) * P], ident)
                        ins.then_inc(rope_turned, 1)

                    for t in range(NT):
                        for s in range(3):
                            if t >= 1 and s < 2:
                                turn_rotary(2 * t - 2 + s)
                            if s == 2:
                                if t == 0:
                                    pe.wait_ge(gate_params, 16)
                                pe.wait_ge(conv_done, t + 1)
                                if t >= 1:
                                    pe.wait_ge(gates_read, t)
                                pe.matmul(PS[:, 5, :], gate_w[:, 0, t, :], xc[t], start=True, stop=True)
                                pe.matmul(PS[:, 6, :], gate_w[:, 1, t, :], xc[t], start=True, stop=True).then_inc(gates_done, 1)
                            u = 8 + 3 * t + s
                            if t == 0:
                                pe.wait_ge(w_ready[2 + s], 16)
                            bank_free(u)
                            for k in range(KC):
                                ins = pe.matmul(PS[:, u % 4, :], hT[:, k, t * P:(t + 1) * P], wqkv[s][:, k, :], start=(k == 0), stop=(k == KC - 1))
                            ins.then_inc(proj, 1)
                        if t == 0:
                            pe.wait_ge(s_read, 4)
                            pe.wait_ge(states, 32)
                            for i in range(NC):
                                pe.transpose(PS[:, 4, 8 * i:8 * i + 8], sxg[:, i * P:(i + 1) * P], ident[0:NS, 0:NS])
                                pe.transpose(PS[:, 4, 32 + 8 * i:40 + 8 * i], sxg[:, 512 + i * P:512 + (i + 1) * P], ident[0:NS, 0:NS])
                                pe.transpose(PS[:, 4, 64 + 24 * i:88 + 24 * i], stc[:, i * P:(i + 1) * P], ident[0:24, 0:24])
                                ins = pe.transpose(PS[:, 4, 160 + 8 * i:168 + 8 * i], sth[:, i * P:(i + 1) * P], ident[0:NS, 0:NS])
                            ins.then_inc(s_turned, 1)
                        if t == 2:
                            pe.wait_ge(s_conv, 1)
                            pe.wait_ge(s_kept, 1)
                            for g in range(2):
                                for i in range(NC):
                                    ins = pe.matmul(PS[:, 4, 256 + 32 * g + 8 * i:264 + 32 * g + 8 * i], gate_w[:, g, i, :], xcs[:, i, :], start=True, stop=True)
                            ins.then_inc(s_gates, 1)
                    turn_rotary(6)
                    turn_rotary(7)
                    pe.wait_ge(s_pe, 1)
                    for k in range(KC):
                        for j in range(3):
                            ins = pe.matmul(PS[32 * j:32 * j + NS, 4, :], hTs[:, k, :], wqkv[j][:, k, :], start=(k == 0), stop=(k == KC - 1))
                    ins.then_inc(s_proj, 1)
                    pe.wait_ge(s_pe, 4)
                    pe.wait_ge(scan_done, NC)
                    pe.wait_ge(rope_kept, 8)
                    for i in range(NC):
                        ins = pe.transpose(PS[0:12, 7, i * P:(i + 1) * P], small[:, i, :], ident)
                    ins.then_inc(small_turned, 1)

                    def spread_query(b):
                        if b == 0:
                            pe.wait_ge(a_row, 1)
                            pe.wait_ge(small_kept, 1)
                        else:
                            pe.wait_ge(a_mul, 2 * b)
                        pe.matmul(PS[:, 7, :], ident[0:NS, b:b + 1].to_broadcast([NS, P]), q_rot, start=True, stop=True).then_inc(a_bc, 1)

                    def sample_turn_scores():
                        pe.wait_ge(a_s, 1)
                        pe.wait_ge(a_prod, 2 * NS)
                        pe.matmul(PS[0:64, 7, 256:264], c("sel_b", NS), own, start=True, stop=True)
                        for g in range(N_PAGES):
                            ins = pe.transpose(PS[0:64, 7, g * P:(g + 1) * P], key_scores[:, g].rearrange("p b h -> p (b h)"), ident)
                        ins.then_inc(a_pe, 1)

                    def sample_turn_probs():
                        pe.wait_ge(a_dve, 2)
                        pe.matmul(PS[0:NS, 7, 264:268], c("sel_t", 64), own_g, start=True, stop=True)
                        for g in range(N_PAGES):
                            ins = pe.transpose(PS[:, 7, 272 + g * 64:272 + (g + 1) * 64], s_row[:, g * P:(g + 1) * P], ident[0:64, 0:64])
                        ins.then_inc(a_pe, 1)

                    def sample_values(tokens):
                        pe.wait_ge(a_dve, 5)
                        pe.wait_ge(v_pages, 16 * NS * N_PAGES)
                        for b in tokens:
                            for g in range(N_PAGES):
                                for m in range(NG):
                                    pe.matmul(PS[32 * m:32 * m + 32, 7, 0:P], spread_map[:, g, b, m, :], vc_nat[:, b * N_PAGES + g, m * P:(m + 1) * P],
                                              start=(b == 0 and g == 0), stop=False)
                        if tokens[-1] == NS - 1:
                            for m in range(NG):
                                ins = pe.matmul(PS[32 * m:32 * m + 32, 7, 0:P], own_map[:, m, :], sqkv[2][:, m * P:(m + 1) * P], start=False, stop=True)
                            ins.then_inc(a_pe, 1)

                    def sample_turn_output():
                        pe.wait_ge(a_dve, 7)
                        pe.transpose(PS[:, 7, 256:384], so2, ident).then_inc(a_pe, 1)

                    def score(u):
                        g, t = UNITS[u]
                        b = 2 * (u % 2)
                        if u == 0:
                            pe.wait_ge(rope_kept, 2 * NT)
                            pe.wait_ge(v_kept, NT)
                        if u >= 2:
                            pe.wait_ge(exps, u - 1)
                        for m in range(2):
                            pe.matmul(PS[:, b + m, 0:(t + 1) * P], qT[64 * m:64 * m + 64, g, t * P:(t + 1) * P], kT[64 * m:64 * m + 64, g, 0:(t + 1) * P],
                                      start=True, stop=False)
                        for m in range(2):
                            ins = pe.matmul(PS[:, b + m, t * P:(t + 1) * P], ident_b[:, :], mask_b[:, :], start=False, stop=True)
                        ins.then_inc(scores, 1)

                    def turn_map(u):
                        g, t = UNITS[u]
                        pe.wait_ge(amap, u + 1)
                        if u == 0:
                            pe.wait_ge(gates_read, NC)
                        if u >= 2:
                            pe.wait_ge(map_kept, u - 1)
                        if u >= 8 and (u - 8) % 4 == 0:
                            pe.wait_ge(o_kept, (u - 8) // 4 + 1)
                        for j in range(t + 1):
                            ins = pe.transpose(PS[:, 5 + u % 2, j * P:(j + 1) * P], prob[u % 2][:, 0, j * P:(j + 1) * P], ident)
                        ins.then_inc(map_turned, 1)

                    def values(u):
                        g, t = UNITS[u]
                        pe.wait_ge(map_kept, u + 1)
                        if u == 0:
                            pe.wait_ge(s_read, 7)
                        if t == 0 and g >= 1:
                            pe.wait_ge(o_read, g)
                        for j in range(t + 1):
                            ins = pe.matmul(PS[:, 4, t * P:(t + 1) * P], kept_map[u % 2][:, j * P:(j + 1) * P], v_nat[:, j, g * P:(g + 1) * P],
                                            start=(j == 0), stop=(j == t))
                        ins.then_inc(av, 1)

                    def turn_o(g):
                        pe.wait_ge(o_norm, g + 1)
                        pe.wait_ge(map_kept, min(NT * g + 7, N_U))
                        for t in range(NT):
                            ins = pe.transpose(PS[:, o_bank(g), t * P:(t + 1) * P], o1[:, t * P:(t + 1) * P], ident)
                        ins.then_inc(o_turned, 1)

                    def rnn_half(u):
                        if u == 0:
                            pe.wait_ge(w_out_ready, 32)
                        pe.wait_ge(exps, N_U - 1 + u // 2)
                        for k in range(NC):
                            pe.matmul(PS[:, u, :], yT[:, k, u // 2 * P:(u // 2 + 1) * P], w_out[:, k, 512 * (u % 2):512 * (u % 2) + 512], start=(k == 0), stop=False)

                    for i in range(N_U + 6):
                        if i < N_U:
                            score(i)
                        elif i < N_U + 4:
                            rnn_half(i - N_U)
                        if i >= 9 and (i - 9) % 4 == 0:
                            turn_o((i - 9) // 4)
                        if 2 <= i <= N_U + 1:
                            turn_map(i - 2)
                        if 3 <= i <= N_U + 2:
                            values(i - 3)
                        if i < NS:
                            spread_query(i)
                        elif i == 8:
                            sample_turn_scores()
                        elif i == 10:
                            sample_turn_probs()
                        elif i in (11, 12):
                            sample_values(range(4 * (i - 11), 4 * (i - 10)))
                        elif i == 15:
                            sample_turn_output()

                    def output_units(p):
                        t = ORDER[p]
                        if t == NT:
                            pe.wait_ge(a_done, 1)
                            pe.wait_ge(o_read, NG)
                            for k in range(KC):
                                for j in range(4):
                                    ins = pe.matmul(PS[32 * j:32 * j + NS, 4, 0:256], yTs[:, k, :], w_out[:, k, 256 * j:256 * j + 256], start=(k == 0), stop=(k == KC - 1))
                            ins.then_inc(op_done, 1)
                            return
                        pe.wait_ge(o_kept, NG)
                        for h in range(2):
                            u = 2 * t + h
                            if u >= 4:
                                pe.wait_ge(x_new, u - 2)
                            for k in range(NC if u < 4 else 0, KC):
                                ins = pe.matmul(PS[:, u % 4, :], yT[:, k, t * P:(t + 1) * P], w_out[:, k, 512 * h:512 * h + 512], start=(k == 0), stop=(k == KC - 1))
                            ins.then_inc(op_done, 1)

                    def turn(p):
                        n = rows_of(p)
                        pe.wait_ge(xn2_ready, p + 1)
                        for h in range(2):
                            if p >= 1:
                                pe.wait_ge(h2_ready, 2 * p - 1 + h)
                            for j in range(4):
                                k = 4 * h + j
                                ins = pe.transpose(PS[:, 5 + h, j * P:j * P + n], xn2[p % 2][0:n, k * P:(k + 1) * P], ident[0:n, 0:n])
                            ins.then_inc(turned2, 1)

                    def route(p):
                        n, t = rows_of(p), ORDER[p]
                        if p == 0:
                            pe.wait_ge(w_route, 16)
                        pe.wait_ge(h2_ready, 2 * p + 2)
                        for k in range(KC):
                            ins = pe.matmul(PS[0:n, 7, 36 * t:36 * t + 36], h2T[p % 2][:, k, 0:n], route_w[:, k, :], start=(k == 0), stop=(k == KC - 1))
                        ins.then_inc(logits, 1)

                    for i in range(NTT + 3):
                        if i < NTT:
                            output_units(i)
                        if 2 <= i <= NTT + 1:
                            turn(i - 2)
                        if i >= 3:
                            route(i - 3)
                    pe.wait_ge(hot, 1)
                    for t in range(NTT):
                        n = P if t < NT else NS
                        for s in range(t):
                            pe.matmul(PS[0:n, 0, 32 * t:32 * t + 32], ones_b[:, 0:n], M_b[:, s, :], start=(s == 0), stop=False)
                        pe.matmul(PS[0:n, 0, 32 * t:32 * t + 32], tri_b[0:n, 0:n], M_b[0:n, t, :], start=(t == 0), stop=True)
                    for t in range(NTT):
                        n = P if t < NT else NS
                        ins = pe.matmul(PS[:, 0, 160:192], ones_b[0:n, :], M_b[0:n, t, :], start=(t == 0), stop=(t == NTT - 1))
                    ins.then_inc(ranks, 1)
                    pe.wait_ge(place, 1)
                    for k in range(2):
                        for t in range(NTT):
                            n = P if t < NT else NS
                            for a in range(2):
                                for h in range(2):
                                    ins = pe.matmul(PS[h * CAP:h * CAP + CAP, 1, 0:NBLK], row_hot[0:n, k * NTT + t, :], tok_hot[0:n, a, k, t, :],
                                                    start=(k == 0 and t == 0 and a == 0), stop=(k == 1 and t == NTT - 1 and a == 1))
                    ins.then_inc(slots_done, 1)

                    def turn(e, s):
                        pe.wait_ge(gathered[s % 3], (e // 3 + 1) * 16 if isinstance(e, int) else e_third(e, s))
                        at_least(pe, xTe_ready, e)
                        turn_rows(pe, xe[s % 3]).then_inc(xe_turned, 1)

                    def e_third(e, s):
                        return ((e - s % 3) * 16) // 3 + 16

                    def uses(e, s):
                        return (e // 3 + 1) * 16 if isinstance(e, int) else e_third(e, s)

                    def before(e, end):
                        return not isinstance(e, int) or e < end

                    def input_product(e, s):
                        p2, b = s % 2, s % 3
                        pe.wait_ge(e_in[b][0], uses(e, s))
                        pe.wait_ge(xTe_ready, e + 1)
                        at_least(pe, h_ready, e - 1)
                        in_product(pe, xTe[p2], expert_in(b), 2 + p2, lambda: pe.wait_ge(e_in[b][1], uses(e, s)), in_half).then_inc(in_done, 1)

                    def step(e, s):
                        p2, b = s % 2, s % 3
                        if before(e, N_EXP - 1):
                            input_product(e + 1, s + 1)
                        pe.wait_ge(h_ready, e + 1)
                        at_least(pe, hT_kept, e)
                        for j in range(2):
                            ins = pe.transpose(PS[:, 4, j * P:(j + 1) * P], hh[p2][:, j * P:(j + 1) * P], ident)
                        ins.then_inc(h_turned, 1)
                        if before(e, N_EXP - 2):
                            turn(e + 2, s + 2)
                        pe.wait_ge(e_out[b], uses(e, s))
                        pe.wait_ge(hT_kept, e + 1)
                        at_least(pe, y_kept, e - 1)
                        out_product(pe, hTe[p2], expert_out(b), 5 + p2).then_inc(out_done, 1)

                    pe.wait_ge(ovf_ready, 1)
                    n_ovf_blocks = pe.value_load(ovf_i[0:1, 0:1], min_val=0, max_val=MAX_OVF)
                    turn(0, 0)
                    input_product(0, 0)
                    turn(1, 1)
                    expert_pass(pe, step)
                    with pe.If(n_ovf_blocks > 0):
                        turn(N_EXP, N_EXP)
                        input_product(N_EXP, N_EXP)
                        step(N_EXP, N_EXP)

            nc.all_engine_barrier()
            n_more = nc.values_load(ovf_i[0:1, 0:1], min_val=0, max_val=MAX_OVF)
            with nc.If(n_more > 1):
                with nc.Fori(1, n_more) as more:
                    with nc.Block() as block:
                        @block.sync
                        def _(sp_):
                            which = sp_.value_load(ovf_i[0:1, bass.ds(more + 1, 1)], min_val=0, max_val=N_EXP - 1)
                            expert = which + layer * N_EXP
                            sp_.dma_start(expert_in(0), w_in_rows[bass.ds(expert, 1)].rearrange("e p k n -> p (e k) n")).then_inc(v_w, 16)
                            sp_.dma_start(expert_out(0), w_out_rows[bass.ds(expert, 1)].rearrange("e p k n -> p (e k) n")).then_inc(v_w, 16)
                            sp_.wait_ge(v_y, 1)
                            for j in range(2):
                                sp_.dma_start(y_blocks[bass.ds(more + N_EXP, 1), :, 512 * j:512 * j + 512].rearrange("e r n -> r (e n)"), ye[0][64 * j:64 * j + 64, :]).then_inc(v_st, 16)
                            sp_.wait_ge(v_st, 32)

                        @block.gpsimd
                        def _(pool):
                            pool.tensor_copy(cur[:, 0:1], idx_i[:, bass.ds(more + N_EXP, 1)]).then_inc(v_g, 16)
                            pool.wait_ge(v_g, 16)
                            pool.indirect_dma_start(xe[0], None, halves, bass.IndirectOffsetOnAxis(cur[:, 0:1], 0)).then_inc(v_t, 16)

                        @block.tensor
                        def _(pe):
                            pe.wait_ge(v_t, 16)
                            turn_rows(pe, xe[0]).then_inc(v_x, 1)
                            pe.wait_ge(v_x, 2)
                            pe.wait_ge(v_w, 32)
                            in_product(pe, xTe[0], expert_in(0), 2).then_inc(v_i, 1)
                            pe.wait_ge(v_h, 1)
                            for j in range(2):
                                ins = pe.transpose(PS[:, 4, j * P:(j + 1) * P], hh[0][:, j * P:(j + 1) * P], ident)
                            ins.then_inc(v_ht, 1)
                            pe.wait_ge(v_hk, 1)
                            out_product(pe, hTe[0], expert_out(0), 5).then_inc(v_o, 1)

                        @block.vector
                        def _(dve):
                            dve.wait_ge(v_x, 1)
                            dve.tensor_tensor(xTe[0], PS[:, 0, :].rearrange("p (c h t) -> p h c t", c=4, h=2), g2hc, ALU.mult).then_inc(v_x, 1)
                            dve.wait_ge(v_s, 1)
                            dve.tensor_tensor(hh[0], hs[0], PS[:, 2, 256:512], ALU.mult).then_inc(v_h, 1)

                        @block.scalar
                        def _(act):
                            act.wait_ge(v_i, 1)
                            act.activation(hs[0], PS[:, 2, 0:256], ACT.Silu).then_inc(v_s, 1)
                            act.wait_ge(v_ht, 1)
                            act.activation(hTe[0], PS[:, 4, 0:256].rearrange("p (j h t) -> p j h t", j=2, h=2), ACT.Copy).then_inc(v_hk, 1)
                            act.wait_ge(v_o, 1)
                            act.activation(ye[0], PS[:, 5, :], ACT.Copy).then_inc(v_y, 1)

                    barrier_and_clear(ovf_sems)

            nc.all_engine_barrier()
            picks = [(t, k) for t in range(NTT) for k in range(2)]
            y_rows = [W[:, 1024 * i:1024 * i + 1024] for i in range(len(picks))]
            with nc.Block() as block:
                @block.scalar
                def _(act):
                    for t in range(NTT):
                        act.wait_ge(added, 2 * t + 2)
                        squares_of_rows(act, t, sumsq)

                @block.gpsimd
                def _(pool):
                    for i, (t, k) in enumerate(picks):
                        n = P if t < NT else NS
                        pool.indirect_dma_start(y_rows[i][0:n, :], None, y_dram, bass.IndirectOffsetOnAxis(slot_i[0:n, k, t:t + 1], 0)).then_inc(got[t], 16)
                    inverse_roots(pool, mean_eps, rstd)

                @block.vector
                def _(dve):
                    for i, (t, k) in enumerate(picks):
                        n = P if t < NT else NS
                        if k == 0:
                            dve.wait_ge(got[t], 32)
                        dve.scalar_tensor_tensor(x[0:n, t, :], y_rows[i][0:n, :], gate[0:n, k, t:t + 1], x[0:n, t, :], ALU.mult, ALU.add).then_inc(added, 1)
                        if k == 0:
                            dve.wait_ge(added, i + 1)
                    mean_of_squares(dve, sumsq, mean_eps)

            barrier_and_clear(all_sems)

        f_gain, f_out, f_stored = (once("final_" + n) for n in ("gain", "rows", "stored"))
        gain = W[:, 0:1024]
        rows_out = W[:, 2048:2048 + NTT * D].rearrange("p (t n) -> p t n", t=NTT)
        with nc.Block() as block:
            @block.sync
            def _(sp_):
                sp_.dma_start(gain, A["ln_f"]).then_inc(f_gain, 16)
                yp = O["y_prompt"].rearrange("b (t p) n -> (b t) p n", p=P)
                ys = O["y_sample"].rearrange("b s n -> (b s) n")
                for t in range(NTT):
                    sp_.wait_ge(f_out, t + 1)
                    if t < NT:
                        sp_.dma_start(yp[t], rows_out[:, t, :]).then_inc(f_stored, 16)
                    else:
                        sp_.dma_start(ys, rows_out[0:NS, t, :]).then_inc(f_stored, 16)
                sp_.wait_ge(f_stored, 16 * NTT)

            @block.vector
            def _(dve):
                dve.wait_ge(f_gain, 16)
                for t in range(NTT):
                    n = P if t < NT else NS
                    dve.scalar_tensor_tensor(rows_out[0:n, t, :], x[0:n, t, :], st[0:n, 2, t:t + 1], gain[0:n, :], ALU.mult, ALU.mult).then_inc(f_out, 1)


def constants():
    def rope(pos):
        half = HEAD // 2
        inv = (10000.0 ** (-np.arange(half, dtype=np.float32) / half)).astype(np.float32)
        ang = pos.astype(np.float32)[:, None] * inv[None, :]
        cos, sin = np.cos(ang), np.sin(ang)
        return np.concatenate([cos, cos], 1), np.concatenate([-sin, sin], 1)

    t = {}
    cos, sin = rope(np.arange(SEQ))
    t["cos"] = cos.reshape(NT, P, 64).transpose(1, 0, 2).reshape(P, -1)
    t["sin"] = sin.reshape(NT, P, 64).transpose(1, 0, 2).reshape(P, -1)
    t["cos_s"], t["sin_s"] = rope(np.full(P, PAST))
    row = np.arange(P)[:, None]
    t["ident"] = np.eye(P)
    t["mask"] = np.where(np.arange(P)[None, :] > row, NEG, 0.0)
    t["tri"] = (row < np.arange(P)[None, :]) * 1.0
    t["iota_e"] = np.arange(N_EXP)[None, :]
    t["iota_blk"] = np.arange(NBLK)[None, :]
    t["cap_steps"] = (np.arange(MAX_OVF)[None, :] + 1.0) * CAP
    t["iota_ovf"] = np.arange(MAX_OVF)[None, :]
    t["slot_row"] = np.arange(CAP)[None, :]
    t["tile_row"] = row
    t["tile_first"] = P * np.arange(NTT)[None, :]
    t["delta"] = (np.arange(NS)[:, None] == np.arange(32)[None, :]).reshape(1, -1) * 1.0
    t["first4"] = N_GRP - np.arange(N_GRP)[None, :]
    t["first8"] = EPG - np.arange(EPG)[None, :]
    t["half"] = (row >= CAP) * 1.0
    t["neghalf"] = np.full((1, 8), -0.5)
    t["sel_b"] = (row == np.arange(64)[None, :] // NH) * 1.0
    t["sel_t"] = (row // NH == np.arange(NS)[None, :]) * 1.0
    t["mask_h"] = (row % NH == np.arange(NH)[None, :]) * 1.0
    t["mask_g"] = (row % NH // 2 == np.arange(NG)[None, :]) * 1.0
    t["even"] = (row % 2 == 0) * 1.0
    t["odd"] = (row % 2 == 1) * 1.0
    t["one"] = np.ones((1, 1))
    out = np.zeros((P, C_W), np.float32)
    for name, (a, b) in C_AT.items():
        out[:, a:b] = t[name]
    return out


def laid_out(inp):
    def by_channel(a):
        return a.reshape(DEPTH, -1, P).transpose(0, 2, 1)

    big = ["x_prompt", "x_sample", "cache_k", "cache_v", "state_h", "state_conv", "w_in", "w_out", "w_exp_in", "w_exp_out"]
    a = {k: np.ascontiguousarray(inp[k]) for k in big}
    a["page_row"] = np.ascontiguousarray(inp["page_table"]).reshape(1, -1)
    cw = inp["conv_w"].reshape(DEPTH, CONV_W, NC, P).transpose(0, 3, 2, 1).reshape(DEPTH, P, 16)
    a["pf"] = np.ascontiguousarray(np.concatenate(
        [cw] + [by_channel(inp[k]) for k in ("conv_b", "b_ga", "b_gx", "lru_lambda", "ln1_g", "ln2_g")], 2))
    rows = [inp[k].reshape(DEPTH, 1, -1) for k in ("subln_g", "b_route_group", "b_route_expert", "lam_q1", "lam_k1", "lam_q2", "lam_k2")]
    li = np.array([0.8 - 0.6 * math.exp(-0.3 * n) for n in range(DEPTH)], np.float64)
    rows += [li.astype(np.float32).reshape(DEPTH, 1, 1), (1.0 - li).astype(np.float32).reshape(DEPTH, 1, 1)]
    a["pb"] = np.ascontiguousarray(np.broadcast_to(np.concatenate(rows, 2), (DEPTH, P, PB_W)))
    g = np.zeros((DEPTH, P, 2, NC, P), np.float32)
    for n, k in enumerate(("w_ga", "w_gx")):
        for i in range(NC):
            g[:, 0:64, n, i, 0:64] = inp[k][:, 2 * i]
            g[:, 64:128, n, i, 64:128] = inp[k][:, 2 * i + 1]
    a["gate_w"] = g
    r = np.concatenate([inp["w_route_group"], inp["w_route_expert"]], 2)
    a["route_w"] = np.ascontiguousarray(r.reshape(DEPTH, KC, P, 36).transpose(0, 2, 1, 3))
    a["ln_f"] = np.ascontiguousarray(np.broadcast_to(inp["ln_f"].reshape(1, D), (P, D)))
    a["consts"] = constants()
    return a


OUTS = [("y_prompt", (1, SEQ, D)), ("y_sample", (NS, 1, D)), ("new_k_prompt", (DEPTH, 1, SEQ, NH, HEAD)),
        ("new_v_prompt", (DEPTH, 1, SEQ, NG, 2 * HEAD)), ("new_h_prompt", (DEPTH, 1, D_RNN)),
        ("new_conv_prompt", (DEPTH, 1, CONV_W - 1, D_RNN)), ("new_k_sample", (DEPTH, NS, 1, NH, HEAD)),
        ("new_v_sample", (DEPTH, NS, 1, NG, 2 * HEAD)), ("new_h_sample", (DEPTH, NS, D_RNN)),
        ("new_conv_sample", (DEPTH, NS, CONV_W - 1, D_RNN))]


def kernel(**inputs):
    import concourse.bacc as _bacc
    from concourse.bass_utils import run_bass_kernel_spmd as _run

    nc = _bacc.Bacc("TRN2", target_bir_lowering=False, num_devices=1)
    arrays = laid_out({k: np.asarray(v) for k, v in inputs.items()})
    A = {k: nc.dram_tensor(f"in_{k}", v.shape, mybir.dt.from_np(v.dtype), kind="ExternalInput").ap() for k, v in arrays.items()}
    O = {k: nc.dram_tensor(f"out_{k}", s, F32, kind="ExternalOutput").ap() for k, s in OUTS}
    hybrid_step(nc, A, O)
    r = _run(nc, [{f"in_{k}": v for k, v in arrays.items()}], core_ids=[0])
    return tuple(r.results[0][f"out_{k}"] for k, _ in OUTS)
```
